# Optimizing a Trainium2 kernel written in Bass

```python
import math
import jax, jax.numpy as jnp
from jax import lax
import numpy as np
import jax
import jax.numpy as jnp

D_MODEL = 1024
BATCH = 1
SEQ = 256
DEPTH = 2

HEAD_DIM = 64
A_Q_HEADS = 8
A_KV_HEADS = 2
A_GROUP = A_Q_HEADS // A_KV_HEADS
WINDOW = 128
BLOCK = 128
ROPE_THETA = 500000.0
ROPE_DIM = HEAD_DIM // 4
A_WIDTH = A_Q_HEADS * HEAD_DIM
KV_WIDTH = A_KV_HEADS * HEAD_DIM
B_GROUPS = 8
B_GROUP_DIM = 64
B_WIDTH = B_GROUPS * B_GROUP_DIM
CHUNK = 128
EVEN_IN_WIDTH = A_WIDTH + 2 * KV_WIDTH + 2 * B_WIDTH
EVEN_MIX_WIDTH = A_WIDTH + B_WIDTH
POOL_WINDOWS = (2, 4, 8, 16)
POOL_GROUPS = len(POOL_WINDOWS)
POOL_WIDTH = D_MODEL
POOL_GROUP_DIM = POOL_WIDTH // POOL_GROUPS
MEM_LEN = 256
X_HEADS = 4
X_HEAD_DIM = D_MODEL // X_HEADS
N_EXPERTS = 16
N_EXPERT_GROUPS = 4
EXPERTS_PER_GROUP = N_EXPERTS // N_EXPERT_GROUPS
TOP_K = 2
D_EXPERT = D_MODEL // 2
ALPHA = (2.0 * DEPTH) ** 0.25
BETA = (8.0 * DEPTH) ** -0.25
LN_EPS = 1e-5


def layer_norm(x, g, b):
    xf = x.astype(jnp.float32)
    mu = jnp.mean(xf, axis=-1, keepdims=True)
    var = jnp.mean(jnp.square(xf - mu), axis=-1, keepdims=True)
    y = (xf - mu) * lax.rsqrt(var + LN_EPS) * g.astype(jnp.float32) + b.astype(jnp.float32)
    return y.astype(x.dtype)

def partial_rope(t, positions):
    half = ROPE_DIM // 2
    inv_freq = ROPE_THETA ** (-(jnp.arange(half, dtype=jnp.float32) * 2.0 / ROPE_DIM))
    ang = positions.astype(jnp.float32)[..., None] * inv_freq
    cos = jnp.cos(ang)[:, :, None, :]
    sin = jnp.sin(ang)[:, :, None, :]
    tr = t[..., :ROPE_DIM].astype(jnp.float32)
    t1, t2 = tr[..., :half], tr[..., half:]
    rot = jnp.concatenate([t1 * cos - t2 * sin, t2 * cos + t1 * sin], axis=-1).astype(t.dtype)
    return jnp.concatenate([rot, t[..., ROPE_DIM:]], axis=-1)

def sliding_window_sink_attention(q, k, v, sinks):
    bsz, s_len = q.shape[0], q.shape[1]
    nb = s_len // BLOCK
    qb = q.reshape(bsz, nb, BLOCK, A_KV_HEADS, A_GROUP, HEAD_DIM)

    def with_prev(t):
        tb = t.reshape(bsz, nb, BLOCK, A_KV_HEADS, HEAD_DIM)
        prev = jnp.pad(tb[:, :-1], ((0, 0), (1, 0), (0, 0), (0, 0), (0, 0)))
        return jnp.concatenate([prev, tb], axis=2)

    kb, vb = with_prev(k), with_prev(v)
    s = jnp.einsum('bnqhgd,bnkhd->bnhgqk', qb, kb).astype(jnp.float32) * (HEAD_DIM ** -0.5)
    qi = jnp.arange(BLOCK)[:, None]
    kj = jnp.arange(2 * BLOCK)[None, :]
    rel = qi + BLOCK - kj
    band = (rel >= 0) & (rel < WINDOW)
    not_before_start = (jnp.arange(nb)[:, None, None] > 0) | (kj[None] >= BLOCK)
    valid = band[None] & not_before_start
    s = jnp.where(valid[None, :, None, None], s, -jnp.inf)
    sink = sinks.astype(jnp.float32).reshape(A_KV_HEADS, A_GROUP)[None, None, :, :, None, None]
    m = jnp.maximum(jnp.max(s, axis=-1, keepdims=True), sink)
    p = jnp.exp(s - m)
    denom = jnp.sum(p, axis=-1, keepdims=True) + jnp.exp(sink - m)
    p = (p / denom).astype(v.dtype)
    o = jnp.einsum('bnhgqk,bnkhd->bnqhgd', p, vb)
    return o.reshape(bsz, s_len, A_WIDTH)

def chunked_spatial_gating(u, v, ln_g, ln_b, w_s, b_s):
    bsz, s_len = u.shape[0], u.shape[1]
    nc = s_len // CHUNK
    vg = v.reshape(bsz, s_len, B_GROUPS, B_GROUP_DIM)
    vg = layer_norm(vg, ln_g.reshape(B_GROUPS, B_GROUP_DIM), ln_b.reshape(B_GROUPS, B_GROUP_DIM))
    vg = vg.reshape(bsz, nc, CHUNK, B_GROUPS, B_GROUP_DIM)
    causal = jnp.tril(jnp.ones((CHUNK, CHUNK), dtype=bool))
    w = jnp.where(causal[None], w_s, jnp.zeros_like(w_s))
    mixed = jnp.einsum('gts,bnsgc->bntgc', w, vg) + b_s.T[None, None, :, :, None]
    return u * mixed.reshape(bsz, s_len, B_WIDTH)

def even_mixer(x, positions, w_in, sinks, sgu_ln_g, sgu_ln_b, sgu_w, sgu_b, w_out):
    bsz, s_len, _ = x.shape
    h = x @ w_in
    c1 = A_WIDTH
    c2 = c1 + KV_WIDTH
    c3 = c2 + KV_WIDTH
    c4 = c3 + B_WIDTH
    q, k, v, bu, bv = h[..., :c1], h[..., c1:c2], h[..., c2:c3], h[..., c3:c4], h[..., c4:]
    q = partial_rope(q.reshape(bsz, s_len, A_Q_HEADS, HEAD_DIM), positions)
    k = partial_rope(k.reshape(bsz, s_len, A_KV_HEADS, HEAD_DIM), positions)
    v = v.reshape(bsz, s_len, A_KV_HEADS, HEAD_DIM)
    a_out = sliding_window_sink_attention(q, k, v, sinks)
    b_out = chunked_spatial_gating(jax.nn.gelu(bu), jax.nn.gelu(bv), sgu_ln_g, sgu_ln_b, sgu_w, sgu_b)
    return jnp.concatenate([a_out, b_out], axis=-1) @ w_out

def odd_mixer(x, w_in, pool_w, pool_scale, w_out):
    bsz, s_len, _ = x.shape
    h = x @ w_in
    hf = h.astype(jnp.float32)
    csum = jnp.cumsum(hf, axis=1)
    counts_base = jnp.arange(1, s_len + 1, dtype=jnp.float32)
    groups = []
    for g, win in enumerate(POOL_WINDOWS):
        sl = slice(g * POOL_GROUP_DIM, (g + 1) * POOL_GROUP_DIM)
        c = csum[..., sl]
        lagged = jnp.pad(c, ((0, 0), (win, 0), (0, 0)))[:, :s_len]
        count = jnp.minimum(counts_base, float(win))[None, :, None]
        groups.append((c - lagged) / count - hf[..., sl])
    pooled = jnp.stack(groups, axis=2).astype(x.dtype)
    mapped = jnp.einsum('bsgc,gcd->bsgd', pooled, pool_w).reshape(bsz, s_len, POOL_WIDTH)
    return (mapped * pool_scale) @ w_out

def memory_cross_attention(x, mem, wq, wkv, wo):
    bsz, s_len, _ = x.shape
    q = (x @ wq).reshape(bsz, s_len, X_HEADS, X_HEAD_DIM)
    kv = (mem @ wkv).reshape(bsz, mem.shape[1], 2, X_HEADS, X_HEAD_DIM)
    k, v = kv[:, :, 0], kv[:, :, 1]
    s = jnp.einsum('bshd,bmhd->bhsm', q, k).astype(jnp.float32) * (X_HEAD_DIM ** -0.5)
    p = jax.nn.softmax(s, axis=-1).astype(v.dtype)
    o = jnp.einsum('bhsm,bmhd->bshd', p, v).reshape(bsz, s_len, D_MODEL)
    return o @ wo

def grouped_moe(x, router_w, router_bias, w_gate, w_up, w_down):
    bsz, s_len, d = x.shape
    xt = x.reshape(-1, d)
    scores = jax.nn.softmax((xt @ router_w).astype(jnp.float32), axis=-1)
    biased = scores + router_bias.astype(jnp.float32)
    grouped = biased.reshape(-1, N_EXPERT_GROUPS, EXPERTS_PER_GROUP)
    group_score = jnp.sum(lax.top_k(grouped, TOP_K)[0], axis=-1)
    g_sel = jnp.argmax(group_score, axis=-1)
    in_group = jnp.take_along_axis(grouped, g_sel[:, None, None], axis=1)[:, 0]
    _, local_idx = lax.top_k(in_group, TOP_K)
    expert_idx = g_sel[:, None] * EXPERTS_PER_GROUP + local_idx
    sel = jnp.take_along_axis(scores, expert_idx, axis=1)
    weights = sel / jnp.sum(sel, axis=-1, keepdims=True)
    combine = jnp.sum(jax.nn.one_hot(expert_idx, N_EXPERTS, dtype=jnp.float32) * weights[..., None], axis=1)
    y = jnp.zeros(xt.shape, dtype=jnp.float32)
    for e in range(N_EXPERTS):
        he = jax.nn.silu(xt @ w_gate[e]) * (xt @ w_up[e])
        y = y + combine[:, e:e + 1] * (he @ w_down[e]).astype(jnp.float32)
    return y.astype(x.dtype).reshape(bsz, s_len, d)

def first_inputs(seed: int = 0) -> dict:
    key = jax.random.key(seed)
    keys = iter(jax.random.split(key, 64))
    f32 = jnp.float32

    def nrm(shape, scale):
        return jax.random.normal(next(keys), shape, f32) * scale

    def gain(n):
        return 1.0 + nrm((n,), 0.05)

    def bias(n):
        return nrm((n,), 0.02)

    inp = {}
    inp["x"] = nrm((BATCH, SEQ, D_MODEL), 1.0)
    inp["mem"] = nrm((BATCH, MEM_LEN, D_MODEL), 1.0)
    offset = jax.random.randint(next(keys), (BATCH, 1), 0, 4096, dtype=jnp.int32)
    inp["positions"] = (offset + jnp.arange(SEQ, dtype=jnp.int32)[None, :]).astype(jnp.int32)
    inp["router_w"] = nrm((D_MODEL, N_EXPERTS), D_MODEL ** -0.5)
    inp["router_bias"] = nrm((N_EXPERTS,), 0.01)

    def common(prefix):
        inp[prefix + "ln1_g"] = gain(D_MODEL)
        inp[prefix + "ln1_b"] = bias(D_MODEL)
        inp[prefix + "xq"] = nrm((D_MODEL, D_MODEL), D_MODEL ** -0.5)
        inp[prefix + "xkv"] = nrm((D_MODEL, 2 * D_MODEL), D_MODEL ** -0.5)
        inp[prefix + "xo"] = nrm((D_MODEL, D_MODEL), BETA * D_MODEL ** -0.5)
        inp[prefix + "ln2_g"] = gain(D_MODEL)
        inp[prefix + "ln2_b"] = bias(D_MODEL)
        inp[prefix + "e_gate"] = nrm((N_EXPERTS, D_MODEL, D_EXPERT), D_MODEL ** -0.5)
        inp[prefix + "e_up"] = nrm((N_EXPERTS, D_MODEL, D_EXPERT), D_MODEL ** -0.5)
        inp[prefix + "e_down"] = nrm((N_EXPERTS, D_EXPERT, D_MODEL), BETA * D_EXPERT ** -0.5)
        inp[prefix + "ln3_g"] = gain(D_MODEL)
        inp[prefix + "ln3_b"] = bias(D_MODEL)

    inp["l0_w_in"] = nrm((D_MODEL, EVEN_IN_WIDTH), D_MODEL ** -0.5)
    inp["l0_sinks"] = nrm((A_Q_HEADS,), 0.5)
    inp["l0_sgu_ln_g"] = gain(B_WIDTH)
    inp["l0_sgu_ln_b"] = bias(B_WIDTH)
    inp["l0_sgu_w"] = nrm((B_GROUPS, CHUNK, CHUNK), CHUNK ** -0.5)
    inp["l0_sgu_b"] = 1.0 + nrm((B_GROUPS, CHUNK), 0.1)
    inp["l0_w_out"] = nrm((EVEN_MIX_WIDTH, D_MODEL), BETA * EVEN_MIX_WIDTH ** -0.5)
    common("l0_")
    inp["l1_w_in"] = nrm((D_MODEL, POOL_WIDTH), D_MODEL ** -0.5)
    inp["l1_pool_w"] = nrm((POOL_GROUPS, POOL_GROUP_DIM, POOL_GROUP_DIM), POOL_GROUP_DIM ** -0.5)
    inp["l1_pool_scale"] = 1.0 + nrm((POOL_WIDTH,), 0.1)
    inp["l1_w_out"] = nrm((POOL_WIDTH, D_MODEL), BETA * POOL_WIDTH ** -0.5)
    common("l1_")

    order = ["x", "mem", "positions", "router_w", "router_bias",
             "l0_w_in", "l0_sinks", "l0_sgu_ln_g", "l0_sgu_ln_b", "l0_sgu_w", "l0_sgu_b", "l0_w_out",
             "l0_ln1_g", "l0_ln1_b", "l0_xq", "l0_xkv", "l0_xo", "l0_ln2_g", "l0_ln2_b",
             "l0_e_gate", "l0_e_up", "l0_e_down", "l0_ln3_g", "l0_ln3_b",
             "l1_w_in", "l1_pool_w", "l1_pool_scale", "l1_w_out",
             "l1_ln1_g", "l1_ln1_b", "l1_xq", "l1_xkv", "l1_xo", "l1_ln2_g", "l1_ln2_b",
             "l1_e_gate", "l1_e_up", "l1_e_down", "l1_ln3_g", "l1_ln3_b"]
    return {name: inp[name] for name in order}

def first_block(x, mem, positions, router_w, router_bias,
              l0_w_in, l0_sinks, l0_sgu_ln_g, l0_sgu_ln_b, l0_sgu_w, l0_sgu_b, l0_w_out,
              l0_ln1_g, l0_ln1_b, l0_xq, l0_xkv, l0_xo, l0_ln2_g, l0_ln2_b,
              l0_e_gate, l0_e_up, l0_e_down, l0_ln3_g, l0_ln3_b,
              l1_w_in, l1_pool_w, l1_pool_scale, l1_w_out,
              l1_ln1_g, l1_ln1_b, l1_xq, l1_xkv, l1_xo, l1_ln2_g, l1_ln2_b,
              l1_e_gate, l1_e_up, l1_e_down, l1_ln3_g, l1_ln3_b):
    mixer_params = [
        (l0_w_in, l0_sinks, l0_sgu_ln_g, l0_sgu_ln_b, l0_sgu_w, l0_sgu_b, l0_w_out),
        (l1_w_in, l1_pool_w, l1_pool_scale, l1_w_out),
    ]
    layer_params = [
        (l0_ln1_g, l0_ln1_b, l0_xq, l0_xkv, l0_xo, l0_ln2_g, l0_ln2_b,
         l0_e_gate, l0_e_up, l0_e_down, l0_ln3_g, l0_ln3_b),
        (l1_ln1_g, l1_ln1_b, l1_xq, l1_xkv, l1_xo, l1_ln2_g, l1_ln2_b,
         l1_e_gate, l1_e_up, l1_e_down, l1_ln3_g, l1_ln3_b),
    ]
    for layer in range(DEPTH):
        if layer % 2 == 0:
            mix = even_mixer(x, positions, *mixer_params[layer])
        else:
            mix = odd_mixer(x, *mixer_params[layer])
        (ln1_g, ln1_b, xq, xkv, xo, ln2_g, ln2_b,
         e_gate, e_up, e_down, ln3_g, ln3_b) = layer_params[layer]
        x = layer_norm(ALPHA * x + mix, ln1_g, ln1_b)
        x = layer_norm(ALPHA * x + memory_cross_attention(x, mem, xq, xkv, xo), ln2_g, ln2_b)
        x = layer_norm(ALPHA * x + grouped_moe(x, router_w, router_bias, e_gate, e_up, e_down), ln3_g, ln3_b)
    return x


GRID_W = 64
CTX_LEN = 256
N_MIXERS = 3
Q_BLOCK = 128
ROPE_BASE = 10000.0
NORM_EPS = 1e-6

DIFF_DH = 64
DIFF_HEADS = D_MODEL // (2 * DIFF_DH)
GQA_DH = 128
GQA_HEADS = D_MODEL // GQA_DH
GQA_KV_HEADS = max(GQA_HEADS // 4, 1)
GQA_GROUP = GQA_HEADS // GQA_KV_HEADS
GLA_HEADS = 4
GLA_DK = D_MODEL // 2
GLA_DV = D_MODEL
GLA_DK_H = GLA_DK // GLA_HEADS
GLA_DV_H = GLA_DV // GLA_HEADS
GLA_GATE_RANK = 16
GLA_TAU = 16.0
GLA_CHUNK = 64
FFN_HIDDEN = ((8 * D_MODEL // 3 + 255) // 256) * 256

N_A = len(range(0, DEPTH, N_MIXERS))
N_B = len(range(1, DEPTH, N_MIXERS))
N_C = len(range(2, DEPTH, N_MIXERS))


def rmsnorm(x, g):
    x32 = x.astype(jnp.float32)
    y = x32 * lax.rsqrt(jnp.mean(x32 * x32, axis=-1, keepdims=True) + NORM_EPS)
    return (y * g.astype(jnp.float32)).astype(x.dtype)

def modulate(t, shift, scale):
    return t * (1 + scale) + shift

def swiglu(t, w_gu, w_down):
    gate, up = jnp.split(t @ w_gu, 2, axis=-1)
    return (jax.nn.silu(gate) * up) @ w_down

def axial_rope_tables(n_tokens, head_dim):
    rows = n_tokens // GRID_W
    row = jnp.broadcast_to(jnp.arange(rows)[:, None], (rows, GRID_W)).reshape(-1)
    col = jnp.broadcast_to(jnp.arange(GRID_W)[None, :], (rows, GRID_W)).reshape(-1)
    half = head_dim // 2
    inv = ROPE_BASE ** (-jnp.arange(0, half, 2, dtype=jnp.float32) / half)

    def axis_angles(pos):
        a = pos.astype(jnp.float32)[:, None] * inv[None, :]
        return jnp.concatenate([a, a], axis=-1)

    ang = jnp.concatenate([axis_angles(row), axis_angles(col)], axis=-1)
    return jnp.cos(ang), jnp.sin(ang)

def apply_axial_rope(x, cos, sin):
    q = x.shape[-1] // 4
    x32 = x.astype(jnp.float32)
    xr = x32.reshape(*x.shape[:-1], 2, 2, q)
    rot = jnp.stack([-xr[..., 1, :], xr[..., 0, :]], axis=-2).reshape(x.shape)
    return (x32 * cos + rot * sin).astype(x.dtype)

def sweep_query_blocks(fn, q):
    B, H, L, d = q.shape
    nb = L // Q_BLOCK
    qb = q.reshape(B, H, nb, Q_BLOCK, d).transpose(2, 0, 1, 3, 4)
    out = lax.map(fn, qb)
    return out.transpose(1, 2, 0, 3, 4).reshape(B, out.shape[2], L, out.shape[-1])

def diff_attention(h, hc, w_in, w_out, q_norm, k_norm, lq1, lk1, lq2, lk2, subln, lambda_init, ctx_out):
    f32 = jnp.float32
    L = h.shape[1]

    def project(t):
        Bt, Lt, _ = t.shape
        q, k, v = jnp.split(t @ w_in, 3, axis=-1)
        q = rmsnorm(q.reshape(Bt, Lt, 2 * DIFF_HEADS, DIFF_DH), q_norm).transpose(0, 2, 1, 3)
        k = rmsnorm(k.reshape(Bt, Lt, 2 * DIFF_HEADS, DIFF_DH), k_norm).transpose(0, 2, 1, 3)
        v = v.reshape(Bt, Lt, DIFF_HEADS, 2 * DIFF_DH).transpose(0, 2, 1, 3)
        return q, k, v

    q, k, v = project(h)
    qc, kc, vc = project(hc)
    cos, sin = axial_rope_tables(L, DIFF_DH)
    q = apply_axial_rope(q, cos, sin)
    k = apply_axial_rope(k, cos, sin)
    lam = (jnp.exp(jnp.sum(lq1.astype(f32) * lk1.astype(f32)))
           - jnp.exp(jnp.sum(lq2.astype(f32) * lk2.astype(f32))) + lambda_init)

    def pair(t):
        return t.reshape(t.shape[0], DIFF_HEADS, 2, t.shape[2], t.shape[3])

    def attend(qb, keys, vals):
        s = jnp.einsum('bhmtd,bhmsd->bhmts', pair(qb), keys).astype(f32) * DIFF_DH ** -0.5
        p = jax.nn.softmax(s, axis=-1)
        a = (p[:, :, 0] - lam * p[:, :, 1]).astype(vals.dtype)
        return jnp.einsum('bhts,bhse->bhte', a, vals)

    def finish(o):
        Bt, _, Lt, _ = o.shape
        o = rmsnorm(o, subln) * (1.0 - lambda_init)
        return o.transpose(0, 2, 1, 3).reshape(Bt, Lt, DIFF_HEADS * 2 * DIFF_DH) @ w_out

    keys = pair(jnp.concatenate([kc, k], axis=2))
    vals = jnp.concatenate([vc, v], axis=2)
    y = finish(sweep_query_blocks(lambda qb: attend(qb, keys, vals), q))
    yc = finish(attend(qc, pair(kc), vc)) if ctx_out else None
    return y, yc

def gqa_attention(h, hc, w_in, w_out, q_norm, k_norm, ctx_out):
    f32 = jnp.float32
    L = h.shape[1]
    kv_w = GQA_KV_HEADS * GQA_DH

    def project(t):
        Bt, Lt, _ = t.shape
        q, k, v = jnp.split(t @ w_in, [GQA_HEADS * GQA_DH, GQA_HEADS * GQA_DH + kv_w], axis=-1)
        q = rmsnorm(q.reshape(Bt, Lt, GQA_HEADS, GQA_DH), q_norm).transpose(0, 2, 1, 3)
        k = rmsnorm(k.reshape(Bt, Lt, GQA_KV_HEADS, GQA_DH), k_norm).transpose(0, 2, 1, 3)
        v = v.reshape(Bt, Lt, GQA_KV_HEADS, GQA_DH).transpose(0, 2, 1, 3)
        return q, k, v

    q, k, v = project(h)
    qc, kc, vc = project(hc)
    cos, sin = axial_rope_tables(L, GQA_DH)
    q = apply_axial_rope(q, cos, sin)
    k = apply_axial_rope(k, cos, sin)

    def attend(qb, keys, vals):
        Bq, _, T, _ = qb.shape
        qg = qb.reshape(Bq, GQA_KV_HEADS, GQA_GROUP, T, GQA_DH)
        s = jnp.einsum('bkgtd,bksd->bkgts', qg, keys).astype(f32) * GQA_DH ** -0.5
        p = jax.nn.softmax(s, axis=-1).astype(vals.dtype)
        o = jnp.einsum('bkgts,bksd->bkgtd', p, vals)
        return o.reshape(Bq, GQA_HEADS, T, GQA_DH)

    def finish(o):
        Bt, _, Lt, _ = o.shape
        return o.transpose(0, 2, 1, 3).reshape(Bt, Lt, GQA_HEADS * GQA_DH) @ w_out

    keys = jnp.concatenate([kc, k], axis=2)
    vals = jnp.concatenate([vc, v], axis=2)
    y = finish(sweep_query_blocks(lambda qb: attend(qb, keys, vals), q))
    yc = finish(attend(qc, kc, vc)) if ctx_out else None
    return y, yc

def gla_chunk_scan(q, k, v, g, s0):
    f32 = jnp.float32
    B, H, L, _ = q.shape
    n = L // GLA_CHUNK
    mask = jnp.tril(jnp.ones((GLA_CHUNK, GLA_CHUNK), dtype=bool))[:, :, None]

    def to_chunks(t):
        return t.reshape(B, H, n, GLA_CHUNK, t.shape[-1]).transpose(2, 0, 1, 3, 4)

    def step(S, inp):
        qc, kc, vc, gc = inp
        qf, kf, vf = qc.astype(f32), kc.astype(f32), vc.astype(f32)
        b = jnp.cumsum(gc.astype(f32), axis=-2)
        o_inter = jnp.einsum('bhtk,bhkv->bhtv', qf * jnp.exp(b), S)
        rel = jnp.where(mask, b[:, :, :, None, :] - b[:, :, None, :, :], -jnp.inf)
        A = jnp.einsum('bhtk,bhtsk,bhsk->bhts', qf, jnp.exp(rel), kf)
        o = o_inter + jnp.einsum('bhts,bhsv->bhtv', A, vf)
        b_last = b[:, :, -1, :]
        S = jnp.exp(b_last)[..., None] * S + jnp.einsum(
            'bhsk,bhsv->bhkv', kf * jnp.exp(b_last[:, :, None, :] - b), vf)
        return S, o.astype(v.dtype)

    S, o = lax.scan(step, s0, (to_chunks(q), to_chunks(k), to_chunks(v), to_chunks(g)))
    o = o.transpose(1, 2, 0, 3, 4).reshape(B, H, L, v.shape[-1])
    return o, S

def gla_mixer(h, hc, w_in, gw1_f, gw2_f, gb_f, gw1_b, gw2_b, gb_b, out_norm, w_out, ctx_out):
    B = h.shape[0]

    def project(t):
        Bt, Lt, _ = t.shape
        q, k, v, r = jnp.split(t @ w_in, [GLA_DK, 2 * GLA_DK, 2 * GLA_DK + GLA_DV], axis=-1)

        def heads(z, e):
            return z.reshape(Bt, Lt, GLA_HEADS, e).transpose(0, 2, 1, 3)

        def log_decay(w1, w2, b):
            return heads(jax.nn.log_sigmoid(((t @ w1) @ w2 + b).astype(jnp.float32)) / GLA_TAU, GLA_DK_H)

        return (heads(q, GLA_DK_H) * GLA_DK_H ** -0.5, heads(k, GLA_DK_H), heads(v, GLA_DV_H), r,
                log_decay(gw1_f, gw2_f, gb_f), log_decay(gw1_b, gw2_b, gb_b))

    def flip(z):
        return jnp.flip(z, axis=2)

    q, k, v, r, g_f, g_b = project(h)
    qc, kc, vc, rc, gc_f, gc_b = project(hc)
    zeros = jnp.zeros((B, GLA_HEADS, GLA_DK_H, GLA_DV_H), jnp.float32)
    oc_f, sc_f = gla_chunk_scan(qc, kc, vc, gc_f, zeros)
    oc_b, sc_b = gla_chunk_scan(flip(qc), flip(kc), flip(vc), flip(gc_b), zeros)
    o_f, _ = gla_chunk_scan(q, k, v, g_f, sc_f)
    o_b, _ = gla_chunk_scan(flip(q), flip(k), flip(v), flip(g_b), sc_b)

    def finish(o, gate_in):
        Bt, _, Lt, _ = o.shape
        o = rmsnorm(o, out_norm).transpose(0, 2, 1, 3).reshape(Bt, Lt, GLA_DV)
        return (o * jax.nn.silu(gate_in)) @ w_out

    y = finish(o_f + flip(o_b), r)
    yc = finish(oc_f + flip(oc_b), rc) if ctx_out else None
    return y, yc

def second_inputs(seed: int = 0) -> dict:
    key = jax.random.key(seed)
    ks = jax.random.split(key, 32)
    f32 = jnp.float32
    D = D_MODEL

    def nrm(k, shape, scale):
        return scale * jax.random.normal(k, shape, f32)

    def gain(k, shape):
        return 1.0 + 0.02 * jax.random.normal(k, shape, f32)

    return {
        'x': nrm(ks[0], (BATCH, SEQ, D), 1.0),
        'c': nrm(ks[1], (BATCH, D), 1.0),
        'ctx': nrm(ks[2], (BATCH, CTX_LEN, D), 1.0),
        'c_ctx': nrm(ks[3], (D,), 1.0),
        'ada_w': nrm(ks[4], (DEPTH, D, 6 * D), 0.5 * D ** -0.5),
        'ada_b': nrm(ks[5], (DEPTH, 6 * D), 0.01),
        'norm1_g': gain(ks[6], (DEPTH, D)),
        'norm2_g': gain(ks[7], (DEPTH, D)),
        'ffn_w_gu': nrm(ks[8], (DEPTH, D, 2 * FFN_HIDDEN), D ** -0.5),
        'ffn_w_down': nrm(ks[9], (DEPTH, FFN_HIDDEN, D), FFN_HIDDEN ** -0.5),
        'diff_w_in': nrm(ks[10], (N_A, D, 3 * D), D ** -0.5),
        'diff_w_out': nrm(ks[11], (N_A, D, D), D ** -0.5),
        'diff_q_norm': gain(ks[12], (N_A, DIFF_DH)),
        'diff_k_norm': gain(ks[13], (N_A, DIFF_DH)),
        'diff_lambda_q1': nrm(ks[14], (N_A, DIFF_DH), 0.1),
        'diff_lambda_k1': nrm(ks[15], (N_A, DIFF_DH), 0.1),
        'diff_lambda_q2': nrm(ks[16], (N_A, DIFF_DH), 0.1),
        'diff_lambda_k2': nrm(ks[17], (N_A, DIFF_DH), 0.1),
        'diff_subln': gain(ks[18], (N_A, 2 * DIFF_DH)),
        'gqa_w_in': nrm(ks[19], (N_B, D, GQA_HEADS * GQA_DH + 2 * GQA_KV_HEADS * GQA_DH), D ** -0.5),
        'gqa_w_out': nrm(ks[20], (N_B, GQA_HEADS * GQA_DH, D), (GQA_HEADS * GQA_DH) ** -0.5),
        'gqa_q_norm': gain(ks[21], (N_B, GQA_DH)),
        'gqa_k_norm': gain(ks[22], (N_B, GQA_DH)),
        'gla_w_in': nrm(ks[23], (N_C, D, 2 * GLA_DK + 2 * GLA_DV), D ** -0.5),
        'gla_gate_w1_fwd': nrm(ks[24], (N_C, D, GLA_GATE_RANK), D ** -0.5),
        'gla_gate_w2_fwd': nrm(ks[25], (N_C, GLA_GATE_RANK, GLA_DK), GLA_GATE_RANK ** -0.5),
        'gla_gate_b_fwd': nrm(ks[26], (N_C, GLA_DK), 0.01),
        'gla_gate_w1_bwd': nrm(ks[27], (N_C, D, GLA_GATE_RANK), D ** -0.5),
        'gla_gate_w2_bwd': nrm(ks[28], (N_C, GLA_GATE_RANK, GLA_DK), GLA_GATE_RANK ** -0.5),
        'gla_gate_b_bwd': nrm(ks[29], (N_C, GLA_DK), 0.01),
        'gla_out_norm': gain(ks[30], (N_C, GLA_DV_H)),
        'gla_w_out': nrm(ks[31], (N_C, GLA_DV, D), GLA_DV ** -0.5),
    }

def second_block(x, c, ctx, c_ctx, ada_w, ada_b, norm1_g, norm2_g, ffn_w_gu, ffn_w_down,
              diff_w_in, diff_w_out, diff_q_norm, diff_k_norm, diff_lambda_q1, diff_lambda_k1,
              diff_lambda_q2, diff_lambda_k2, diff_subln, gqa_w_in, gqa_w_out, gqa_q_norm, gqa_k_norm,
              gla_w_in, gla_gate_w1_fwd, gla_gate_w2_fwd, gla_gate_b_fwd, gla_gate_w1_bwd,
              gla_gate_w2_bwd, gla_gate_b_bwd, gla_out_norm, gla_w_out):
    xc = ctx
    cond_lat = jax.nn.silu(c)
    cond_ctx = jax.nn.silu(c_ctx)
    for i in range(DEPTH):
        last = i == DEPTH - 1
        mod = (cond_lat @ ada_w[i] + ada_b[i])[:, None, :]
        modc = (cond_ctx @ ada_w[i] + ada_b[i])[None, None, :]
        sh1, sc1, g1, sh2, sc2, g2 = jnp.split(mod, 6, axis=-1)
        csh1, csc1, cg1, csh2, csc2, cg2 = jnp.split(modc, 6, axis=-1)

        h = modulate(rmsnorm(x, norm1_g[i]), sh1, sc1)
        hc = modulate(rmsnorm(xc, norm1_g[i]), csh1, csc1)
        kind, j = i % N_MIXERS, i // N_MIXERS
        if kind == 0:
            lambda_init = 0.8 - 0.6 * math.exp(-0.3 * i)
            y, yc = diff_attention(h, hc, diff_w_in[j], diff_w_out[j], diff_q_norm[j], diff_k_norm[j],
                                   diff_lambda_q1[j], diff_lambda_k1[j], diff_lambda_q2[j],
                                   diff_lambda_k2[j], diff_subln[j], lambda_init, not last)
        elif kind == 1:
            y, yc = gqa_attention(h, hc, gqa_w_in[j], gqa_w_out[j], gqa_q_norm[j], gqa_k_norm[j], not last)
        else:
            y, yc = gla_mixer(h, hc, gla_w_in[j], gla_gate_w1_fwd[j], gla_gate_w2_fwd[j], gla_gate_b_fwd[j],
                              gla_gate_w1_bwd[j], gla_gate_w2_bwd[j], gla_gate_b_bwd[j],
                              gla_out_norm[j], gla_w_out[j], not last)

        x = x + g1 * y
        x = x + g2 * swiglu(modulate(rmsnorm(x, norm2_g[i]), sh2, sc2), ffn_w_gu[i], ffn_w_down[i])
        if not last:
            xc = xc + cg1 * yc
            xc = xc + cg2 * swiglu(modulate(rmsnorm(xc, norm2_g[i]), csh2, csc2), ffn_w_gu[i], ffn_w_down[i])
    return x


def setup_inputs(seed=0):
    out = dict(first_inputs(seed))
    for name, value in second_inputs(seed + 1).items():
        if name != "x":
            out[name + "_2"] = value
    return out


def reference(
    x, mem, positions, router_w, router_bias, l0_w_in, l0_sinks, l0_sgu_ln_g, l0_sgu_ln_b,
    l0_sgu_w, l0_sgu_b, l0_w_out, l0_ln1_g, l0_ln1_b, l0_xq, l0_xkv, l0_xo, l0_ln2_g, l0_ln2_b,
    l0_e_gate, l0_e_up, l0_e_down, l0_ln3_g, l0_ln3_b, l1_w_in, l1_pool_w, l1_pool_scale,
    l1_w_out, l1_ln1_g, l1_ln1_b, l1_xq, l1_xkv, l1_xo, l1_ln2_g, l1_ln2_b, l1_e_gate, l1_e_up,
    l1_e_down, l1_ln3_g, l1_ln3_b, c_2, ctx_2, c_ctx_2, ada_w_2, ada_b_2, norm1_g_2, norm2_g_2,
    ffn_w_gu_2, ffn_w_down_2, diff_w_in_2, diff_w_out_2, diff_q_norm_2, diff_k_norm_2,
    diff_lambda_q1_2, diff_lambda_k1_2, diff_lambda_q2_2, diff_lambda_k2_2, diff_subln_2,
    gqa_w_in_2, gqa_w_out_2, gqa_q_norm_2, gqa_k_norm_2, gla_w_in_2, gla_gate_w1_fwd_2,
    gla_gate_w2_fwd_2, gla_gate_b_fwd_2, gla_gate_w1_bwd_2, gla_gate_w2_bwd_2, gla_gate_b_bwd_2,
    gla_out_norm_2, gla_w_out_2,
):
    x = first_block(
        x, mem, positions, router_w, router_bias, l0_w_in, l0_sinks, l0_sgu_ln_g, l0_sgu_ln_b,
        l0_sgu_w, l0_sgu_b, l0_w_out, l0_ln1_g, l0_ln1_b, l0_xq, l0_xkv, l0_xo, l0_ln2_g,
        l0_ln2_b, l0_e_gate, l0_e_up, l0_e_down, l0_ln3_g, l0_ln3_b, l1_w_in, l1_pool_w,
        l1_pool_scale, l1_w_out, l1_ln1_g, l1_ln1_b, l1_xq, l1_xkv, l1_xo, l1_ln2_g, l1_ln2_b,
        l1_e_gate, l1_e_up, l1_e_down, l1_ln3_g, l1_ln3_b,
    )
    return second_block(
        x, c_2, ctx_2, c_ctx_2, ada_w_2, ada_b_2, norm1_g_2, norm2_g_2, ffn_w_gu_2,
        ffn_w_down_2, diff_w_in_2, diff_w_out_2, diff_q_norm_2, diff_k_norm_2, diff_lambda_q1_2,
        diff_lambda_k1_2, diff_lambda_q2_2, diff_lambda_k2_2, diff_subln_2, gqa_w_in_2,
        gqa_w_out_2, gqa_q_norm_2, gqa_k_norm_2, gla_w_in_2, gla_gate_w1_fwd_2,
        gla_gate_w2_fwd_2, gla_gate_b_fwd_2, gla_gate_w1_bwd_2, gla_gate_w2_bwd_2,
        gla_gate_b_bwd_2, gla_out_norm_2, gla_w_out_2,
    )


_drawn_inputs = setup_inputs


def setup_inputs(seed=0):
    import zlib

    import numpy as np

    out = dict(_drawn_inputs(seed))
    spreads = {}
    factors = {'l0_sinks': 8.0,
     'l0_sgu_ln_b': 5.392,
     'ada_b_2': 3.25,
     'norm1_g_2': 8.0,
     'norm2_g_2': 6.848,
     'diff_q_norm_2': 8.0,
     'diff_k_norm_2': 8.0,
     'diff_lambda_q1_2': 64.0,
     'diff_lambda_k1_2': 64.0,
     'diff_lambda_q2_2': 8.0,
     'diff_lambda_k2_2': 8.0,
     'diff_subln_2': 8.0,
     'gqa_q_norm_2': 8.0,
     'gqa_k_norm_2': 8.0}
    for name, (base, spread) in spreads.items():
        noise = np.random.default_rng([zlib.crc32(name.encode()), seed]).standard_normal(out[name].shape)
        drawn = base * np.exp(spread * noise) if base else spread * noise
        out[name] = jnp.asarray(drawn.astype(out[name].dtype))
    for name, factor in factors.items():
        out[name] = (out[name] * factor).astype(out[name].dtype)
    return out
```

```python
from contextlib import ExitStack
import math

import numpy as np
import concourse.bass as bass
from concourse import mybir

F32 = mybir.dt.float32
F32R = mybir.dt.float32r
I32 = mybir.dt.int32
ACT = mybir.ActivationFunctionType
ALU = mybir.AluOpType
AXX = mybir.AxisListType.X

P = 128
TOK = 256
NT = TOK // P
D = 1024
KC = D // P
TILE = 2048
RAW, RING = 3, 4
LOOP_TILES = 12
F_EXPERT, N_EXP, N_GRP = 512, 16, 4
F_FFN = 2816
ALPHA = 4.0 ** 0.25
LN_EPS, RMS_EPS = 1e-5, 1e-6
WINDOWS = (2, 4, 8, 16)
LAMBDA_INIT = 0.8 - 0.6 * math.exp(0.0)
TWO_PI = 2.0 * math.pi
PI_HI, PI_MID = 6.28125, float(np.float32(0.0019350051879882812))
PI_LO = TWO_PI - PI_HI - PI_MID
ROUND = 12582912.0

C_LAT, C_CTX, C_N1, C_N2, C_POOL, C_SGUB, C_ROWS = 0, 8, 16, 32, 48, 56, 64
B_SINK, B_RBIAS, B_DQ, B_DK, B_SUB, B_GQ, B_GK, B_LAM, B_INVF, B_COLS = 0, 8, 24, 88, 152, 280, 408, 536, 792, 800


N_SETUP = 24


def gated_tiles(n_f):
    return n_f + n_f // 2


TOTAL = (2 * 12 * 2
         + 12 + 4 + gated_tiles(F_FFN // P) + 2
         + 7 + 5 + 2 * (4 + 8 + 4 + 4 + gated_tiles(N_EXP * F_EXPERT // P))
         + 12 + 4 + gated_tiles(F_FFN // P)
         + 6 + 4 + gated_tiles(F_FFN // P))


class Count:

    STRIDE = dict(tile=LOOP_TILES, wb=8, gu=8)

    def __init__(self):
        self.n = {}
        self.i = None

    def get(self, name):
        return self.n.get(name, 0)

    def add(self, name, k=1):
        self.n[name] = self.get(name) + k

    def at(self, name, offset=0):
        value = self.get(name) + offset
        return value if self.i is None else self.i * self.STRIDE[name] + value

    def enter(self, i):
        self.i, self.entered = i, dict(self.n)

    def leave(self, iterations):
        self.i = None
        for name, stride in self.STRIDE.items():
            gone = self.get(name) - self.entered.get(name, 0)
            assert gone in (0, stride), (name, gone)
            self.add(name, gone * (iterations - 1))


def steps_of(n_f):
    steps = n_f // 2 - 1
    return steps, (steps - 1) // 4


def build(nc, A, out):
    ctx = ExitStack()
    with ctx:
        def sb(name, shape, dt=F32):
            return ctx.enter_context(nc.sbuf_tensor(name, shape, dt))

        def sem(name):
            return ctx.enter_context(nc.semaphore(name))

        def dram(name, shape):
            return nc.dram_tensor(name, shape, F32, kind="Internal").ap()

        raw = sb("raw", [P, RAW, TILE])
        w_hi = sb("w_hi", [P, RING, TILE], F32R)
        w_lo = sb("w_lo", [P, RING, TILE], F32R)
        X = sb("X", [P, NT, D])
        at_hi = sb("at_hi", [P, KC, TOK], F32R)
        at_lo = sb("at_lo", [P, KC, TOK], F32R)
        he_hi = sb("he_hi", [P, 4, TOK], F32R)
        he_lo = sb("he_lo", [P, 4, TOK], F32R)
        H = sb("H", [P, NT, 2048])
        KT = sb("KT", [P, KC, 512])
        V = sb("V", [P, 4, D])
        QT = sb("QT", [P, KC, TOK])
        PB = sb("PB", [P, 4, 512])
        PT = sb("PT", [P, 2, 4, TOK])
        PRM = sb("PRM", [P, 2, D])
        TAB = sb("TAB", [P, 512])
        ident = sb("ident", [P, P])
        colin = sb("colin", [P, P])
        col = sb("col", [P, C_ROWS])
        modcol = sb("modcol", [P, 2, 96])
        affA = sb("affA", [P, KC])
        bc = sb("bc", [P, B_COLS])
        rw = sb("rw", [P, KC, N_EXP])
        rw_hi = sb("rw_hi", [P, KC, N_EXP], F32R)
        rw_lo = sb("rw_lo", [P, KC, N_EXP], F32R)
        cond = sb("cond", [P, 2, KC])
        cond_hi = sb("cond_hi", [P, KC, 2], F32R)
        cond_lo = sb("cond_lo", [P, KC, 2], F32R)
        pos_i = sb("pos_i", [P, NT], I32)
        pos_f = sb("pos_f", [P, NT])
        trig = sb("trig", [P, 4, NT, 8])
        lam = sb("lam", [P, 4])
        bn = sb("bn", [P, 2, 6])
        mv = sb("mv", [P, 2])
        st = sb("st", [P, 8, 4])
        hs = sb("hs", [P, 3, 32])
        rt = sb("rt", [P, 12, NT, N_EXP])
        PS = ctx.enter_context(nc.psum_tensor("PS", [P, 8, 512], F32))

        mods_d = dram("mods_d", (2, 12 * D))
        kd_d, vd_d = dram("kd_d", (P, KC, TOK)), dram("vd_d", (P, NT, D))
        kg_d, vg_d = dram("kg_d", (P, 2, TOK)), dram("vg_d", (P, NT, TOK))

        raw_landed = [sem(f"raw_landed{i}") for i in range(RAW)]
        hi_done = sem("hi_done")
        lo_done = sem("lo_done")
        tile_used = sem("tile_used")
        wb_full, wb_freed = sem("wb_full"), sem("wb_freed")
        y_freed = sem("y_freed")
        o_full = sem("o_full")
        t_full, t_freed = sem("t_full"), sem("t_freed")
        src_ready = sem("src_ready")
        hi_evac = sem("hi_evac")
        aff_ready = sem("aff_ready")
        stat_ready = sem("stat_ready")
        stat_done = sem("stat_done")
        max_ready, exp_done, p_ready = sem("max_ready"), sem("exp_done"), sem("p_ready")
        silu_done, he_f32, he_hi_done, he_ready = sem("silu_done"), sem("he_f32"), sem("he_hi_done"), sem("he_ready")
        dve_step = sem("dve_step")
        act_step = sem("act_step")
        setup_landed, x_landed, tab_landed, prm_landed = sem("setup_landed"), sem("x_landed"), sem("tab_landed"), sem("prm_landed")
        prm_used = sem("prm_used")
        mod_out, mod_in = sem("mod_out"), sem("mod_in")
        kv_out, kv_in = sem("kv_out"), sem("kv_in")
        result_ready = sem("result_ready")
        out_done = sem("out_done")

        PBf = PB[:, :, :].rearrange("p a b -> p (a b)")
        KTf = KT[:, :, :].rearrange("p a b -> p (a b)")
        Vf = V[:, :, :].rearrange("p a b -> p (a b)")
        Hf = H[:, :, :].rearrange("p a b -> p (a b)")
        QTf = QT[:, :, :].rearrange("p a b -> p (a b)")
        sgu_raw = KTf[:, 2048:3072].rearrange("p (g s) -> p g s", g=8)
        WT = QTf[:, 1024:2048].rearrange("p (g t) -> p g t", g=8)
        cbc = KTf.rearrange("p (e t) -> p e t", t=TOK)
        silu_buf = PBf[:, 0:512].rearrange("p (s t) -> p s t", s=2)
        he_buf = PBf[:, 512:1024].rearrange("p (s t) -> p s t", s=2)
        BAND = V[:, 0:2, :].rearrange("p a (g t) -> p a g t", g=4)

        mods_rows = mods_d.rearrange("c (l r p) -> l c r p", l=2, p=P)

        def gate_of(cnd, layer, part):
            lo = layer * 6 * D + part * D
            return mods_d[cnd:cnd + 1, lo:lo + D].rearrange("a d -> (a d)").partition_broadcast(P)

        def rowb(ap):
            return ap.partition_broadcast(P)

        prm_loads = []
        for part in (2, 5):
            prm_loads.append([(0, gate_of(1, 0, part))])
        prm_loads.append([(0, (A["l0_sgu_ln_g"], A["l0_sgu_ln_b"]))])
        for layer in (0, 1):
            for n in (1, 2, 3):
                prm_loads.append([(0, rowb(A[f"l{layer}_ln{n}_g"])), (1, rowb(A[f"l{layer}_ln{n}_b"]))])
        for layer in (0, 1):
            for part in (2, 5):
                prm_loads.append([(0, gate_of(0, layer, part))])

        ada = [A["ada_w_2"][i] for i in range(2)]
        gu_w = [A["ffn_w_gu_2"][i] for i in range(2)]
        dn_w = [A["ffn_w_down_2"][i] for i in range(2)]
        diff_in, diff_out = A["diff_w_in_2"][0], A["diff_w_out_2"][0]
        gqa_in, gqa_out = A["gqa_w_in_2"][0], A["gqa_w_out_2"][0]

        block = ctx.enter_context(nc.Block())

        @block.sync
        def _(sp):
            c = Count()

            def load(pieces):
                n = c.get("tile")
                slot = n % RAW
                if n >= RAW:
                    sp.wait_ge(lo_done, c.at("tile", 1 - RAW))
                for dst, src in pieces(raw[:, slot, :]):
                    sp.dma_start(dst, src).then_inc(raw_landed[slot], 16)
                c.add("tile")

            def cols512(w, n0):
                for h in range(2):
                    def pieces(t, h=h):
                        v = t.rearrange("p (k n) -> p k n", n=512)
                        s = w[h * 512:(h + 1) * 512, n0:n0 + 512].rearrange("(k p) n -> p k n", p=P)
                        return [(v[:, 2 * j:2 * j + 2, :], s[:, 2 * j:2 * j + 2, :]) for j in range(2)]
                    load(pieces)

            def cols256(w, n0):
                def pieces(t):
                    v = t.rearrange("p (k n) -> p k n", n=256)
                    s = w[:, n0:n0 + 256].rearrange("(k p) n -> p k n", p=P)
                    return [(v[:, 4 * j:4 * j + 4, :], s[:, 4 * j:4 * j + 4, :]) for j in range(2)]
                load(pieces)

            def gated(gate, up, down, n_f):
                def gu(q, f):
                    def pieces(t):
                        v = t.rearrange("p (g k n) -> p g k n", g=2, n=P)
                        return [(v[:, g, :, :], w(q, f).rearrange("(k p) n -> p k n", p=P))
                                for g, w in enumerate((gate, up))]
                    load(pieces)

                def dn(q, f):
                    def pieces(t):
                        v = t.rearrange("p (j n) -> p j n", j=2)
                        return [(v[:, j, :], down(q, f + j)) for j in range(2)]
                    load(pieces)

                steps, loops = steps_of(n_f)
                gu(0, 0)
                gu(0, 1)

                def step(q, m):
                    gu(q, 2 * m + 2)
                    gu(q, 2 * m + 3)
                    dn(q, 2 * m)
                step(0, 0)
                with sp.Fori(0, loops) as i:
                    c.enter(i)
                    for m in range(1, 5):
                        step(i, m)
                    c.leave(loops)
                for m in range(1 + 4 * loops, steps):
                    step(0, m)
                dn(0, 2 * steps)

            def ffn(layer):
                gu = gu_w[layer].rearrange("k (f n) -> k f n", n=P)
                dn = dn_w[layer].rearrange("(f p) n -> f p n", p=P)
                gated(lambda q, f: gu[:, q * 8 + f, :], lambda q, f: gu[:, q * 8 + (f + F_FFN // P), :],
                      lambda q, f: dn[q * 8 + f], F_FFN // P)

            def moe(layer):
                g, u, dw = (A[f"l{layer}_e_{s}"] for s in ("gate", "up", "down"))
                nf = F_EXPERT // P

                def part(w):
                    return lambda q, f: w[q * 2 + f // nf, :, (f % nf) * P:(f % nf + 1) * P]

                def down(q, f):
                    return dw[q * 2 + f // nf, (f % nf) * P:(f % nf + 1) * P, :]
                gated(part(g), part(u), down, N_EXP * nf)

            def gemm(w, n0, n1):
                for n in range(n0, n1, 512):
                    cols512(w, n)

            def by256(w, n0, n1):
                for n in range(n0, n1, 256):
                    cols256(w, n)

            for layer in range(2):
                gemm(ada[layer], 0, 6 * D)
            gemm(diff_in, 0, 3 * D)
            gemm(diff_out, 0, D)
            ffn(0)
            gemm(gqa_in, D, D + 512)
            for layer in range(2):
                if layer == 0:
                    gemm(A["l0_w_in"], 0, 1536)
                    cols256(A["l0_w_in"], 1536)
                else:
                    gemm(A["l1_w_in"], 0, D)
                    pw = A["l1_pool_w"].rearrange("g (c p) d -> p g c d", p=P)
                    load(lambda t: [(t.rearrange("p (g c d) -> p g c d", g=4, c=2)[:, :, j, :], pw[:, :, j, :])
                                    for j in range(2)])
                gemm(A[f"l{layer}_w_out"], 0, D)
                by256(A[f"l{layer}_xkv"], 0, D)
                gemm(A[f"l{layer}_xkv"], D, 2 * D)
                by256(A[f"l{layer}_xq"], 0, D)
                gemm(A[f"l{layer}_xo"], 0, D)
                moe(layer)
            gemm(diff_in, 0, 3 * D)
            gemm(diff_out, 0, D)
            ffn(0)
            gemm(gqa_in, 0, D + 512)
            gemm(gqa_out, 0, D)
            ffn(1)
            assert c.get("tile") == TOTAL
            sp.wait_ge(result_ready, 1)
            sp.dma_start(out[0].rearrange("(t p) d -> p t d", p=P), X[:, :, :]).then_inc(out_done, 16)
            sp.wait_ge(out_done, 16)
            sp.wait_ge(mod_out, 48)
            sp.wait_ge(kv_out, 64)

        @block.gpsimd
        def _(pool):
            c = Count()

            def lo():
                n = c.get("tile")
                pool.wait_ge(hi_done, c.at("tile", 1))
                nc.gpsimd.tensor_tensor(w_lo[:, n % RING, :], raw[:, n % RAW, :],
                                        w_hi[:, n % RING, :].bitcast(F32), ALU.subtract).then_inc(lo_done, 1)
                c.add("tile")

            loops = TOTAL // LOOP_TILES
            with pool.Fori(0, loops) as i:
                c.enter(i)
                for _ in range(LOOP_TILES):
                    lo()
                c.leave(loops)
            for _ in range(TOTAL - loops * LOOP_TILES):
                lo()

        @block.tensor
        def _(pe):
            c = Count()

            def tile_wait():
                pe.wait_ge(lo_done, c.at("tile", 1))
                slot = c.get("tile") % RING
                return w_hi[:, slot, :], w_lo[:, slot, :]

            def tile_end(ins):
                ins.then_inc(tile_used, 1)
                c.add("tile")

            def wb_wait():
                if c.get("wb") >= 4:
                    pe.wait_ge(wb_freed, c.at("wb", -3))
                bank = PS[:, 4 + c.get("wb") % 4, :]
                c.add("wb")
                return bank

            def y_wait(pairs=1):
                if c.get("y") + pairs > 2:
                    pe.wait_ge(y_freed, c.get("y") + pairs - 2)
                at = c.get("y")
                c.add("y", pairs)
                return at % 2

            def parts(dst, s_hi, s_lo, m_hi, m_lo, first, last):
                pe.matmul(dst, s_hi, m_hi, start=first, stop=False)
                pe.matmul(dst, s_hi, m_lo, start=False, stop=False)
                return pe.matmul(dst, s_lo, m_hi, start=False, stop=last)

            def at_wait():
                pe.wait_ge(wb_freed, c.at("wb"))

            def transpose_src(n=1):
                c.add("src", n)
                pe.wait_ge(src_ready, c.get("src"))

            def to_at(src):
                for t in range(NT):
                    transpose_src()
                    for h in range(2):
                        bank = wb_wait()
                        for j in range(4):
                            k = 4 * h + j
                            ins = pe.transpose(bank[:, j * P:(j + 1) * P], src[:, t, k * P:(k + 1) * P], ident[:, :])
                        ins.then_inc(wb_full, 1)
                at_wait()

            def gemm(groups, width=512):
                for _ in range(groups):
                    pair = y_wait()
                    tiles = width * KC // TILE
                    for h in range(tiles):
                        hi, lo = tile_wait()
                        nk = KC // tiles
                        for kk in range(nk):
                            k = h * nk + kk
                            for t in range(NT):
                                ins = parts(PS[:, 2 * pair + t, 0:width],
                                            at_hi[:, k, t * P:(t + 1) * P], at_lo[:, k, t * P:(t + 1) * P],
                                            hi[:, kk * width:(kk + 1) * width], lo[:, kk * width:(kk + 1) * width],
                                            k == 0, k == KC - 1)
                        tile_end(ins)

            def gemm_t(tiles):
                for _ in range(tiles):
                    bank = wb_wait()
                    hi, lo = tile_wait()
                    for m in range(2):
                        for k in range(KC):
                            at = k * 256 + m * P
                            ins = parts(bank[:, m * TOK:(m + 1) * TOK], hi[:, at:at + P], lo[:, at:at + P],
                                        at_hi[:, k, :], at_lo[:, k, :], k == 0, k == KC - 1)
                    tile_end(ins)

            def gated(n_f):
                pair = y_wait(2)

                def gu():
                    bank = wb_wait()
                    hi, lo = tile_wait()
                    for g in range(2):
                        for k in range(KC):
                            at = (g * KC + k) * P
                            ins = parts(bank[:, g * TOK:(g + 1) * TOK], hi[:, at:at + P], lo[:, at:at + P],
                                        at_hi[:, k, :], at_lo[:, k, :], k == 0, k == KC - 1)
                    tile_end(ins)

                def dn(first, last):
                    c.add("gu", 2)
                    pe.wait_ge(he_ready, c.at("gu"))
                    hi, lo = tile_wait()
                    f0 = (c.get("gu") - 2) % 4
                    for j in range(2):
                        for t in range(NT):
                            s_hi = he_hi[:, f0 + j, t * P:(t + 1) * P]
                            s_lo = he_lo[:, f0 + j, t * P:(t + 1) * P]
                            for n in range(2):
                                at = j * D + n * 512
                                ins = parts(PS[:, 2 * ((pair + n) % 2) + t, :], s_hi, s_lo, hi[:, at:at + 512],
                                            lo[:, at:at + 512], first and j == 0, last and j == 1)
                    tile_end(ins)

                steps, loops = steps_of(n_f)
                gu()
                gu()

                def step(first=False):
                    gu()
                    gu()
                    dn(first, False)
                step(True)
                with pe.Fori(0, loops) as i:
                    c.enter(i)
                    for _ in range(4):
                        step()
                    c.leave(loops)
                for _ in range(1 + 4 * loops, steps):
                    step()
                dn(False, True)

            def attention(n, s_groups, scores, n_chunks, pv):
                pe.wait_ge(y_freed, c.get("y"))
                pe.wait_ge(wb_freed, c.get("wb"))

                def transposed(i):
                    c.add("p")
                    pe.wait_ge(p_ready, c.get("p"))
                    if c.get("t") >= 2:
                        pe.wait_ge(t_freed, c.get("t") - 1)
                    bank = PS[:, 1 + 2 * (c.get("t") % 2), :]
                    for j in range(n_chunks(i)):
                        ins = pe.transpose(bank[:, j * P:(j + 1) * P], prob(i, n_chunks(i))[:, j * P:(j + 1) * P], ident[:, :])
                    ins.then_inc(t_full, 1)
                    c.add("t")

                def prob(i, _):
                    return PB[:, i % 4, :] if s_groups == 1 else PB[:, 2 * (i % 2), :]

                base = c.get("t")
                for it in range(n + 3):
                    if it < n:
                        for g in range(s_groups):
                            bank = wb_wait()
                            scores(it, g, bank).then_inc(wb_full, 1)
                    if 0 <= it - 2 < n:
                        transposed(it - 2)
                    if 0 <= it - 3 < n:
                        pe.wait_ge(t_freed, base + it - 2)
                        pv(it - 3)
                pe.wait_ge(t_freed, c.get("t"))

            def o_bank():
                pair = y_wait()
                return PS[:, 2 * pair, :]

            def to_cols(srcs):
                for at in range(0, len(srcs), 4):
                    bank = wb_wait()
                    for j, s in enumerate(srcs[at:at + 4]):
                        ins = pe.transpose(bank[:, j * P:(j + 1) * P], s, ident[:, :])
                    ins.then_inc(wb_full, 1)

            pe.wait_ge(setup_landed, 16 * N_SETUP)
            bank = wb_wait()
            pe.transpose(bank[:, 0:C_ROWS], colin[0:C_ROWS, :], ident[0:C_ROWS, 0:C_ROWS]).then_inc(wb_full, 1)
            transpose_src()
            for _ in range(24):
                bank = wb_wait()
                for h in range(2):
                    hi, lo = tile_wait()
                    for kk in range(4):
                        k = 4 * h + kk
                        ins = parts(bank[0:2, :], cond_hi[:, k, :], cond_lo[:, k, :], hi[:, kk * 512:(kk + 1) * 512],
                                    lo[:, kk * 512:(kk + 1) * 512], k == 0, k == KC - 1)
                    tile_end(ins)
            pe.wait_ge(mod_in, 64)
            for layer in range(2):
                bank = wb_wait()
                pe.transpose(bank[:, 0:96], QT[0:96, layer, 0:P], ident[0:96, 0:96]).then_inc(wb_full, 1)

            def diff(path):
                nk = TOK * (1 + path)
                to_at(H)
                gemm(6)
                for t in range(NT):
                    transpose_src()
                    to_cols([H[:, t, j * P:(j + 1) * P] for j in range(16)])

                def scores(i, m, bank):
                    t, h = divmod(i, 8)
                    r = slice(64 * m, 64 * m + 64)
                    return pe.matmul(bank[:, 0:nk], QT[r, h, t * P:(t + 1) * P], KT[r, h, 0:nk], start=True, stop=True)

                state = {}

                def pv(i):
                    h = i % 8
                    if h % 4 == 0:
                        state["bank"] = o_bank()
                    for kc in range(nk // P):
                        ins = pe.matmul(state["bank"][:, (h % 4) * P:(h % 4 + 1) * P], PT[:, i % 2, kc, 0:P],
                                        V[:, kc, h * P:(h + 1) * P], start=kc == 0, stop=kc == nk // P - 1)
                    if h % 4 == 3:
                        ins.then_inc(o_full, 1)
                if path:
                    pe.wait_ge(kv_in, 32)
                attention(16, 2, scores, lambda i: nk // P, pv)
                to_at(H)
                gemm(2)
                to_at(H)
                gated(F_FFN // P)

            def gqa_kv_cols(t, first):
                return [H[:, t, first + j * P:first + (j + 1) * P] for j in range(2)]

            diff(0)
            to_at(H)
            gemm(1)
            for t in range(NT):
                transpose_src()
                to_cols(gqa_kv_cols(t, 0))

            def cross(layer):
                to_at(H)
                gemm_t(4)
                gemm(2)
                to_at(X)
                gemm_t(4)

                def scores(i, _, bank):
                    h, t = divmod(i, 2)
                    for j in range(2):
                        ins = pe.matmul(bank[:, 0:TOK], QT[:, 2 * h + j, t * P:(t + 1) * P], KT[:, 2 * h + j, 0:TOK],
                                        start=j == 0, stop=j == 1)
                    return ins

                def pv(i):
                    h, t = divmod(i, 2)
                    if t == 0:
                        return
                    bank = o_bank()
                    for dc in range(2):
                        for kc in range(2):
                            at = h * 256 + dc * P
                            ins = pe.matmul(bank[:, dc * TOK:(dc + 1) * TOK], V[:, kc, at:at + P], PT[:, h % 2, kc, :],
                                            start=kc == 0, stop=kc == 1)
                    ins.then_inc(o_full, 1)
                attention(8, 1, scores, lambda i: 2, pv)
                pe.wait_ge(y_freed, c.get("y"))
                gemm(2)

            def moe():
                to_at(X)
                bank = wb_wait()
                for t in range(NT):
                    for k in range(KC):
                        ins = parts(bank[:, t * N_EXP:(t + 1) * N_EXP], at_hi[:, k, t * P:(t + 1) * P],
                                    at_lo[:, k, t * P:(t + 1) * P], rw_hi[:, k, :], rw_lo[:, k, :], k == 0, k == KC - 1)
                ins.then_inc(wb_full, 1)
                transpose_src()
                for e2 in range(N_EXP // 2):
                    bank = wb_wait()
                    for e in (2 * e2, 2 * e2 + 1):
                        for t in range(NT):
                            at = (e % 2) * TOK + t * P
                            ins = pe.matmul(bank[:, at:at + P], rt[:, 11, t, e:e + 1].to_broadcast([P, P]), ident[:, :],
                                            start=True, stop=True)
                    ins.then_inc(wb_full, 1)
                gated(N_EXP * F_EXPERT // P)

            for layer in range(2):
                to_at(X)
                if layer == 0:
                    pe.wait_ge(tab_landed, 16 * 5)
                    gemm(3)
                    gemm(1, 256)
                    to_cols([sgu_raw[:, g, :] for g in range(8)])
                    for t in range(NT):
                        transpose_src()
                        to_cols([H[:, t, j * P:(j + 1) * P] for j in range(4)])
                        to_cols([PB[:, 3, (2 * t + j) * P:(2 * t + j + 1) * P] for j in range(2)])

                    def scores(i, _, bank):
                        t, h = divmod(i, 8)
                        r = slice(64 * (h % 2), 64 * (h % 2) + 64)
                        nk = (t + 1) * P
                        return pe.matmul(bank[:, 0:nk], QT[r, h // 2, t * P:(t + 1) * P], KT[r, h // 4, 0:nk],
                                         start=True, stop=True)

                    state = {}

                    def pv(i):
                        t, h = divmod(i, 8)
                        if h == 0:
                            state["bank"] = o_bank()
                        r = slice(64 * (h % 2), 64 * (h % 2) + 64)
                        v0 = 640 + 64 * (h // 4)
                        for kc in range(t + 1):
                            ins = pe.matmul(state["bank"][r, (h // 2) * P:(h // 2 + 1) * P], H[:, kc, v0:v0 + 64],
                                            PT[:, i % 2, kc, 0:P], start=kc == 0, stop=kc == t)
                        if h == 7:
                            ins.then_inc(o_full, 1)
                    attention(16, 1, scores, lambda i: i // 8 + 1, pv)
                    pe.wait_ge(y_freed, c.get("y"))
                    for t in range(NT):
                        transpose_src()
                        bank = wb_wait()
                        for g in range(8):
                            ins = pe.matmul(bank[:, g * 64:(g + 1) * 64], WT[:, g, :],
                                            H[:, t, 1280 + 64 * g:1344 + 64 * g], start=True, stop=True)
                        ins.then_inc(wb_full, 1)
                    for t in range(NT):
                        transpose_src()
                        to_cols([H[:, t, 768 + j * P:768 + (j + 1) * P] for j in range(4)])
                    at_wait()
                else:
                    gemm(2)
                    transpose_src()
                    pe.wait_ge(tab_landed, 16 * 6)
                    for j2 in range(4):
                        bank = wb_wait()
                        for j in (2 * j2, 2 * j2 + 1):
                            for s in range(NT):
                                ins = pe.matmul(bank[:, (j % 2) * TOK:(j % 2 + 1) * TOK], H[:, s, j * P:(j + 1) * P],
                                                BAND[:, s, j2, :], start=s == 0, stop=s == NT - 1)
                        ins.then_inc(wb_full, 1)
                    at_wait()
                    hi, lo = tile_wait()
                    for g in range(4):
                        bank = wb_wait()
                        for m in range(2):
                            for cc in range(2):
                                at = (2 * g + cc) * 256 + m * P
                                ins = parts(bank[:, m * TOK:(m + 1) * TOK], hi[:, at:at + P], lo[:, at:at + P],
                                            at_hi[:, 2 * g + cc, :], at_lo[:, 2 * g + cc, :], cc == 0, cc == 1)
                    tile_end(ins)
                    at_wait()
                gemm(2)
                cross(layer)
                moe()

            diff(1)
            to_at(H)
            gemm(3)
            for t in range(NT):
                transpose_src()
                to_cols([H[:, t, j * P:(j + 1) * P] for j in range(10)])

            def scores(i, _, bank):
                h, t = divmod(i, 2)
                return pe.matmul(bank, QT[:, h, t * P:(t + 1) * P], KT[:, h // 4, :], start=True, stop=True)

            state = {}

            def pv(i):
                h, t = divmod(i, 2)
                if t == 0:
                    return
                if h % 2 == 0:
                    state["bank"] = o_bank()
                for kc in range(4):
                    ins = pe.matmul(state["bank"][:, (h % 2) * TOK:(h % 2 + 1) * TOK],
                                    V[:, kc, (h // 4) * P:(h // 4 + 1) * P], PT[:, h % 2, kc, :],
                                    start=kc == 0, stop=kc == 3)
                if h % 2 == 1:
                    ins.then_inc(o_full, 1)
            pe.wait_ge(kv_in, 64)
            attention(16, 1, scores, lambda i: 4, pv)
            pe.wait_ge(y_freed, c.get("y"))
            gemm(2)
            to_at(H)
            gated(F_FFN // P)

        @block.scalar
        def _(act):
            c = Count()

            def split():
                n = c.get("split")
                i = c.i
                use = 32 * (n // RAW + 1)
                act.wait_ge(raw_landed[n % RAW], use if i is None else i * (32 * LOOP_TILES // RAW) + use)
                if n >= RING:
                    used = n - RING + 1
                    act.wait_ge(tile_used, used if i is None else i * LOOP_TILES + used)
                nc.scalar.activation(w_hi[:, n % RING, :], raw[:, n % RAW, :], ACT.Copy).then_inc(hi_done, 1)
                c.add("split")

            def ahead(more=RING):
                while c.get("split") < min(c.get("tile") + more, TOTAL):
                    split()

            def tiles(n):
                for _ in range(n):
                    c.add("tile")
                    ahead()

            def full():
                ahead()
                c.add("full")
                act.wait_ge(wb_full, c.get("full"))

            def bank():
                b = PS[:, 4 + c.get("wb") % 4, :]
                c.add("wb")
                return b

            def prm():
                n = c.get("prm")
                ahead()
                if n:
                    act.wait_ge(prm_used, n)
                for j, src in prm_loads[n]:
                    if isinstance(src, tuple):
                        for m, s in enumerate(src):
                            act.dma_start(PRM[:, 0, m * 512:(m + 1) * 512], rowb(s)).then_inc(prm_landed, 16)
                    else:
                        act.dma_start(PRM[:, j, :], src).then_inc(prm_landed, 16)
                c.add("prm")

            def stat():
                ahead()
                c.add("stat")
                act.wait_ge(stat_ready, c.get("stat"))

            def root(ap):
                stat()
                nc.scalar.activation(ap, ap, ACT.Sqrt).then_inc(stat_done, 1)

            def hi_of(dst, src):
                nc.scalar.activation(dst, src, ACT.Copy).then_inc(hi_evac, 1)

            def to_at(affine=False):
                for t in range(NT):
                    for h in range(2):
                        dst = at_hi[:, 4 * h:4 * h + 4, t * P:(t + 1) * P]
                        if affine:
                            ahead()
                            bank()
                            c.add("full")
                            c.add("aff")
                            act.wait_ge(aff_ready, c.get("aff"))
                            hi_of(dst, PBf[:, 0:512].rearrange("p (k t) -> p k t", k=4))
                        else:
                            full()
                            hi_of(dst, bank().rearrange("p (k t) -> p k t", k=4))

            def plain(n):
                c.add("full", n)
                c.add("wb", n)

            def gated(n_f, moe):
                def gu():
                    ahead()
                    act.wait_ge(tile_used, c.at("tile", 1))
                    f = c.get("gu")
                    nc.scalar.activation(silu_buf[:, f % 2, :], bank()[:, 0:TOK], ACT.Silu).then_inc(silu_done, 1)
                    c.add("tile")
                    c.add("gu")
                    if moe:
                        c.add("he32")
                        v = c.get("he32")
                        act.wait_ge(he_f32, v if c.i is None else c.i * 8 + v)
                    else:
                        act.wait_ge(wb_freed, c.at("wb"))
                    nc.scalar.activation(he_hi[:, f % 4, :], he_buf[:, f % 2, :], ACT.Copy).then_inc(he_hi_done, 1)

                steps, loops = steps_of(n_f)
                gu()
                gu()

                def step():
                    gu()
                    gu()
                    c.add("tile")
                    ahead(3)
                step()
                with act.Fori(0, loops) as i:
                    c.enter(i)
                    before = c.get("split"), c.get("he32")
                    for _ in range(4):
                        step()
                    assert c.get("split") - before[0] == LOOP_TILES
                    c.leave(loops)
                    c.add("split", LOOP_TILES * (loops - 1))
                    c.add("he32", (c.get("he32") - before[1]) * (loops - 1))
                for _ in range(1 + 4 * loops, steps):
                    step()
                c.add("tile")

            def attention(n, s_groups, nk, kind, scale, o_at=None, evac=None, chunks=None):
                def e(i):
                    ahead()
                    c.add("max")
                    act.wait_ge(max_ready, c.get("max"))
                    c.add("full", s_groups)
                    for g in range(s_groups):
                        b = bank()
                        s = st[:, (s_groups * i + g) % 8, :]
                        w = nk(i)
                        p = PB[:, i % 4, 0:w] if s_groups == 1 else PB[:, 2 * (i % 2) + g, 0:w]
                        if kind == "sink":
                            nc.scalar.activation(s[:, 2:3], bc[:, B_SINK + i % 8:B_SINK + i % 8 + 1], ACT.Exp, bias=s[:, 0:1])
                            ins = nc.scalar.activation(p, p, ACT.Exp, bias=s[:, 0:1], accum_out=s[:, 1:2])
                        else:
                            ins = nc.scalar.activation(p, b[:, 0:w], ACT.Exp, bias=s[:, 0:1], scale=scale, accum_out=s[:, 1:2])
                    ins.then_inc(exp_done, 1)

                def copy_t(i):
                    ahead()
                    c.add("t")
                    act.wait_ge(t_full, c.get("t"))
                    b = PS[:, 1 + 2 * ((c.get("t") - 1) % 2), :]
                    k = chunks(i)
                    if kind in ("cross", "gqa"):
                        h, t = divmod(i, 2)
                        dst = PT[:, h % 2, 0:k, t * P:(t + 1) * P]
                    else:
                        dst = PT[:, i % 2, 0:k, 0:P]
                    nc.scalar.activation(dst, b[:, 0:k * P].rearrange("p (k q) -> p k q", k=k), ACT.Copy).then_inc(t_freed, 1)

                for it in range(n + 3):
                    if s_groups == 2 and 0 <= it - 2 < n:
                        copy_t(it - 2)
                    if it < n:
                        e(it)
                    if s_groups == 1 and 0 <= it - 2 < n:
                        copy_t(it - 2)
                    if 0 <= it - 3 < n and o_at and o_at(it - 3):
                        c.add("o")
                        act.wait_ge(o_full, c.get("o"))
                        hi_of(*evac(it - 3))

            def o_bank():
                b = PS[:, 2 * (c.get("y") % 2), :]
                c.add("y")
                return b

            loads = [(ident[:, :], A["c_ident"]), (colin[C_LAT:C_LAT + 8, :], A["c_2"].rearrange("a (k p) -> (a k) p", p=P)),
                     (colin[C_CTX:C_CTX + 8, :], A["c_ctx_2"].rearrange("(k p) -> k p", p=P)),
                     (colin[C_N1:C_N1 + 16, :], A["norm1_g_2"].rearrange("l (k p) -> (l k) p", p=P)),
                     (colin[C_N2:C_N2 + 16, :], A["norm2_g_2"].rearrange("l (k p) -> (l k) p", p=P)),
                     (colin[C_POOL:C_POOL + 8, :], A["l1_pool_scale"].rearrange("(k p) -> k p", p=P)),
                     (colin[C_SGUB:C_SGUB + 8, :], A["l0_sgu_b"]),
                     (bc[:, B_SINK:B_SINK + 8], rowb(A["l0_sinks"])),
                     (bc[:, B_RBIAS:B_RBIAS + 16], rowb(A["router_bias"])),
                     (bc[:, B_DQ:B_DQ + 64], rowb(A["diff_q_norm_2"][0])),
                     (bc[:, B_DK:B_DK + 64], rowb(A["diff_k_norm_2"][0])),
                     (bc[:, B_SUB:B_SUB + 128], rowb(A["diff_subln_2"][0])),
                     (bc[:, B_GQ:B_GQ + 128], rowb(A["gqa_q_norm_2"][0])),
                     (bc[:, B_GK:B_GK + 128], rowb(A["gqa_k_norm_2"][0])),
                     (bc[:, B_LAM:B_LAM + 64], rowb(A["diff_lambda_q1_2"][0])),
                     (bc[:, B_LAM + 64:B_LAM + 128], rowb(A["diff_lambda_k1_2"][0])),
                     (bc[:, B_LAM + 128:B_LAM + 192], rowb(A["diff_lambda_q2_2"][0])),
                     (bc[:, B_LAM + 192:B_LAM + 256], rowb(A["diff_lambda_k2_2"][0])),
                     (bc[:, B_INVF:B_INVF + 8], rowb(A["c_invf"])),
                     (rw[:, :, :], A["router_w"].rearrange("(k p) n -> p k n", p=P)),
                     (pos_i[:, :], A["positions"][0].rearrange("(t p) -> p t", p=P))]
            bias = A["ada_b_2"].rearrange("l n -> (l n)")
            for j, region in enumerate((KTf, Vf, Hf)):
                loads.append((region[0:2, :], bias[j * 4096:(j + 1) * 4096].partition_broadcast(2)))
            assert len(loads) == N_SETUP
            for dst, src in loads:
                act.dma_start(dst, src, allow_slow_non_contiguous=True).then_inc(setup_landed, 16)
            act.dma_start(X[:, :, :], A["ctx_2"][0].rearrange("(t p) d -> p t d", p=P)).then_inc(x_landed, 16)
            act.wait_ge(setup_landed, 16 * N_SETUP)
            nc.scalar.activation(rw_hi[:, :, :], rw[:, :, :], ACT.Copy).then_inc(hi_evac, 1)
            c.add("full")
            act.wait_ge(wb_full, 1)
            b = bank()
            nc.scalar.activation(cond[:, :, :], b[:, 0:16].rearrange("p (c k) -> p c k", c=2), ACT.Silu).then_inc(act_step, 1)
            act.wait_ge(act_step, 1)
            hi_of(cond_hi[:, :, :], cond[:, :, :].rearrange("p c k -> p k c"))
            c.add("wb", 24)
            tiles(48)
            c.add("stat")
            ahead()
            act.wait_ge(stat_ready, 1)
            for j, region in enumerate((KTf, Vf, Hf)):
                act.dma_start(mods_d[:, j * 4096:(j + 1) * 4096], region[0:2, :]).then_inc(mod_out, 16)
            act.wait_ge(mod_out, 48)
            for layer in range(2):
                for cnd in range(2):
                    act.dma_start(QT[48 * cnd:48 * cnd + 48, layer, 0:P], mods_rows[layer, cnd]).then_inc(mod_in, 16)
            plain(2)
            stat()
            nc.scalar.activation(lam[:, 0:2], lam[:, 0:2], ACT.Exp).then_inc(stat_done, 1)

            def rms(n=NT):
                for _ in range(n):
                    root(mv[:, 0:1])

            def heads(n):
                root(hs[:, 1, 0:n])

            def diff(path):
                nk = TOK * (1 + path)
                act.wait_ge(mod_out, 48)
                if path:
                    act.dma_start(KT[:, :, 0:TOK], kd_d).then_inc(kv_in, 16)
                    act.dma_start(V[:, 0:2, :], vd_d).then_inc(kv_in, 16)
                    act.dma_start(TAB[:, 0:256].rearrange("p (t c) -> p t c", t=NT),
                                  A["c_ax64"].rearrange("(t p) c -> p t c", p=P)).then_inc(tab_landed, 16)
                rms()
                to_at(True)
                prm()
                tiles(8)
                for t in range(NT):
                    heads(32)
                tiles(4)
                plain(8)
                if not path:
                    ahead()
                    c.add("stat")
                    act.wait_ge(stat_ready, c.get("stat"))
                    act.dma_start(kd_d, KT[:, :, 0:TOK]).then_inc(kv_out, 16)
                    act.dma_start(vd_d, V[:, 0:2, :]).then_inc(kv_out, 16)
                attention(16, 2, lambda i: nk, "diff", 64 ** -0.5, chunks=lambda i: nk // P)
                c.add("y", 4)
                c.add("o", 4)
                for t in range(NT):
                    heads(8)
                to_at()
                c.add("y", 2)
                tiles(4)
                rms()
                prm()
                to_at(True)
                c.add("y", 2)
                gated(F_FFN // P, False)

            c.add("y", 0)
            c.add("y", 6)
            diff(0)
            rms()
            to_at(True)
            c.add("y", 1)
            tiles(2)
            for t in range(NT):
                heads(2)
                plain(1)
            ahead()
            c.add("stat")
            act.wait_ge(stat_ready, c.get("stat"))
            act.dma_start(kg_d, KT[:, 0:2, 0:TOK]).then_inc(kv_out, 16)
            act.dma_start(vg_d, V[:, 0:2, 0:TOK]).then_inc(kv_out, 16)
            act.wait_ge(kv_out, 64)
            act.dma_start(X[:, :, :], A["x"][0].rearrange("(t p) d -> p t d", p=P)).then_inc(x_landed, 16)
            act.dma_start(TAB[:, 0:384], A["c_masks"]).then_inc(tab_landed, 16)
            for q in range(4):
                act.dma_start(sgu_raw[:, 2 * q:2 * q + 2, :], A["l0_sgu_w"][2 * q:2 * q + 2].rearrange("g t s -> t g s"))\
                    .then_inc(tab_landed, 16)

            def norm():
                rms()

            for layer in range(2):
                to_at()
                if layer == 0:
                    prm()
                    c.add("y", 4)
                    stat()
                    nc.scalar.activation(trig[:, 2:4, :, :], trig[:, 2:4, :, :], ACT.Sin).then_inc(stat_done, 1)
                    tiles(7)
                    for t in range(NT):
                        stat()
                        nc.scalar.activation(H[:, t, 768:1792], H[:, t, 768:1792], ACT.Gelu_apprx_tanh).then_inc(stat_done, 1)
                    plain(2)
                    plain(4)
                    attention(16, 1, lambda i: (i // 8 + 1) * P, "sink", 1.0,
                              o_at=lambda i: i % 8 == 7, chunks=lambda i: i // 8 + 1,
                              evac=lambda i: (at_hi[:, 0:4, (i // 8) * P:(i // 8 + 1) * P],
                                              o_bank().rearrange("p (k q) -> p k q", k=4)))
                    for t in range(NT):
                        root(hs[:, 1, 0:8])
                    plain(2)
                    for t in range(NT):
                        full()
                        hi_of(at_hi[:, 4:8, t * P:(t + 1) * P], bank().rearrange("p (k q) -> p k q", k=4))
                else:
                    c.add("y", 2)
                    act.dma_start(V[:, 0:2, :], A["c_band"]).then_inc(tab_landed, 16)
                    tiles(4)
                    for j2 in range(4):
                        full()
                        hi_of(at_hi[:, 2 * j2:2 * j2 + 2, :], bank().rearrange("p (k t) -> p k t", k=2))
                    tiles(1)
                    for g in range(4):
                        ahead()
                        c.add("aff")
                        act.wait_ge(aff_ready, c.get("aff"))
                        bank()
                        hi_of(at_hi[:, 2 * g:2 * g + 2, :], PBf[:, 0:512].rearrange("p (k t) -> p k t", k=2))
                act.dma_start(H[:, :, 0:D], A["mem"][0].rearrange("(t p) d -> p t d", p=P)).then_inc(x_landed, 16)
                prm()
                c.add("y", 2)
                tiles(4)
                to_at()
                norm()
                c.add("wb", 4)
                c.add("y", 2)
                tiles(8)
                to_at()
                c.add("wb", 4)
                tiles(4)
                prm()
                attention(8, 1, lambda i: TOK, "cross", 256 ** -0.5, o_at=lambda i: i % 2 == 1, chunks=lambda i: 2,
                          evac=lambda i: (at_hi[:, 2 * (i // 2):2 * (i // 2) + 2, :], o_bank().rearrange("p (k q) -> p k q", k=2)))
                c.add("y", 2)
                tiles(4)
                norm()
                prm()
                to_at()
                plain(1)
                stat()
                nc.scalar.activation(rt[:, 1, :, :], rt[:, 1, :, :], ACT.Exp).then_inc(stat_done, 1)
                plain(8)
                c.add("y", 2)
                gated(N_EXP * F_EXPERT // P, True)
                norm()

            diff(1)
            act.dma_start(KT[:, 0:2, 0:TOK], kg_d).then_inc(kv_in, 16)
            act.dma_start(V[:, 0:2, 0:TOK], vg_d).then_inc(kv_in, 16)
            act.dma_start(TAB[:, :].rearrange("p (t c) -> p t c", t=NT),
                          A["c_ax128"].rearrange("(t p) c -> p t c", p=P)).then_inc(tab_landed, 16)
            rms()
            to_at(True)
            c.add("y", 3)
            prm()
            tiles(6)
            for t in range(NT):
                heads(10)
                plain(3)
            attention(16, 1, lambda i: 512, "gqa", 128 ** -0.5, o_at=lambda i: i % 4 == 3, chunks=lambda i: 4,
                      evac=lambda i: (at_hi[:, 2 * (i // 4):2 * (i // 4) + 2, :], o_bank().rearrange("p (k q) -> p k q", k=2)))
            c.add("y", 2)
            tiles(4)
            rms()
            prm()
            to_at(True)
            c.add("y", 2)
            gated(F_FFN // P, False)

        @block.vector
        def _(dve):
            c = Count()

            def D1(ins):
                ins.then_inc(dve_step, 1)
                c.add("step")
                dve.wait_ge(dve_step, c.get("step"))

            def freed(ins):
                ins.then_inc(wb_freed, 1)
                dve.wait_ge(wb_freed, c.at("wb"))

            def y_done(ins):
                ins.then_inc(y_freed, 1)
                c.add("y")
                dve.wait_ge(y_freed, c.get("y"))

            def full():
                c.add("full")
                dve.wait_ge(wb_full, c.get("full"))

            def bank():
                b = PS[:, 4 + c.get("wb") % 4, :]
                c.add("wb")
                return b

            def hi_wait():
                c.add("hi")
                dve.wait_ge(hi_evac, c.get("hi"))

            def lo_of(dst, src, hi):
                return dve.tensor_tensor(dst, src, hi.bitcast(F32), ALU.subtract)

            def done():
                c.add("done")
                dve.wait_ge(stat_done, c.get("done"))

            def ask(ins):
                ins.then_inc(stat_ready, 1)
                c.add("ask")
                dve.wait_ge(stat_ready, c.get("ask"))

            def ready(ins):
                ins.then_inc(src_ready, 1)
                c.add("src")
                dve.wait_ge(src_ready, c.get("src"))

            def tiles(n):
                c.add("tile", n)
                dve.wait_ge(tile_used, c.get("tile"))

            def ybank(pair, t):
                return PS[:, 2 * (pair % 2) + t, :]

            def to_at(A8=None, B8=None):
                for t in range(NT):
                    for h in range(2):
                        sl = (slice(None), slice(4 * h, 4 * h + 4), slice(t * P, (t + 1) * P))
                        full()
                        b = bank().rearrange("p (k t) -> p k t", k=4)
                        if A8 is not None:
                            tmp = PBf[:, 0:512].rearrange("p (k t) -> p k t", k=4)
                            for j in range(4):
                                k = 4 * h + j
                                ins = dve.tensor_scalar(tmp[:, j, :], b[:, j, :], A8[:, k:k + 1], B8[:, k:k + 1], ALU.mult, ALU.add)
                            ins.then_inc(aff_ready, 1)
                            c.add("aff")
                            dve.wait_ge(aff_ready, c.get("aff"))
                            hi_wait()
                            freed(lo_of(at_lo[sl], tmp, at_hi[sl]))
                        else:
                            hi_wait()
                            freed(lo_of(at_lo[sl], b, at_hi[sl]))

            def mean_var(t):
                for h in range(2):
                    D1(dve.bn_stats(bn[:, h, :], X[:, t, h * 512:(h + 1) * 512]))
                D1(dve.bn_aggr(mv[:, :], bn[:, :, :]))

            def prm_wait():
                n = c.get("prm")
                need = sum(sum(len(s) if isinstance(s, tuple) else 1 for _, s in prm_loads[j]) for j in range(n + 1))
                dve.wait_ge(prm_landed, 16 * need)
                c.add("prm")

            def layer_norm_tiles(signal=True):
                prm_wait()
                for t in range(NT):
                    mean_var(t)
                    D1(dve.tensor_copy(hs[:, 0, 0:1], mv[:, 0:1]))
                    ask(dve.tensor_scalar(mv[:, 0:1], mv[:, 1:2], LN_EPS, None, ALU.add))
                    done()
                    D1(dve.reciprocal(mv[:, 1:2], mv[:, 0:1]))
                    D1(dve.tensor_scalar(X[:, t, :], X[:, t, :], hs[:, 0, 0:1], mv[:, 1:2], ALU.subtract, ALU.mult))
                    D1(dve.tensor_tensor(X[:, t, :], X[:, t, :], PRM[:, 0, :], ALU.mult))
                    (ready if signal else D1)(dve.tensor_tensor(X[:, t, :], X[:, t, :], PRM[:, 1, :], ALU.add))
                if signal:
                    dve.wait_ge(src_ready, c.get("src"))
                dve.tensor_copy(mv[:, 0:1], mv[:, 1:2]).then_inc(prm_used, 1)

            def residual_add(per_pair):
                for p in range(2):
                    pair = c.get("y")
                    if per_pair:
                        tiles(per_pair)
                    for t in range(NT):
                        x = X[:, t, p * 512:(p + 1) * 512]
                        ins = dve.scalar_tensor_tensor(x, x, ALPHA, ybank(pair, t), ALU.mult, ALU.add)
                        if t == NT - 1:
                            ins.then_inc(y_freed, 1)
                        else:
                            ins.then_inc(dve_step, 1)
                            c.add("step")
                    c.add("y")
                settled()

            def residual_gate(per_pair):
                prm_wait()
                for p in range(2):
                    pair = c.get("y")
                    if per_pair:
                        tiles(per_pair)
                    for t in range(NT):
                        tmp = PBf[:, t * 512:(t + 1) * 512]
                        ins = dve.tensor_tensor(tmp, ybank(pair, t), PRM[:, 0, p * 512:(p + 1) * 512], ALU.mult)
                        if t == NT - 1:
                            ins.then_inc(y_freed, 1)
                        else:
                            ins.then_inc(dve_step, 1)
                            c.add("step")
                    c.add("y")
                    dve.wait_ge(dve_step, c.get("step"))
                    dve.wait_ge(y_freed, c.get("y"))
                    for t in range(NT):
                        x = X[:, t, p * 512:(p + 1) * 512]
                        D1(dve.tensor_tensor(x, x, PBf[:, t * 512:(t + 1) * 512], ALU.add))
                dve.tensor_copy(mv[:, 0:1], mv[:, 1:2]).then_inc(prm_used, 1)

            def rms_to_h():
                for t in range(NT):
                    mean_var(t)
                    D1(dve.scalar_tensor_tensor(mv[:, 0:1], mv[:, 0:1], mv[:, 0:1], mv[:, 1:2], ALU.mult, ALU.add))
                    ask(dve.tensor_scalar(mv[:, 0:1], mv[:, 0:1], RMS_EPS, None, ALU.add))
                    done()
                    D1(dve.reciprocal(mv[:, 1:2], mv[:, 0:1]))
                    ready(dve.tensor_scalar(H[:, t, 0:D], X[:, t, :], mv[:, 1:2], None, ALU.mult))

            def affine_of(cnd, layer, norm):
                first = cnd * 48 + (0 if norm == 0 else 24)
                g0 = (C_N1 if norm == 0 else C_N2) + 8 * layer
                D1(dve.tensor_scalar(affA[:, :], modcol[:, layer, first + 8:first + 16], 1.0, None, ALU.add))
                D1(dve.tensor_tensor(affA[:, :], affA[:, :], col[:, g0:g0 + 8], ALU.mult))
                return affA, modcol[:, layer, first:first + 8]

            def y_to(dsts, width=512, per=2):
                pair = c.get("y")
                tiles(per)
                for t in range(NT):
                    ins = dve.tensor_copy(dsts[t], ybank(pair, t)[:, 0:width])
                    if t == NT - 1:
                        ins.then_inc(y_freed, 1)
                    else:
                        ins.then_inc(dve_step, 1)
                        c.add("step")
                c.add("y")

            def settled():
                dve.wait_ge(dve_step, c.get("step"))
                dve.wait_ge(y_freed, c.get("y"))

            def head_norm(t, n, dh, at, eps):
                v = H[:, t, at:at + n * dh].rearrange("p (h d) -> p h d", h=n)
                sq = PBf[:, 0:n * dh].rearrange("p (h d) -> p h d", h=n)
                D1(dve.tensor_tensor(sq, v, v, ALU.mult))
                D1(dve.tensor_reduce(hs[:, 0, 0:n], sq, AXX, ALU.add))
                ask(dve.tensor_scalar(hs[:, 1, 0:n], hs[:, 0, 0:n], 1.0 / dh, eps, ALU.mult, ALU.add))
                done()
                D1(dve.reciprocal(hs[:, 2, 0:n], hs[:, 1, 0:n]))
                D1(dve.tensor_tensor(v, v, hs[:, 2, 0:n].unsqueeze(2).to_broadcast([P, n, dh]), ALU.mult))

            def head_gain(t, n, dh, at, gain):
                v = H[:, t, at:at + n * dh].rearrange("p (h d) -> p h d", h=n)
                ins = dve.tensor_tensor(v, v, bc[:, gain:gain + dh].unsqueeze(1).to_broadcast([P, n, dh]), ALU.mult)
                D1(ins)

            def axial(t, n, dh):
                q = dh // 4
                tab = TAB[:, 0:NT * 2 * dh].rearrange("p (t c) -> p t c", t=NT)[:, t, :]
                v = H[:, t, 0:n * dh].rearrange("p (h d) -> p h d", h=n)
                v4 = H[:, t, 0:n * dh].rearrange("p (h a b q) -> p h a b q", h=n, a=2, b=2)
                r4 = PBf[:, 0:n * dh].rearrange("p (h a b q) -> p h a b q", h=n, a=2, b=2)
                s4 = tab[:, dh:2 * dh].rearrange("p (a b q) -> p a b q", a=2, b=2)
                for b in range(2):
                    D1(dve.tensor_tensor(r4[:, :, :, b, :], v4[:, :, :, 1 - b, :],
                                         s4[:, :, b, :].unsqueeze(1).to_broadcast([P, n, 2, q]), ALU.mult))
                D1(dve.tensor_tensor(v, v, tab[:, 0:dh].unsqueeze(1).to_broadcast([P, n, dh]), ALU.mult))
                return dve.tensor_tensor(v, v, PBf[:, 0:n * dh].rearrange("p (h d) -> p h d", h=n), ALU.add)

            def cols_out(dst):
                full()
                b = bank()
                n = dst.shape[1] if len(dst.shape) == 3 else 1
                freed(dve.tensor_copy(dst, b[:, 0:n * P].rearrange("p (k t) -> p k t", k=n)))

            def gated(n_f, moe):
                def gu(e):
                    dve.wait_ge(tile_used, c.at("tile", 1))
                    c.add("tile")
                    f = c.get("gu")
                    c.add("gu")
                    dve.wait_ge(silu_done, c.at("gu"))
                    b = bank()
                    h = he_buf[:, f % 2, :]
                    freed(dve.tensor_tensor(h, silu_buf[:, f % 2, :], b[:, TOK:2 * TOK], ALU.mult))
                    if moe:
                        dve.tensor_tensor(h, h, cbc[:, e, :], ALU.mult).then_inc(he_f32, 1)
                        c.add("he32")
                        v = c.get("he32")
                        dve.wait_ge(he_f32, v if c.i is None else c.i * 8 + v)
                    dve.wait_ge(he_hi_done, c.at("gu"))
                    lo_of(he_lo[:, f % 4, :], h, he_hi[:, f % 4, :]).then_inc(he_ready, 1)

                steps, loops = steps_of(n_f)

                def step(i, m):
                    for f in (2 * m + 2, 2 * m + 3):
                        gu(i * 2 + f // 4 if moe else 0)
                    c.add("tile")
                gu(0)
                gu(0)
                step(0, 0)
                with dve.Fori(0, loops) as i:
                    c.enter(i)
                    before = c.get("he32")
                    for m in range(1, 5):
                        step(i, m)
                    c.leave(loops)
                    c.add("he32", (c.get("he32") - before) * (loops - 1))
                for m in range(1 + 4 * loops, steps):
                    step(0, m)
                c.add("tile")
                dve.wait_ge(tile_used, c.get("tile"))

            def attention(n, s_groups, nk, kind, scale, o_at, o_evac):
                t0 = c.get("t")

                def m(i):
                    w = nk(i)
                    for g in range(s_groups):
                        full()
                        b = bank()
                        s = st[:, (s_groups * i + g) % 8, :]
                        if kind == "sink":
                            t, h = divmod(i, 8)
                            p = PB[:, i % 4, 0:w]
                            if i >= 4:
                                dve.wait_ge(t_freed, t0 + i - 3)
                            dve.scalar_tensor_tensor(p, b[:, 0:w], 0.125, TAB[:, 256 - w:256], ALU.mult, ALU.add)\
                                .then_inc(wb_freed, 1)
                            dve.wait_ge(wb_freed, c.get("wb"))
                            D1(dve.tensor_reduce(s[:, 3:4], p, AXX, ALU.max))
                            ins = dve.tensor_scalar(s[:, 0:1], s[:, 3:4], bc[:, B_SINK + h:B_SINK + h + 1], -1.0, ALU.max, ALU.mult)
                        else:
                            D1(dve.tensor_reduce(s[:, 3:4], b[:, 0:w], AXX, ALU.max))
                            ins = dve.tensor_scalar(s[:, 0:1], s[:, 3:4], -scale, None, ALU.mult)
                    ins.then_inc(max_ready, 1)

                def norm(i):
                    c.add("exp")
                    dve.wait_ge(exp_done, c.get("exp"))
                    w = nk(i)
                    if kind == "diff":
                        s0, s1 = st[:, (2 * i) % 8, :], st[:, (2 * i + 1) % 8, :]
                        p0, p1 = PB[:, 2 * (i % 2), 0:w], PB[:, 2 * (i % 2) + 1, 0:w]
                        dve.reciprocal(s0[:, 3:4], s0[:, 1:2]).then_inc(wb_freed, 1)
                        dve.reciprocal(s1[:, 2:3], s1[:, 1:2]).then_inc(wb_freed, 1)
                        dve.wait_ge(wb_freed, c.get("wbn") + 2)
                        c.add("wbn", 2)
                        D1(dve.tensor_scalar(p1, p1, s1[:, 2:3], lam[:, 2:3], ALU.mult, ALU.mult))
                        dve.scalar_tensor_tensor(p0, p0, s0[:, 3:4], p1, ALU.mult, ALU.add).then_inc(p_ready, 1)
                        return
                    s = st[:, i % 8, :]
                    p = PB[:, i % 4, 0:w]
                    if kind == "sink":
                        D1(dve.tensor_tensor(s[:, 1:2], s[:, 1:2], s[:, 2:3], ALU.add))
                        D1(dve.reciprocal(s[:, 3:4], s[:, 1:2]))
                    else:
                        dve.reciprocal(s[:, 3:4], s[:, 1:2]).then_inc(wb_freed, 1)
                        c.add("wbn")
                        dve.wait_ge(wb_freed, c.get("wbn"))
                    dve.tensor_scalar(p, p, s[:, 3:4], None, ALU.mult).then_inc(p_ready, 1)

                c.n["wbn"] = c.get("wb")
                for it in range(n + 3):
                    if it < n:
                        m(it)
                    if 0 <= it - 1 < n:
                        norm(it - 1)
                    if 0 <= it - 3 < n and o_at(it - 3):
                        o_evac(it - 3)
                c.add("t", n)

            def o_split(dst_hi, dst_lo, k):
                b = ybank(c.get("y"), 0).rearrange("p (k q) -> p k q", k=k)
                hi_wait()
                c.add("o")
                y_done(lo_of(dst_lo, b, dst_hi))

            for small in (hs[:, :, :], mv[:, :], lam[:, :]):
                D1(dve.memset(small, 0.0))
            dve.wait_ge(setup_landed, 16 * N_SETUP)
            full()
            hi_wait()
            D1(lo_of(rw_lo[:, :, :], rw[:, :, :], rw_hi[:, :, :]))
            hi_wait()
            freed(dve.tensor_copy(col[:, :], bank()[:, 0:C_ROWS]))
            dve.wait_ge(wb_freed, 1)
            ready(lo_of(cond_lo[:, :, :], cond[:, :, :].rearrange("p c k -> p k c"), cond_hi[:, :, :]))
            for j in range(24):
                tiles(2)
                region = (KTf, Vf, Hf)[j // 8][0:2, (j % 8) * 512:(j % 8 + 1) * 512]
                freed(dve.tensor_tensor(region, region, bank()[0:2, :], ALU.add))
            dve.wait_ge(wb_freed, c.get("wb"))
            ask(dve.tensor_copy(hs[:, 0, 0:1], hs[:, 0, 0:1]))
            for j in range(2):
                l0 = B_LAM + 128 * j
                D1(dve.tensor_tensor(bc[:, l0:l0 + 64], bc[:, l0:l0 + 64], bc[:, l0 + 64:l0 + 128], ALU.mult))
                D1(dve.tensor_reduce(lam[:, j:j + 1], bc[:, l0:l0 + 64], AXX, ALU.add))
            for layer in range(2):
                full()
                freed(dve.tensor_copy(modcol[:, layer, :], bank()[:, 0:96]))
            dve.wait_ge(wb_freed, c.get("wb"))
            ask(dve.tensor_scalar(lam[:, 3:4], lam[:, 0:1], 1.0, None, ALU.mult))
            done()
            D1(dve.tensor_tensor(lam[:, 2:3], lam[:, 1:2], lam[:, 0:1], ALU.subtract))
            D1(dve.tensor_scalar(lam[:, 2:3], lam[:, 2:3], -LAMBDA_INIT, None, ALU.add))
            D1(dve.tensor_scalar(bc[:, B_SUB:B_SUB + 128], bc[:, B_SUB:B_SUB + 128], 1.0 - LAMBDA_INIT, None, ALU.mult))
            dve.wait_ge(x_landed, 16)

            def diff(path):
                nk = TOK * (1 + path)
                a, b8 = affine_of(1 - path, 0, 0)
                rms_to_h()
                to_at(a, b8)
                for n in range(4):
                    y_to([H[:, t, n * 512:(n + 1) * 512] for t in range(NT)])
                settled()
                if path:
                    dve.wait_ge(tab_landed, 16 * 7)
                for t in range(NT):
                    head_norm(t, 32, 64, 0, RMS_EPS)
                    head_gain(t, 16, 64, 0, B_DQ)
                    v = H[:, t, D:2 * D].rearrange("p (h d) -> p h d", h=16)
                    g = bc[:, B_DK:B_DK + 64].unsqueeze(1).to_broadcast([P, 16, 64])
                    if path:
                        D1(dve.tensor_tensor(v, v, g, ALU.mult))
                        ready(axial(t, 32, 64))
                    else:
                        ready(dve.tensor_tensor(v, v, g, ALU.mult))
                for n in range(2):
                    y_to([V[:, 2 * path + u, n * 512:(n + 1) * 512] for u in range(NT)])
                settled()
                for t in range(NT):
                    for j in range(4):
                        if j < 2:
                            cols_out(QT[:, 4 * j:4 * j + 4, t * P:(t + 1) * P])
                        else:
                            k0 = path * TOK + t * P
                            cols_out(KT[:, 4 * j - 8:4 * j - 4, k0:k0 + P])
                dve.wait_ge(wb_freed, c.get("wb"))
                if not path:
                    ask(dve.tensor_copy(hs[:, 0, 0:1], hs[:, 0, 0:1]))

                def o_evac(i):
                    c.add("o")
                    dve.wait_ge(o_full, c.get("o"))
                    t, h = divmod(i, 8)
                    y_done(dve.tensor_copy(H[:, t, (h // 4) * 512:(h // 4 + 1) * 512], ybank(c.get("y"), 0)))
                attention(16, 2, lambda i: nk, "diff", 64 ** -0.5, lambda i: i % 4 == 3, o_evac)
                dve.wait_ge(y_freed, c.get("y"))
                for t in range(NT):
                    head_norm(t, 8, P, 0, RMS_EPS)
                    v = H[:, t, 0:D].rearrange("p (h d) -> p h d", h=8)
                    ready(dve.tensor_tensor(v, v, bc[:, B_SUB:B_SUB + P].unsqueeze(1).to_broadcast([P, 8, P]), ALU.mult))
                to_at()
                residual_gate(2)
                a, b8 = affine_of(1 - path, 0, 1)
                rms_to_h()
                to_at(a, b8)
                gated(F_FFN // P, False)
                residual_gate(0)

            diff(0)
            a, b8 = affine_of(1, 1, 0)
            rms_to_h()
            to_at(a, b8)
            y_to_split = c.get("y")
            tiles(2)
            for t in range(NT):
                D1(dve.tensor_copy(H[:, t, 0:256], ybank(y_to_split, t)[:, 0:256]))
                ins = dve.tensor_copy(V[:, t, 0:256], ybank(y_to_split, t)[:, 256:512])
                if t == NT - 1:
                    ins.then_inc(y_freed, 1)
                else:
                    D1(ins)
            c.add("y")
            for t in range(NT):
                head_norm(t, 2, P, 0, RMS_EPS)
                v = H[:, t, 0:256].rearrange("p (h d) -> p h d", h=2)
                ready(dve.tensor_tensor(v, v, bc[:, B_GK:B_GK + P].unsqueeze(1).to_broadcast([P, 2, P]), ALU.mult))
            for t in range(NT):
                cols_out(KT[:, 0:2, t * P:(t + 1) * P])
            dve.wait_ge(wb_freed, c.get("wb"))
            dve.wait_ge(y_freed, c.get("y"))
            ask(dve.tensor_copy(hs[:, 0, 0:1], hs[:, 0, 0:1]))

            def cross(layer):
                dve.wait_ge(x_landed, 16 * (3 + layer))
                for _ in range(NT):
                    ready(dve.tensor_copy(hs[:, 0, 0:1], hs[:, 0, 0:1]))
                residual_add(2)
                to_at()
                layer_norm_tiles()
                for j in range(4):
                    tiles(1)
                    freed(dve.tensor_copy(KT[:, 2 * j:2 * j + 2, 0:TOK], bank().rearrange("p (k t) -> p k t", k=2)))
                for n in range(2):
                    y_to([V[:, t, n * 512:(n + 1) * 512] for t in range(NT)])
                to_at()
                for j in range(4):
                    tiles(1)
                    freed(dve.tensor_copy(QT[:, 2 * j:2 * j + 2, :], bank().rearrange("p (k t) -> p k t", k=2)))
                settled()

                def o_evac(i):
                    h = i // 2
                    o_split(at_hi[:, 2 * h:2 * h + 2, :], at_lo[:, 2 * h:2 * h + 2, :], 2)
                attention(8, 1, lambda i: TOK, "cross", 256 ** -0.5, lambda i: i % 2 == 1, o_evac)
                residual_add(2)
                layer_norm_tiles()

            def top2(v, n, rank, cmp):
                D1(dve.memset(rank, 0.0))
                for i in range(n):
                    if i + 1 < n:
                        w = n - 1 - i
                        D1(dve.tensor_tensor(cmp[:, :, 0:w], v[:, :, i:i + 1].to_broadcast([P, v.shape[1], w]), v[:, :, i + 1:n], ALU.is_ge))
                        D1(dve.tensor_tensor(rank[:, :, i + 1:n], rank[:, :, i + 1:n], cmp[:, :, 0:w], ALU.add))
                    if i:
                        D1(dve.tensor_tensor(cmp[:, :, 0:i], v[:, :, i:i + 1].to_broadcast([P, v.shape[1], i]), v[:, :, 0:i], ALU.is_gt))
                        D1(dve.tensor_tensor(rank[:, :, 0:i], rank[:, :, 0:i], cmp[:, :, 0:i], ALU.add))

            def router():
                full()
                b = bank()[:, 0:NT * N_EXP].rearrange("p (t e) -> p t e", t=NT)

                def R(j):
                    return rt[:, j, :, :]

                def small(j, k=0):
                    return rt[:, j, :, k:k + 1]
                D1(dve.tensor_reduce(small(0), b, AXX, ALU.max))
                freed(dve.tensor_tensor(R(1), b, small(0).to_broadcast([P, NT, N_EXP]), ALU.subtract))
                dve.wait_ge(wb_freed, c.get("wb"))
                ask(dve.tensor_copy(hs[:, 0, 0:1], hs[:, 0, 0:1]))
                done()
                D1(dve.tensor_reduce(small(0), R(1), AXX, ALU.add))
                D1(dve.reciprocal(small(0, 1), small(0)))
                D1(dve.tensor_tensor(R(1), R(1), small(0, 1).to_broadcast([P, NT, N_EXP]), ALU.mult))
                D1(dve.tensor_tensor(R(2), R(1), bc[:, B_RBIAS:B_RBIAS + N_EXP].unsqueeze(1).to_broadcast([P, NT, N_EXP]), ALU.add))
                v = R(2).rearrange("p t (g e) -> p (t g) e", e=4)
                rank = R(3).rearrange("p t (g e) -> p (t g) e", e=4)
                top2(v, 4, rank, R(4).rearrange("p t (g e) -> p (t g) e", e=4))
                D1(dve.tensor_scalar(R(3), R(3), 2.0, None, ALU.is_lt))
                D1(dve.tensor_tensor(R(4), R(2), R(3), ALU.mult))
                gs = rt[:, 5, :, 0:4]
                D1(dve.tensor_reduce(gs, R(4).rearrange("p t (g e) -> p t g e", e=4), AXX, ALU.add))
                grank = rt[:, 6, :, 0:4]
                top2(gs, 4, grank, rt[:, 7, :, 0:4])
                D1(dve.tensor_scalar(grank, grank, 1.0, None, ALU.is_lt))
                D1(dve.tensor_tensor(rank.rearrange("p (t g) e -> p t g e", t=NT), rank.rearrange("p (t g) e -> p t g e", t=NT),
                                     grank.unsqueeze(3).to_broadcast([P, NT, 4, 4]), ALU.mult))
                D1(dve.tensor_tensor(R(4), R(1), R(3), ALU.mult))
                D1(dve.tensor_reduce(small(0), R(4), AXX, ALU.add))
                D1(dve.reciprocal(small(0, 1), small(0)))
                ready(dve.tensor_tensor(R(11), R(4), small(0, 1).to_broadcast([P, NT, N_EXP]), ALU.mult))

            def moe(layer):
                to_at()
                router()
                for e2 in range(N_EXP // 2):
                    full()
                    freed(dve.tensor_copy(cbc[:, 2 * e2:2 * e2 + 2, :], bank().rearrange("p (e t) -> p e t", e=2)))
                dve.wait_ge(wb_freed, c.get("wb"))
                gated(N_EXP * F_EXPERT // P, True)
                residual_add(0)
                layer_norm_tiles(layer == 0)

            for layer in range(2):
                if layer == 0:
                    dve.wait_ge(x_landed, 32)
                    ready(dve.tensor_copy(hs[:, 0, 0:1], hs[:, 0, 0:1]))
                    ready(dve.tensor_copy(hs[:, 0, 0:1], hs[:, 0, 0:1]))
                to_at()
                if layer == 0:
                    D1(dve.tensor_copy(pos_f[:, :], pos_i[:, :]))
                    for t in range(NT):
                        D1(dve.tensor_scalar(trig[:, 0, t, :], bc[:, B_INVF:B_INVF + 8], pos_f[:, t:t + 1], None, ALU.mult))
                    D1(dve.tensor_scalar(trig[:, 1, :, :], trig[:, 0, :, :], 1.0 / TWO_PI, ROUND, ALU.mult, ALU.add))
                    D1(dve.tensor_scalar(trig[:, 1, :, :], trig[:, 1, :, :], -ROUND, None, ALU.add))
                    for k in (PI_HI, PI_MID, PI_LO):
                        D1(dve.scalar_tensor_tensor(trig[:, 0, :, :], trig[:, 1, :, :], -k, trig[:, 0, :, :], ALU.mult, ALU.add))
                    D1(dve.tensor_scalar(trig[:, 3, :, :], trig[:, 0, :, :], 3.1415925, -3.1415925, ALU.min, ALU.max))
                    D1(dve.tensor_scalar(trig[:, 1, :, :], trig[:, 3, :, :], -1.0, None, ALU.mult))
                    D1(dve.tensor_tensor(trig[:, 1, :, :], trig[:, 1, :, :], trig[:, 3, :, :], ALU.max))
                    ask(dve.tensor_scalar(trig[:, 2, :, :], trig[:, 1, :, :], -1.0, math.pi / 2, ALU.mult, ALU.add))
                    done()
                    for n in range(3):
                        y_to([H[:, t, n * 512:(n + 1) * 512] for t in range(NT)])
                    y_to([H[:, t, 1536:1792] for t in range(NT)], 256, 1)
                    settled()
                    dve.wait_ge(tab_landed, 16 * 5)
                    for t in range(NT):
                        ask(dve.tensor_copy(hs[:, 0, 0:1], hs[:, 0, 0:1]))
                    for g2 in range(2):
                        full()
                        freed(dve.tensor_tensor(WT[:, 4 * g2:4 * g2 + 4, :], bank().rearrange("p (g t) -> p g t", g=4),
                                          TAB[:, 256:384].unsqueeze(1).to_broadcast([P, 4, P]), ALU.mult))
                    for t in range(NT):
                        v = H[:, t, 0:640].rearrange("p (h d) -> p h d", h=10)
                        cos = trig[:, 2, t, :].unsqueeze(1).to_broadcast([P, 10, 8])
                        sin = trig[:, 3, t, :].unsqueeze(1).to_broadcast([P, 10, 8])
                        r = PBf[:, 0:320].rearrange("p (j h d) -> p j h d", j=4, h=10)
                        D1(dve.tensor_tensor(r[:, 0, :, :], v[:, :, 0:8], cos, ALU.mult))
                        D1(dve.tensor_tensor(r[:, 1, :, :], v[:, :, 8:16], sin, ALU.mult))
                        D1(dve.tensor_tensor(r[:, 2, :, :], v[:, :, 8:16], cos, ALU.mult))
                        D1(dve.tensor_tensor(r[:, 3, :, :], v[:, :, 0:8], sin, ALU.mult))
                        D1(dve.tensor_tensor(v[:, :, 0:8], r[:, 0, :, :], r[:, 1, :, :], ALU.subtract))
                        D1(dve.tensor_tensor(v[:, :, 8:16], r[:, 2, :, :], r[:, 3, :, :], ALU.add))
                        kd = PB[:, 3, t * 256:(t + 1) * 256].rearrange("p (h r d) -> p h r d", h=2, r=2)
                        k2 = H[:, t, 512:640].rearrange("p (h d) -> p h d", h=2)
                        D1(dve.tensor_copy(kd[:, :, 0, :], k2))
                        ready(dve.tensor_copy(kd[:, :, 1, :], k2))
                        cols_out(QT[:, 0:4, t * P:(t + 1) * P])
                        cols_out(KT[:, 0:2, t * P:(t + 1) * P])
                    dve.wait_ge(wb_freed, c.get("wb"))

                    def o_evac(i):
                        t = i // 8
                        o_split(at_hi[:, 0:4, t * P:(t + 1) * P], at_lo[:, 0:4, t * P:(t + 1) * P], 4)
                    attention(16, 1, lambda i: (i // 8 + 1) * P, "sink", 1.0, lambda i: i % 8 == 7, o_evac)
                    done()
                    done()
                    prm_wait()
                    for t in range(NT):
                        v = H[:, t, 1280:1792].rearrange("p (g c) -> p g c", g=8)
                        sq = PBf[:, 0:512].rearrange("p (g c) -> p g c", g=8)
                        D1(dve.tensor_reduce(hs[:, 0, 0:8], v, AXX, ALU.add))
                        D1(dve.tensor_scalar(hs[:, 0, 0:8], hs[:, 0, 0:8], 1.0 / 64, None, ALU.mult))
                        D1(dve.tensor_tensor(v, v, hs[:, 0, 0:8].unsqueeze(2).to_broadcast([P, 8, 64]), ALU.subtract))
                        D1(dve.tensor_tensor(sq, v, v, ALU.mult))
                        D1(dve.tensor_reduce(hs[:, 2, 0:8], sq, AXX, ALU.add))
                        ask(dve.tensor_scalar(hs[:, 1, 0:8], hs[:, 2, 0:8], 1.0 / 64, LN_EPS, ALU.mult, ALU.add))
                        done()
                        D1(dve.reciprocal(hs[:, 2, 0:8], hs[:, 1, 0:8]))
                        D1(dve.tensor_tensor(v, v, hs[:, 2, 0:8].unsqueeze(2).to_broadcast([P, 8, 64]), ALU.mult))
                        D1(dve.tensor_tensor(H[:, t, 1280:1792], H[:, t, 1280:1792], PRM[:, 0, 0:512], ALU.mult))
                        ready(dve.tensor_tensor(H[:, t, 1280:1792], H[:, t, 1280:1792], PRM[:, 0, 512:1024], ALU.add))
                    dve.tensor_copy(mv[:, 0:1], mv[:, 1:2]).then_inc(prm_used, 1)
                    for t in range(NT):
                        full()
                        b = bank().rearrange("p (g c) -> p g c", g=8)
                        sq = PBf[:, t * 512:(t + 1) * 512].rearrange("p (g c) -> p g c", g=8)
                        freed(dve.tensor_tensor(sq, b, col[:, C_SGUB:C_SGUB + 8].unsqueeze(2).to_broadcast([P, 8, 64]), ALU.add))
                        dve.wait_ge(wb_freed, c.get("wb"))
                        ready(dve.tensor_tensor(H[:, t, 768:1280], H[:, t, 768:1280], PBf[:, t * 512:(t + 1) * 512], ALU.mult))
                    for t in range(NT):
                        full()
                        b = bank().rearrange("p (k q) -> p k q", k=4)
                        hi_wait()
                        sl = (slice(None), slice(4, 8), slice(t * P, (t + 1) * P))
                        freed(lo_of(at_lo[sl], b, at_hi[sl]))
                else:
                    for n in range(2):
                        y_to([H[:, t, n * 512:(n + 1) * 512] for t in range(NT)])
                    settled()
                    ready(dve.tensor_copy(hs[:, 0, 0:1], hs[:, 0, 0:1]))
                    for j2 in range(4):
                        full()
                        hi_wait()
                        freed(lo_of(at_lo[:, 2 * j2:2 * j2 + 2, :], bank().rearrange("p (k t) -> p k t", k=2),
                              at_hi[:, 2 * j2:2 * j2 + 2, :]))
                    tiles(1)
                    for g in range(4):
                        b = bank()
                        for m in range(2):
                            ins = dve.tensor_scalar(PBf[:, m * TOK:(m + 1) * TOK], b[:, m * TOK:(m + 1) * TOK],
                                                    col[:, C_POOL + 2 * g + m:C_POOL + 2 * g + m + 1], None, ALU.mult)
                        ins.then_inc(aff_ready, 1)
                        c.add("aff")
                        dve.wait_ge(aff_ready, c.get("aff"))
                        hi_wait()
                        freed(lo_of(at_lo[:, 2 * g:2 * g + 2, :], PBf[:, 0:512].rearrange("p (k t) -> p k t", k=2),
                              at_hi[:, 2 * g:2 * g + 2, :]))
                cross(layer)
                moe(layer)

            diff(1)
            a, b8 = affine_of(0, 1, 0)
            rms_to_h()
            to_at(a, b8)
            dve.wait_ge(tab_landed, 16 * 8)
            for n in range(2):
                y_to([H[:, t, n * 512:(n + 1) * 512] for t in range(NT)])
            pair = c.get("y")
            tiles(2)
            for t in range(NT):
                D1(dve.tensor_copy(H[:, t, D:D + 256], ybank(pair, t)[:, 0:256]))
                ins = dve.tensor_copy(V[:, 2 + t, 0:256], ybank(pair, t)[:, 256:512])
                if t == NT - 1:
                    ins.then_inc(y_freed, 1)
                else:
                    D1(ins)
            c.add("y")
            settled()
            for t in range(NT):
                head_norm(t, 10, P, 0, RMS_EPS)
                head_gain(t, 8, P, 0, B_GQ)
                head_gain(t, 2, P, D, B_GK)
                ready(axial(t, 10, P))
            for t in range(NT):
                for j in range(2):
                    cols_out(QT[:, 4 * j:4 * j + 4, t * P:(t + 1) * P])
                cols_out(KT[:, 0:2, TOK + t * P:TOK + (t + 1) * P])
            dve.wait_ge(wb_freed, c.get("wb"))

            def o_evac(i):
                j = i // 4
                o_split(at_hi[:, 2 * j:2 * j + 2, :], at_lo[:, 2 * j:2 * j + 2, :], 2)
            attention(16, 1, lambda i: 512, "gqa", 128 ** -0.5, lambda i: i % 4 == 3, o_evac)
            residual_gate(2)
            a, b8 = affine_of(0, 1, 1)
            rms_to_h()
            to_at(a, b8)
            gated(F_FFN // P, False)
            residual_gate(0)
            dve.tensor_copy(hs[:, 0, 0:1], hs[:, 0, 0:1]).then_inc(result_ready, 1)



_INS = ["x", "mem", "positions", "router_w", "router_bias",
        "l0_w_in", "l0_sinks", "l0_sgu_ln_g", "l0_sgu_ln_b", "l0_sgu_w", "l0_sgu_b", "l0_w_out",
        "l0_ln1_g", "l0_ln1_b", "l0_xq", "l0_xkv", "l0_xo", "l0_ln2_g", "l0_ln2_b",
        "l0_e_gate", "l0_e_up", "l0_e_down", "l0_ln3_g", "l0_ln3_b",
        "l1_w_in", "l1_pool_w", "l1_pool_scale", "l1_w_out",
        "l1_ln1_g", "l1_ln1_b", "l1_xq", "l1_xkv", "l1_xo", "l1_ln2_g", "l1_ln2_b",
        "l1_e_gate", "l1_e_up", "l1_e_down", "l1_ln3_g", "l1_ln3_b",
        "c_2", "ctx_2", "c_ctx_2", "ada_w_2", "ada_b_2", "norm1_g_2", "norm2_g_2", "ffn_w_gu_2", "ffn_w_down_2",
        "diff_w_in_2", "diff_w_out_2", "diff_q_norm_2", "diff_k_norm_2", "diff_lambda_q1_2", "diff_lambda_k1_2",
        "diff_lambda_q2_2", "diff_lambda_k2_2", "diff_subln_2", "gqa_w_in_2", "gqa_w_out_2", "gqa_q_norm_2",
        "gqa_k_norm_2"]


def constants():
    f = np.float32
    i = np.arange(P)
    prev = np.where(i[None, :] > i[:, None], 0.0, -1e30)
    own = np.where(i[None, :] <= i[:, None], 0.0, -1e30)
    masks = np.concatenate([prev, own, (i[:, None] <= i[None, :]).astype(f)], axis=1)
    t, s = np.arange(TOK)[:, None], np.arange(TOK)[None, :]
    band = np.zeros((P, NT, 4, TOK), f)
    for g, w in enumerate(WINDOWS):
        m = ((t - s >= 0) & (t - s < w)) / np.minimum(t + 1, w) - (t == s)
        band[:, :, g, :] = m.T.reshape(NT, P, TOK).transpose(1, 0, 2)
    out = {"c_ident": np.eye(P, dtype=f), "c_masks": masks.astype(f), "c_band": band.reshape(P, NT, 4 * TOK),
           "c_invf": (500000.0 ** (-(np.arange(8) * 2.0 / 16))).astype(f)}
    row, cl = np.arange(TOK) // 64, np.arange(TOK) % 64
    for dh in (64, 128):
        half = dh // 2
        inv = (f(10000.0) ** (-np.arange(0, half, 2, dtype=f) / f(half))).astype(f)
        ang = [np.concatenate([a, a], axis=-1) for a in (row.astype(f)[:, None] * inv, cl.astype(f)[:, None] * inv)]
        ang = np.concatenate(ang, axis=-1)
        sign = np.tile(np.concatenate([-np.ones(half // 2), np.ones(half // 2)]), 2)
        out[f"c_ax{dh}"] = np.concatenate([np.cos(ang), np.sin(ang) * sign], axis=1).astype(f)
    return out


def kernel(**inputs):
    import concourse.bacc as bacc
    from concourse.bass_utils import run_bass_kernel_spmd

    nc = bacc.Bacc("TRN2", target_bir_lowering=False, num_devices=1, dynamic_dma_scratch_size=1024)
    arrays = {name: np.ascontiguousarray(inputs[name]) for name in _INS}
    arrays.update(constants())
    aps = {name: nc.dram_tensor(name, a.shape, mybir.dt.from_np(a.dtype), kind="ExternalInput").ap()
           for name, a in arrays.items()}
    out = nc.dram_tensor("out", (1, TOK, D), F32, kind="ExternalOutput").ap()
    build(nc, aps, out)
    r = run_bass_kernel_spmd(nc, [arrays], core_ids=[0])
    return r.results[0]["out"]
```

```python
from contextlib import ExitStack
import math

import numpy as np
import concourse.bass as bass
from concourse import mybir

F32 = mybir.dt.float32
F32R = mybir.dt.float32r
I32 = mybir.dt.int32
ACT = mybir.ActivationFunctionType
ALU = mybir.AluOpType
AXX = mybir.AxisListType.X

P = 128
TOK = 256
NT = TOK // P
D = 1024
KC = D // P
TILE = 2048
RAW, RING = 4, 4
LOOP_TILES = 12
F_EXPERT, N_EXP, N_GRP = 512, 16, 4
F_FFN = 2816
ALPHA = 4.0 ** 0.25
LN_EPS, RMS_EPS = 1e-5, 1e-6
WINDOWS = (2, 4, 8, 16)
LAMBDA_INIT = 0.8 - 0.6 * math.exp(0.0)
TWO_PI = 2.0 * math.pi
PI_HI, PI_MID = 6.28125, float(np.float32(0.0019350051879882812))
PI_LO = TWO_PI - PI_HI - PI_MID
ROUND = 12582912.0

C_LAT, C_CTX, C_N1, C_N2, C_POOL, C_SGUB, C_ROWS = 0, 8, 16, 32, 48, 56, 64
B_SINK, B_RBIAS, B_DQ, B_DK, B_SUB, B_GQ, B_GK, B_LAM, B_INVF, B_COLS = 0, 8, 24, 88, 152, 280, 408, 536, 792, 800


N_SETUP = 26
SLOTS = 64
T_IOTA, T_FOLD, T_COLS = 384, 448, 512
PAIR = dict(made=2, slots=2, gu=8, hidden=8, down=4, spread=2)


def gated_tiles(n_f):
    return n_f + n_f // 2


TOTAL = (2 * 24
         + 12 + 4 + gated_tiles(F_FFN // P) + 2
         + 7 + 5 + 2 * (4 + 8 + 4 + 4 + gated_tiles(N_EXP * F_EXPERT // P))
         + 12 + 4 + gated_tiles(F_FFN // P)
         + 6 + 4 + gated_tiles(F_FFN // P))


MOD_COLS_AT = 20
N_MOD = 48
MOE_TILES = gated_tiles(N_EXP * F_EXPERT // P)
LAYER_TILES = 4 + 4 + 4 + 4 + 4 + MOE_TILES
MOE_AT = [N_MOD + 16 + gated_tiles(F_FFN // P) + 2 + 7 + 20]
MOE_AT.append(MOE_AT[0] + MOE_TILES + 5 + 20)


def by_vector(n):
    return any(0 <= n - at - 2 < MOE_TILES - 3 and n % 2 == at % 2 for at in MOE_AT)


def lo_count(n):
    mine = sum(by_vector(j) for j in range(n + 1))
    return (True, mine) if by_vector(n) else (False, n + 1 - N_MOD - mine)


class Count:

    STRIDE = dict(tile=LOOP_TILES, wb=8, gu=8)

    def __init__(self, stride=None):
        self.n = {}
        self.i = None
        self.stride = stride or self.STRIDE

    def get(self, name):
        return self.n.get(name, 0)

    def add(self, name, k=1):
        self.n[name] = self.get(name) + k

    def at(self, name, offset=0):
        value = self.get(name) + offset
        return value if self.i is None else self.i * self.stride[name] + value

    def enter(self, i):
        self.i, self.entered = i, dict(self.n)

    def lo(self, n, moe):
        vector, value = lo_count(n)
        if self.i is not None:
            stride = LOOP_TILES // 2 if moe else LOOP_TILES
            value = self.i * stride + value
        return vector, value

    def leave(self, iterations):
        self.i = None
        for name, stride in self.stride.items():
            gone = self.get(name) - self.entered.get(name, 0)
            assert gone in (0, stride), (name, gone)
            self.add(name, gone * (iterations - 1))


def steps_of(n_f):
    steps = n_f // 2 - 1
    return steps, (steps - 1) // 4


def build(nc, A, out):
    ctx = ExitStack()
    with ctx:
        def sb(name, shape, dt=F32):
            return ctx.enter_context(nc.sbuf_tensor(name, shape, dt))

        def sem(name):
            return ctx.enter_context(nc.semaphore(name))

        def dram(name, shape):
            return nc.dram_tensor(name, shape, F32, kind="Internal").ap()

        raw = sb("raw", [P, RAW, TILE])
        w_hi = sb("w_hi", [P, RING, TILE], F32R)
        w_lo = sb("w_lo", [P, RING, TILE], F32R)
        X = sb("X", [P, NT, D])
        at_hi = sb("at_hi", [P, KC, TOK], F32R)
        at_lo = sb("at_lo", [P, KC, TOK], F32R)
        he_hi = sb("he_hi", [P, 4, TOK], F32R)
        he_lo = sb("he_lo", [P, 4, TOK], F32R)
        H = sb("H", [P, NT, 2048])
        KT = sb("KT", [P, KC, 512])
        V = sb("V", [P, 4, D])
        QT = sb("QT", [P, KC, TOK])
        PB = sb("PB", [P, 4, 512])
        PT = sb("PT", [P, 2, 4, TOK])
        PRM = sb("PRM", [P, 2, D])
        TAB = sb("TAB", [P, 512])
        ident = sb("ident", [P, P])
        colin = sb("colin", [P, P])
        col = sb("col", [P, C_ROWS])
        modcol = sb("modcol", [P, 2, 96])
        affA = sb("affA", [P, KC])
        bc = sb("bc", [P, B_COLS])
        rw = sb("rw", [P, KC, N_EXP])
        rw_hi = sb("rw_hi", [P, KC, N_EXP], F32R)
        rw_lo = sb("rw_lo", [P, KC, N_EXP], F32R)
        cond = sb("cond", [P, 2, KC])
        pos_i = sb("pos_i", [P, NT], I32)
        pos_f = sb("pos_f", [P, NT])
        trig = sb("trig", [P, 4, NT, 8])
        lam = sb("lam", [P, 4])
        bn = sb("bn", [P, 2, 6])
        mv = sb("mv", [P, 2])
        ms = sb("ms", [P, 6])
        st = sb("st", [P, 8, 4])
        hs = sb("hs", [P, 3, 32])
        rt = sb("rt", [P, 12, NT, N_EXP])
        route = sb("route", [1, 1], I32)
        PS = ctx.enter_context(nc.psum_tensor("PS", [P, 8, 512], F32))

        mods_d = dram("mods_d", (2, 12 * D))
        kd_d, vd_d = dram("kd_d", (P, KC, TOK)), dram("vd_d", (P, NT, D))
        kg_d, vg_d = dram("kg_d", (P, 2, TOK)), dram("vg_d", (P, NT, TOK))

        raw_landed = [sem(f"raw_landed{i}") for i in range(RAW)]
        hi_done = sem("hi_done")
        lo_done = sem("lo_done")
        lo_done_v = sem("lo_done_v")
        tile_used = sem("tile_used")
        wb_full, wb_freed = sem("wb_full"), sem("wb_freed")
        y_freed = sem("y_freed")
        o_full = sem("o_full")
        t_full, t_freed = sem("t_full"), sem("t_freed")
        src_ready = sem("src_ready")
        hi_evac = sem("hi_evac")
        aff_ready = sem("aff_ready")
        stat_ready = sem("stat_ready")
        stat_done = sem("stat_done")
        max_ready, exp_done, p_ready = sem("max_ready"), sem("exp_done"), sem("p_ready")
        silu_done, he_f32, he_hi_done, he_ready = sem("silu_done"), sem("he_f32"), sem("he_hi_done"), sem("he_ready")
        dve_step = sem("dve_step")
        act_step = sem("act_step")
        setup_landed, x_landed, tab_landed, prm_landed = sem("setup_landed"), sem("x_landed"), sem("tab_landed"), sem("prm_landed")
        prm_used = sem("prm_used")
        mod_out, mod_in = sem("mod_out"), sem("mod_in")
        kv_out, kv_in = sem("kv_out"), sem("kv_in")
        route_ready = sem("route_ready")
        gathered_sems = ["slots_made",
                         "x_full", "x_hi", "x_ready",
                         "map_full", "map_ready",
                         "gu_copied",
                         "hidden_full", "hidden_silu", "hidden_read",
                         "hidden_ready",
                         "o_hi", "o_ready",
                         "y_full", "own"]
        gs = [{name: sem(f"l{layer}_{name}") for name in gathered_sems} for layer in range(2)]
        result_ready = sem("result_ready")
        out_done = sem("out_done")

        PBf = PB[:, :, :].rearrange("p a b -> p (a b)")
        KTf = KT[:, :, :].rearrange("p a b -> p (a b)")
        Vf = V[:, :, :].rearrange("p a b -> p (a b)")
        Hf = H[:, :, :].rearrange("p a b -> p (a b)")
        PTf = PT[:, :, :, :].rearrange("p a b c -> p (a b c)")
        PRMf = PRM[:, :, :].rearrange("p a b -> p (a b)")
        rtf = rt[:, :, :, :].rearrange("p a b c -> p (a b c)")
        mod_rows = [[(KTf, 0, 4096), (Vf, 0, 2048)], [(Vf, 2048, 2048), (PTf, 0, 2048), (PRMf, 0, 2048)]]
        mod_groups = [buf[0:2, at + g * 512:at + (g + 1) * 512] for layer in mod_rows for buf, at, n in layer
                      for g in range(n // 512)]
        mod_staged = [QT[0:96, 0, 0:P], rtf[0:96, 0:P]]
        QTf = QT[:, :, :].rearrange("p a b -> p (a b)")
        sgu_raw = KTf[:, 2048:3072].rearrange("p (g s) -> p g s", g=8)
        WT = QTf[:, 1024:2048].rearrange("p (g t) -> p g t", g=8)
        cbc = KTf.rearrange("p (e t) -> p e t", t=TOK)
        silu_buf = PBf[:, 0:512].rearrange("p (s t) -> p s t", s=2)
        he_buf = PBf[:, 512:1024].rearrange("p (s t) -> p s t", s=2)
        xe = [t[:, :, :].rearrange("p a (b s) -> p (a b) s", s=P) for t in (he_hi, he_lo)]
        hid = at_lo[:, 0:2, :].rearrange("p a (b s) -> p (a b) s", s=P)
        slot_map = at_lo[:, 2:4, :]
        o_parts = [at_hi[:, 4 * j:4 * j + 4, :].rearrange("p a b -> p (a b)") for j in range(2)]
        onehot = PBf[:, 0:512].rearrange("p (e t s) -> p e t s", e=2, t=NT)
        hid_f32 = PBf[:, 512:640].rearrange("p (e s) -> p e s", e=2)
        hid_silu = PBf[:, 640:768].rearrange("p (e s) -> p e s", e=2)
        gu_rows = PBf[:, 1024:1536].rearrange("p (e n) -> p e n", e=2)
        zero_row = Vf[0:1, 0:512]
        BAND = V[:, 0:2, :].rearrange("p a (g t) -> p a g t", g=4)

        mods_rows = mods_d.rearrange("c (l r p) -> l c r p", l=2, p=P)

        def gate_of(cnd, layer, part):
            lo = layer * 6 * D + part * D
            return mods_d[cnd:cnd + 1, lo:lo + D].rearrange("a d -> (a d)").partition_broadcast(P)

        def rowb(ap):
            return ap.partition_broadcast(P)

        prm_loads = []
        for part in (2, 5):
            prm_loads.append([(0, gate_of(1, 0, part))])
        prm_loads.append([(0, (A["l0_sgu_ln_g"], A["l0_sgu_ln_b"]))])
        for layer in (0, 1):
            for n in (1, 2, 3):
                prm_loads.append([(0, rowb(A[f"l{layer}_ln{n}_g"])), (1, rowb(A[f"l{layer}_ln{n}_b"]))])
        for layer in (0, 1):
            for part in (2, 5):
                prm_loads.append([(0, gate_of(0, layer, part))])

        ada = [A["ada_w_2"][i] for i in range(2)]
        gu_w = [A["ffn_w_gu_2"][i] for i in range(2)]
        dn_w = [A["ffn_w_down_2"][i] for i in range(2)]
        diff_in, diff_out = A["diff_w_in_2"][0], A["diff_w_out_2"][0]
        gqa_in, gqa_out = A["gqa_w_in_2"][0], A["gqa_w_out_2"][0]

        block = ctx.enter_context(nc.Block())

        @block.sync
        def _(sp):
            c = Count()

            def load(pieces, moe=False):
                n = c.get("tile")
                slot = n % RAW
                if n >= N_MOD + RAW:
                    vector, value = c.lo(n - RAW, moe)
                    sp.wait_ge(lo_done_v if vector else lo_done, value)
                elif n >= RAW:
                    sp.wait_ge(tile_used, n + 1 - RAW)
                for dst, src in pieces(raw[:, slot, :]):
                    sp.dma_start(dst, src).then_inc(raw_landed[slot], 16)
                c.add("tile")

            def cols512(w, n0):
                for h in range(2):
                    def pieces(t, h=h):
                        v = t.rearrange("p (k n) -> p k n", n=512)
                        s = w[h * 512:(h + 1) * 512, n0:n0 + 512].rearrange("(k p) n -> p k n", p=P)
                        return [(v[:, 2 * j:2 * j + 2, :], s[:, 2 * j:2 * j + 2, :]) for j in range(2)]
                    load(pieces)

            def cols256(w, n0):
                def pieces(t):
                    v = t.rearrange("p (k n) -> p k n", n=256)
                    s = w[:, n0:n0 + 256].rearrange("(k p) n -> p k n", p=P)
                    return [(v[:, 4 * j:4 * j + 4, :], s[:, 4 * j:4 * j + 4, :]) for j in range(2)]
                load(pieces)

            def gated(gate, up, down, n_f, moe=False):
                def gu(q, f):
                    def pieces(t):
                        v = t.rearrange("p (g k n) -> p g k n", g=2, n=P)
                        return [(v[:, g, :, :], w(q, f).rearrange("(k p) n -> p k n", p=P))
                                for g, w in enumerate((gate, up))]
                    load(pieces, moe)

                def dn(q, f):
                    def pieces(t):
                        v = t.rearrange("p (j n) -> p j n", j=2)
                        return [(v[:, j, :], down(q, f + j)) for j in range(2)]
                    load(pieces, moe)

                steps, loops = steps_of(n_f)
                gu(0, 0)
                gu(0, 1)

                def step(q, m):
                    gu(q, 2 * m + 2)
                    gu(q, 2 * m + 3)
                    dn(q, 2 * m)
                step(0, 0)
                with sp.Fori(0, loops) as i:
                    c.enter(i)
                    for m in range(1, 5):
                        step(i, m)
                    c.leave(loops)
                for m in range(1 + 4 * loops, steps):
                    step(0, m)
                dn(0, 2 * steps)

            def ffn(layer):
                gu = gu_w[layer].rearrange("k (f n) -> k f n", n=P)
                dn = dn_w[layer].rearrange("(f p) n -> f p n", p=P)
                gated(lambda q, f: gu[:, q * 8 + f, :], lambda q, f: gu[:, q * 8 + (f + F_FFN // P), :],
                      lambda q, f: dn[q * 8 + f], F_FFN // P)

            def moe(layer):
                g, u, dw = (A[f"l{layer}_e_{s}"] for s in ("gate", "up", "down"))
                nf = F_EXPERT // P

                def part(w):
                    return lambda q, f: w[q * 2 + f // nf, :, (f % nf) * P:(f % nf + 1) * P]

                def down(q, f):
                    return dw[q * 2 + f // nf, (f % nf) * P:(f % nf + 1) * P, :]
                assert c.get("tile") == MOE_AT[layer]
                gated(part(g), part(u), down, N_EXP * nf, True)

            def gemm(w, n0, n1):
                for n in range(n0, n1, 512):
                    cols512(w, n)

            def by256(w, n0, n1):
                for n in range(n0, n1, 256):
                    cols256(w, n)

            for layer in range(2):
                gemm(ada[layer], 0, 6 * D)
            gemm(diff_in, 0, 3 * D)
            gemm(diff_out, 0, D)
            ffn(0)
            gemm(gqa_in, D, D + 512)
            for layer in range(2):
                if layer == 0:
                    gemm(A["l0_w_in"], 0, 1536)
                    cols256(A["l0_w_in"], 1536)
                else:
                    gemm(A["l1_w_in"], 0, D)
                    pw = A["l1_pool_w"].rearrange("g (c p) d -> p g c d", p=P)
                    load(lambda t: [(t.rearrange("p (g c d) -> p g c d", g=4, c=2)[:, :, j, :], pw[:, :, j, :])
                                    for j in range(2)])
                gemm(A[f"l{layer}_w_out"], 0, D)
                by256(A[f"l{layer}_xkv"], 0, D)
                gemm(A[f"l{layer}_xkv"], D, 2 * D)
                by256(A[f"l{layer}_xq"], 0, D)
                gemm(A[f"l{layer}_xo"], 0, D)
                moe(layer)
            gemm(diff_in, 0, 3 * D)
            gemm(diff_out, 0, D)
            ffn(0)
            gemm(gqa_in, 0, D + 512)
            gemm(gqa_out, 0, D)
            ffn(1)
            assert c.get("tile") == TOTAL
            sp.wait_ge(result_ready, 1)
            sp.dma_start(out[0].rearrange("(t p) d -> p t d", p=P), X[:, :, :]).then_inc(out_done, 16)
            sp.wait_ge(out_done, 16)
            sp.wait_ge(mod_out, 80)
            sp.wait_ge(kv_out, 64)

        @block.gpsimd
        def _(pool):
            c = Count()

            def lo():
                n = c.get("tile")
                if not by_vector(n):
                    pool.wait_ge(hi_done, c.at("tile", 1 - N_MOD))
                    nc.gpsimd.tensor_tensor(w_lo[:, n % RING, :], raw[:, n % RAW, :],
                                            w_hi[:, n % RING, :].bitcast(F32), ALU.subtract).then_inc(lo_done, 1)
                c.add("tile")

            def lo_until(end, head=0):
                for _ in range(head):
                    lo()
                loops = (end - c.get("tile")) // LOOP_TILES
                with pool.Fori(0, loops) as i:
                    c.enter(i)
                    for _ in range(LOOP_TILES):
                        lo()
                    c.leave(loops)
                while c.get("tile") < end:
                    lo()

            c.add("tile", N_MOD)
            for at in MOE_AT:
                lo_until(at)
                lo_until(at + MOE_TILES, 5)
            lo_until(TOTAL)

        @block.tensor
        def _(pe):
            c = Count()

            def tile_wait(moe=False):
                vector, value = c.lo(c.get("tile"), moe)
                pe.wait_ge(lo_done_v if vector else lo_done, value)
                slot = c.get("tile") % RING
                return w_hi[:, slot, :], w_lo[:, slot, :]

            def tile_end(ins):
                ins.then_inc(tile_used, 1)
                c.add("tile")

            def wb_wait():
                if c.get("wb") >= 4:
                    pe.wait_ge(wb_freed, c.at("wb", -3))
                bank = PS[:, 4 + c.get("wb") % 4, :]
                c.add("wb")
                return bank

            def y_wait(pairs=1):
                if c.get("y") + pairs > 2:
                    pe.wait_ge(y_freed, c.get("y") + pairs - 2)
                at = c.get("y")
                c.add("y", pairs)
                return at % 2

            def parts(dst, s_hi, s_lo, m_hi, m_lo, first, last):
                pe.matmul(dst, s_hi, m_hi, start=first, stop=False)
                pe.matmul(dst, s_hi, m_lo, start=False, stop=False)
                return pe.matmul(dst, s_lo, m_hi, start=False, stop=last)

            def at_wait():
                pe.wait_ge(wb_freed, c.at("wb"))

            def transpose_src(n=1):
                c.add("src", n)
                pe.wait_ge(src_ready, c.get("src"))

            def to_at(src):
                for t in range(NT):
                    transpose_src()
                    for h in range(2):
                        bank = wb_wait()
                        for j in range(4):
                            k = 4 * h + j
                            ins = pe.transpose(bank[:, j * P:(j + 1) * P], src[:, t, k * P:(k + 1) * P], ident[:, :])
                        ins.then_inc(wb_full, 1)
                at_wait()

            def gemm(groups, width=512):
                for _ in range(groups):
                    pair = y_wait()
                    tiles = width * KC // TILE
                    for h in range(tiles):
                        hi, lo = tile_wait()
                        nk = KC // tiles
                        for kk in range(nk):
                            k = h * nk + kk
                            for t in range(NT):
                                ins = parts(PS[:, 2 * pair + t, 0:width],
                                            at_hi[:, k, t * P:(t + 1) * P], at_lo[:, k, t * P:(t + 1) * P],
                                            hi[:, kk * width:(kk + 1) * width], lo[:, kk * width:(kk + 1) * width],
                                            k == 0, k == KC - 1)
                        tile_end(ins)

            def gemm_t(tiles):
                for _ in range(tiles):
                    bank = wb_wait()
                    hi, lo = tile_wait()
                    for m in range(2):
                        for k in range(KC):
                            at = k * 256 + m * P
                            ins = parts(bank[:, m * TOK:(m + 1) * TOK], hi[:, at:at + P], lo[:, at:at + P],
                                        at_hi[:, k, :], at_lo[:, k, :], k == 0, k == KC - 1)
                    tile_end(ins)

            def gated(n_f, moe=False):
                pair = y_wait(2)

                def gu():
                    bank = wb_wait()
                    hi, lo = tile_wait(moe)
                    for g in range(2):
                        for k in range(KC):
                            at = (g * KC + k) * P
                            ins = parts(bank[:, g * TOK:(g + 1) * TOK], hi[:, at:at + P], lo[:, at:at + P],
                                        at_hi[:, k, :], at_lo[:, k, :], k == 0, k == KC - 1)
                    tile_end(ins)

                def dn(first, last):
                    c.add("gu", 2)
                    pe.wait_ge(he_ready, c.at("gu"))
                    hi, lo = tile_wait(moe)
                    f0 = (c.get("gu") - 2) % 4
                    for j in range(2):
                        for t in range(NT):
                            s_hi = he_hi[:, f0 + j, t * P:(t + 1) * P]
                            s_lo = he_lo[:, f0 + j, t * P:(t + 1) * P]
                            for n in range(2):
                                at = j * D + n * 512
                                ins = parts(PS[:, 2 * ((pair + n) % 2) + t, :], s_hi, s_lo, hi[:, at:at + 512],
                                            lo[:, at:at + 512], first and j == 0, last and j == 1)
                    tile_end(ins)

                steps, loops = steps_of(n_f)
                gu()
                gu()

                def step(first=False):
                    gu()
                    gu()
                    dn(first, False)
                step(True)
                with pe.Fori(0, loops) as i:
                    c.enter(i)
                    for _ in range(4):
                        step()
                    c.leave(loops)
                for _ in range(1 + 4 * loops, steps):
                    step()
                dn(False, True)

            def attention(n, s_groups, scores, n_chunks, pv):
                pe.wait_ge(y_freed, c.get("y"))
                pe.wait_ge(wb_freed, c.get("wb"))

                def transposed(i):
                    c.add("p")
                    pe.wait_ge(p_ready, c.get("p"))
                    if c.get("t") >= 2:
                        pe.wait_ge(t_freed, c.get("t") - 1)
                    bank = PS[:, 1 + 2 * (c.get("t") % 2), :]
                    for j in range(n_chunks(i)):
                        ins = pe.transpose(bank[:, j * P:(j + 1) * P], prob(i, n_chunks(i))[:, j * P:(j + 1) * P], ident[:, :])
                    ins.then_inc(t_full, 1)
                    c.add("t")

                def prob(i, _):
                    return PB[:, i % 4, :] if s_groups == 1 else PB[:, 2 * (i % 2), :]

                base = c.get("t")
                for it in range(n + 3):
                    if it < n:
                        for g in range(s_groups):
                            bank = wb_wait()
                            scores(it, g, bank).then_inc(wb_full, 1)
                    if 0 <= it - 2 < n:
                        transposed(it - 2)
                    if 0 <= it - 3 < n:
                        pe.wait_ge(t_freed, base + it - 2)
                        pv(it - 3)
                pe.wait_ge(t_freed, c.get("t"))

            def o_bank():
                pair = y_wait()
                return PS[:, 2 * pair, :]

            def to_cols(srcs):
                for at in range(0, len(srcs), 4):
                    bank = wb_wait()
                    for j, s in enumerate(srcs[at:at + 4]):
                        ins = pe.transpose(bank[:, j * P:(j + 1) * P], s, ident[:, :])
                    ins.then_inc(wb_full, 1)

            pe.wait_ge(setup_landed, 16 * N_SETUP)
            bank = wb_wait()
            pe.transpose(bank[:, 0:C_ROWS], colin[0:C_ROWS, :], ident[0:C_ROWS, 0:C_ROWS]).then_inc(wb_full, 1)
            pe.wait_ge(act_step, 1)
            def mod_cols(layer):
                pe.wait_ge(mod_in, 32 * (layer + 1))
                bank = wb_wait()
                pe.transpose(bank[:, 0:96], mod_staged[layer], ident[0:96, 0:96]).then_inc(wb_full, 1)

            for j in range(len(mod_groups)):
                bank = wb_wait()
                for h in range(2):
                    n = c.get("tile")
                    pe.wait_ge(raw_landed[n % RAW], 32 * (n // RAW + 1))
                    for kk in range(4):
                        k = 4 * h + kk
                        ins = pe.matmul(bank[0:2, :], cond[:, :, k], raw[:, n % RAW, kk * 512:(kk + 1) * 512],
                                        start=k == 0, stop=k == KC - 1)
                    tile_end(ins)
                if j == MOD_COLS_AT:
                    mod_cols(0)

            def diff(path):
                nk = TOK * (1 + path)
                to_at(H)
                gemm(6)
                for t in range(NT):
                    transpose_src()
                    to_cols([H[:, t, j * P:(j + 1) * P] for j in range(16)])

                def scores(i, m, bank):
                    t, h = divmod(i, 8)
                    r = slice(64 * m, 64 * m + 64)
                    return pe.matmul(bank[:, 0:nk], QT[r, h, t * P:(t + 1) * P], KT[r, h, 0:nk], start=True, stop=True)

                state = {}

                def pv(i):
                    h = i % 8
                    if h % 4 == 0:
                        state["bank"] = o_bank()
                    for kc in range(nk // P):
                        ins = pe.matmul(state["bank"][:, (h % 4) * P:(h % 4 + 1) * P], PT[:, i % 2, kc, 0:P],
                                        V[:, kc, h * P:(h + 1) * P], start=kc == 0, stop=kc == nk // P - 1)
                    if h % 4 == 3:
                        ins.then_inc(o_full, 1)
                if path:
                    pe.wait_ge(kv_in, 32)
                attention(16, 2, scores, lambda i: nk // P, pv)
                to_at(H)
                gemm(2)
                to_at(H)
                gated(F_FFN // P)

            def gqa_kv_cols(t, first):
                return [H[:, t, first + j * P:first + (j + 1) * P] for j in range(2)]

            diff(0)
            mod_cols(1)
            to_at(H)
            gemm(1)
            for t in range(NT):
                transpose_src()
                to_cols(gqa_kv_cols(t, 0))

            def cross(layer):
                to_at(H)
                gemm_t(4)
                gemm(2)
                to_at(X)
                gemm_t(4)

                def scores(i, _, bank):
                    h, t = divmod(i, 2)
                    for j in range(2):
                        ins = pe.matmul(bank[:, 0:TOK], QT[:, 2 * h + j, t * P:(t + 1) * P], KT[:, 2 * h + j, 0:TOK],
                                        start=j == 0, stop=j == 1)
                    return ins

                def pv(i):
                    h, t = divmod(i, 2)
                    if t == 0:
                        return
                    bank = o_bank()
                    for dc in range(2):
                        for kc in range(2):
                            at = h * 256 + dc * P
                            ins = pe.matmul(bank[:, dc * TOK:(dc + 1) * TOK], V[:, kc, at:at + P], PT[:, h % 2, kc, :],
                                            start=kc == 0, stop=kc == 1)
                    ins.then_inc(o_full, 1)
                attention(8, 1, scores, lambda i: 2, pv)
                pe.wait_ge(y_freed, c.get("y"))
                gemm(2)

            def moe(layer):
                to_at(X)
                bank = wb_wait()
                for k in range(KC):
                    ins = parts(bank[0:N_EXP, 0:TOK], rw_hi[:, k, :], rw_lo[:, k, :], at_hi[:, k, :], at_lo[:, k, :],
                                k == 0, k == KC - 1)
                ins.then_inc(wb_full, 1)
                transpose_src()
                bank = wb_wait()
                for t in range(NT):
                    ins = pe.transpose(bank[:, t * N_EXP:(t + 1) * N_EXP], PBf[0:N_EXP, t * P:(t + 1) * P],
                                       ident[0:N_EXP, 0:N_EXP])
                ins.then_inc(wb_full, 1)
                transpose_src()
                bank = wb_wait()
                upto, ones = TAB[:, 256:384], TAB[:, 383:384].to_broadcast([P, P])
                for at, pairs in enumerate((((upto, 0),), ((ones, 0), (upto, 1)), ((ones, 0), (ones, 1)))):
                    for j, (w, t) in enumerate(pairs):
                        ins = pe.matmul(bank[:, at * N_EXP:(at + 1) * N_EXP], w, rt[:, 3, t, :], start=j == 0,
                                        stop=j == len(pairs) - 1)
                ins.then_inc(wb_full, 1)
                pe.wait_ge(route_ready, layer + 1)
                most = pe.value_load(route[0:1, 0:1], min_val=0, max_val=TOK)
                with pe.If(most <= SLOTS):
                    before = dict(c.n)
                    experts_gathered(layer)
                    c.n = before
                with pe.Else():
                    experts_dense()

            def experts_gathered(layer):
                g, q = gs[layer], Count(PAIR)
                for name in PAIR:
                    q.add(name, 0)
                pair = y_wait(2)

                def y_bank(n, t):
                    return PS[:, 2 * ((pair + n) % 2) + t, :]

                def slots():
                    p = q.get("slots") % 2
                    q.add("slots")
                    pe.wait_ge(g["slots_made"], q.at("slots"))
                    for k in range(KC):
                        for t in range(NT):
                            ins = pe.matmul(PS[:, 6, k * SLOTS:(k + 1) * SLOTS], X[:, t, k * P:(k + 1) * P],
                                            onehot[:, p, t, 0:SLOTS], start=t == 0, stop=t == NT - 1)
                    ins.then_inc(g["x_full"], 1)
                    for t in range(NT):
                        pe.matmul(PS[:, 7, TOK:TOK + 1], onehot[:, p, t, :], rt[:, 10, t, 2 * p + 1:2 * p + 2],
                                  start=t == 0, stop=t == NT - 1)
                    for t in range(NT):
                        ins = pe.matmul(PS[:, 7, t * P:(t + 1) * P], onehot[:, p, t, :], ident[:, :], start=True, stop=True)
                    ins.then_inc(g["map_full"], 1)

                def gu():
                    n = q.get("gu")
                    hi, lo = tile_wait(True)
                    if n % 4 == 0:
                        value = n // 4 + 1
                        pe.wait_ge(g["x_ready"], value if q.i is None else q.i * 2 + value)
                    if n >= 2:
                        pe.wait_ge(g["hidden_read"], q.at("gu", -1))
                    for k in range(KC):
                        for w in (hi, lo):
                            ins = pe.matmul(PS[:, 4 + n % 2, 0:2 * P], xe[n // 4 % 2][:, k, :],
                                            w.rearrange("p (g k n) -> p g k n", g=2, n=P)[:, :, k, :],
                                            start=k == 0 and w is hi, stop=k == KC - 1 and w is lo)
                    tile_end(ins)
                    q.add("gu")

                def hidden():
                    n = q.get("hidden")
                    q.add("hidden")
                    pe.wait_ge(g["gu_copied"], q.at("hidden"))
                    for j in range(2):
                        at = 2 * P + j * SLOTS
                        ins = pe.matmul(PS[:, 4 + n % 2, at:at + SLOTS], gu_rows[:, n % 2, j * P:(j + 1) * P],
                                        TAB[:, T_FOLD:T_FOLD + SLOTS], start=True, stop=True)
                    ins.then_inc(g["hidden_full"], 1)

                def down():
                    n = q.get("down")
                    q.add("down")
                    value = 2 * q.get("down")
                    pe.wait_ge(g["hidden_ready"], value if q.i is None else q.i * 8 + value)
                    if n % 2 == 0:
                        pe.wait_ge(g["x_ready"], q.at("slots"))
                        pe.wait_ge(g["map_ready"], q.at("slots"))
                    hi, lo = tile_wait(True)
                    for j in range(2):
                        for m in range(2):
                            at = j * D + m * 512
                            for w in (hi, lo):
                                ins = pe.matmul(PS[:, 6 + m, :], hid[:, (2 * n + j) % 4, :], w[:, at:at + 512],
                                                start=n % 2 == 0 and j == 0 and w is hi,
                                                stop=n % 2 == 1 and j == 1 and w is lo)
                    tile_end(ins)

                def spread(last=False):
                    p = q.get("spread") % 2
                    q.add("spread")
                    pe.wait_ge(g["o_ready"], q.at("spread"))
                    for part in range(2):
                        for t in range(NT):
                            for m in range(2):
                                ins = pe.matmul(y_bank(m, t), slot_map[:, p, t * P:(t + 1) * P],
                                                o_parts[part][:, m * 512:(m + 1) * 512], start=False,
                                                stop=last and part == 1)
                    return ins

                def step(m, first=False, last=False):
                    gu()
                    hidden()
                    if m % 2 == 0 and not first:
                        spread()
                    if m % 2 == 0 and not last:
                        slots()
                    gu()
                    hidden()
                    down()

                pe.wait_ge(wb_freed, c.get("wb"))
                slots()
                for m in range(2):
                    for t in range(NT):
                        pe.matmul(y_bank(m, t), ident[0:1, :], zero_row, start=True, stop=False)
                gu()
                gu()
                hidden()
                pe.wait_ge(g["map_ready"], 1)
                step(0, first=True)
                steps, loops = steps_of(N_EXP * F_EXPERT // P)
                with pe.Fori(0, loops) as i:
                    c.enter(i)
                    q.enter(i)
                    for m in range(1, 5):
                        step(m)
                    c.leave(loops)
                    q.leave(loops)
                for m in range(1 + 4 * loops, steps):
                    step(m, last=m == steps - 1)
                hidden()
                down()
                spread(last=True).then_inc(g["y_full"], 1)
                pe.sem_inc(wb_full, N_EXP // 2)

            def experts_dense():
                for e2 in range(N_EXP // 2):
                    bank = wb_wait()
                    for e in (2 * e2, 2 * e2 + 1):
                        for t in range(NT):
                            at = (e % 2) * TOK + t * P
                            ins = pe.matmul(bank[:, at:at + P], rt[:, 11, t, e:e + 1].to_broadcast([P, P]), ident[:, :],
                                            start=True, stop=True)
                    ins.then_inc(wb_full, 1)
                gated(N_EXP * F_EXPERT // P, True)

            for layer in range(2):
                to_at(X)
                if layer == 0:
                    pe.wait_ge(tab_landed, 16 * 5)
                    gemm(3)
                    gemm(1, 256)
                    to_cols([sgu_raw[:, g, :] for g in range(8)])
                    for t in range(NT):
                        transpose_src()
                        to_cols([H[:, t, j * P:(j + 1) * P] for j in range(4)])
                        to_cols([PB[:, 3, (2 * t + j) * P:(2 * t + j + 1) * P] for j in range(2)])

                    def scores(i, _, bank):
                        t, h = divmod(i, 8)
                        r = slice(64 * (h % 2), 64 * (h % 2) + 64)
                        nk = (t + 1) * P
                        return pe.matmul(bank[:, 0:nk], QT[r, h // 2, t * P:(t + 1) * P], KT[r, h // 4, 0:nk],
                                         start=True, stop=True)

                    state = {}

                    def pv(i):
                        t, h = divmod(i, 8)
                        if h == 0:
                            state["bank"] = o_bank()
                        r = slice(64 * (h % 2), 64 * (h % 2) + 64)
                        v0 = 640 + 64 * (h // 4)
                        for kc in range(t + 1):
                            ins = pe.matmul(state["bank"][r, (h // 2) * P:(h // 2 + 1) * P], H[:, kc, v0:v0 + 64],
                                            PT[:, i % 2, kc, 0:P], start=kc == 0, stop=kc == t)
                        if h == 7:
                            ins.then_inc(o_full, 1)
                    attention(16, 1, scores, lambda i: i // 8 + 1, pv)
                    pe.wait_ge(y_freed, c.get("y"))
                    for t in range(NT):
                        transpose_src()
                        bank = wb_wait()
                        for g in range(8):
                            ins = pe.matmul(bank[:, g * 64:(g + 1) * 64], WT[:, g, :],
                                            H[:, t, 1280 + 64 * g:1344 + 64 * g], start=True, stop=True)
                        ins.then_inc(wb_full, 1)
                    for t in range(NT):
                        transpose_src()
                        to_cols([H[:, t, 768 + j * P:768 + (j + 1) * P] for j in range(4)])
                    at_wait()
                else:
                    gemm(2)
                    transpose_src()
                    pe.wait_ge(tab_landed, 16 * 6)
                    for j2 in range(4):
                        bank = wb_wait()
                        for j in (2 * j2, 2 * j2 + 1):
                            for s in range(NT):
                                ins = pe.matmul(bank[:, (j % 2) * TOK:(j % 2 + 1) * TOK], H[:, s, j * P:(j + 1) * P],
                                                BAND[:, s, j2, :], start=s == 0, stop=s == NT - 1)
                        ins.then_inc(wb_full, 1)
                    at_wait()
                    hi, lo = tile_wait()
                    for g in range(4):
                        bank = wb_wait()
                        for m in range(2):
                            for cc in range(2):
                                at = (2 * g + cc) * 256 + m * P
                                ins = parts(bank[:, m * TOK:(m + 1) * TOK], hi[:, at:at + P], lo[:, at:at + P],
                                            at_hi[:, 2 * g + cc, :], at_lo[:, 2 * g + cc, :], cc == 0, cc == 1)
                    tile_end(ins)
                    at_wait()
                gemm(2)
                cross(layer)
                moe(layer)

            diff(1)
            to_at(H)
            gemm(3)
            for t in range(NT):
                transpose_src()
                to_cols([H[:, t, j * P:(j + 1) * P] for j in range(10)])

            def scores(i, _, bank):
                h, t = divmod(i, 2)
                return pe.matmul(bank, QT[:, h, t * P:(t + 1) * P], KT[:, h // 4, :], start=True, stop=True)

            state = {}

            def pv(i):
                h, t = divmod(i, 2)
                if t == 0:
                    return
                if h % 2 == 0:
                    state["bank"] = o_bank()
                for kc in range(4):
                    ins = pe.matmul(state["bank"][:, (h % 2) * TOK:(h % 2 + 1) * TOK],
                                    V[:, kc, (h // 4) * P:(h // 4 + 1) * P], PT[:, h % 2, kc, :],
                                    start=kc == 0, stop=kc == 3)
                if h % 2 == 1:
                    ins.then_inc(o_full, 1)
            pe.wait_ge(kv_in, 64)
            attention(16, 1, scores, lambda i: 4, pv)
            pe.wait_ge(y_freed, c.get("y"))
            gemm(2)
            to_at(H)
            gated(F_FFN // P)

        @block.scalar
        def _(act):
            c = Count()

            def split():
                n = c.get("split")
                i = c.i
                use = 32 * (n // RAW + 1)
                act.wait_ge(raw_landed[n % RAW], use if i is None else i * (32 * LOOP_TILES // RAW) + use)
                if n >= N_MOD + RING:
                    used = n - RING + 1
                    act.wait_ge(tile_used, used if i is None else i * LOOP_TILES + used)
                nc.scalar.activation(w_hi[:, n % RING, :], raw[:, n % RAW, :], ACT.Copy).then_inc(hi_done, 1)
                c.add("split")

            def ahead(more=RING):
                while c.get("split") < min(c.get("tile") + more, TOTAL):
                    split()

            def tiles(n):
                for _ in range(n):
                    c.add("tile")
                    ahead()

            def full():
                ahead()
                c.add("full")
                act.wait_ge(wb_full, c.get("full"))

            def bank():
                b = PS[:, 4 + c.get("wb") % 4, :]
                c.add("wb")
                return b

            def prm():
                n = c.get("prm")
                ahead()
                if n:
                    act.wait_ge(prm_used, n)
                for j, src in prm_loads[n]:
                    if isinstance(src, tuple):
                        for m, s in enumerate(src):
                            act.dma_start(PRM[:, 0, m * 512:(m + 1) * 512], rowb(s)).then_inc(prm_landed, 16)
                    else:
                        act.dma_start(PRM[:, j, :], src).then_inc(prm_landed, 16)
                c.add("prm")

            def stat():
                ahead()
                c.add("stat")
                act.wait_ge(stat_ready, c.get("stat"))

            def root(ap):
                stat()
                nc.scalar.activation(ap, ap, ACT.Sqrt).then_inc(stat_done, 1)

            def hi_of(dst, src):
                nc.scalar.activation(dst, src, ACT.Copy).then_inc(hi_evac, 1)

            def to_at(affine=False):
                for t in range(NT):
                    for h in range(2):
                        dst = at_hi[:, 4 * h:4 * h + 4, t * P:(t + 1) * P]
                        if affine:
                            ahead()
                            bank()
                            c.add("full")
                            c.add("aff")
                            act.wait_ge(aff_ready, c.get("aff"))
                            hi_of(dst, PBf[:, h * 512:(h + 1) * 512].rearrange("p (k t) -> p k t", k=4))
                        else:
                            full()
                            hi_of(dst, bank().rearrange("p (k t) -> p k t", k=4))

            def plain(n):
                c.add("full", n)
                c.add("wb", n)

            def gated(n_f, moe):
                def gu():
                    ahead()
                    act.wait_ge(tile_used, c.at("tile", 1))
                    f = c.get("gu")
                    nc.scalar.activation(silu_buf[:, f % 2, :], bank()[:, 0:TOK], ACT.Silu).then_inc(silu_done, 1)
                    c.add("tile")
                    c.add("gu")
                    if moe:
                        c.add("he32")
                        v = c.get("he32")
                        act.wait_ge(he_f32, v if c.i is None else c.i * 8 + v)
                    else:
                        act.wait_ge(wb_freed, c.at("wb"))
                    nc.scalar.activation(he_hi[:, f % 4, :], he_buf[:, f % 2, :], ACT.Copy).then_inc(he_hi_done, 1)

                steps, loops = steps_of(n_f)
                gu()
                gu()

                def step():
                    gu()
                    gu()
                    c.add("tile")
                    ahead(3)
                step()
                with act.Fori(0, loops) as i:
                    c.enter(i)
                    before = c.get("split"), c.get("he32")
                    for _ in range(4):
                        step()
                    assert c.get("split") - before[0] == LOOP_TILES
                    c.leave(loops)
                    c.add("split", LOOP_TILES * (loops - 1))
                    c.add("he32", (c.get("he32") - before[1]) * (loops - 1))
                for _ in range(1 + 4 * loops, steps):
                    step()
                c.add("tile")

            def attention(n, s_groups, nk, kind, scale, o_at=None, evac=None, chunks=None):
                def e(i):
                    ahead()
                    c.add("max")
                    act.wait_ge(max_ready, c.get("max"))
                    c.add("full", s_groups)
                    for g in range(s_groups):
                        b = bank()
                        s = st[:, (s_groups * i + g) % 8, :]
                        w = nk(i)
                        p = PB[:, i % 4, 0:w] if s_groups == 1 else PB[:, 2 * (i % 2) + g, 0:w]
                        if kind == "sink":
                            nc.scalar.activation(s[:, 2:3], bc[:, B_SINK + i % 8:B_SINK + i % 8 + 1], ACT.Exp, bias=s[:, 0:1])
                            ins = nc.scalar.activation(p, p, ACT.Exp, bias=s[:, 0:1], accum_out=s[:, 1:2])
                        else:
                            ins = nc.scalar.activation(p, b[:, 0:w], ACT.Exp, bias=s[:, 0:1], scale=scale, accum_out=s[:, 1:2])
                    ins.then_inc(exp_done, 1)

                def copy_t(i):
                    ahead()
                    c.add("t")
                    act.wait_ge(t_full, c.get("t"))
                    b = PS[:, 1 + 2 * ((c.get("t") - 1) % 2), :]
                    k = chunks(i)
                    if kind in ("cross", "gqa"):
                        h, t = divmod(i, 2)
                        dst = PT[:, h % 2, 0:k, t * P:(t + 1) * P]
                    else:
                        dst = PT[:, i % 2, 0:k, 0:P]
                    nc.scalar.activation(dst, b[:, 0:k * P].rearrange("p (k q) -> p k q", k=k), ACT.Copy).then_inc(t_freed, 1)

                for it in range(n + 3):
                    if s_groups == 2 and 0 <= it - 2 < n:
                        copy_t(it - 2)
                    if it < n:
                        e(it)
                    if s_groups == 1 and 0 <= it - 2 < n:
                        copy_t(it - 2)
                    if 0 <= it - 3 < n and o_at and o_at(it - 3):
                        c.add("o")
                        act.wait_ge(o_full, c.get("o"))
                        hi_of(*evac(it - 3))

            def experts_gathered(layer):
                g, q = gs[layer], Count(PAIR)
                for name in PAIR:
                    q.add(name, 0)

                def slots():
                    p = q.get("slots") % 2
                    q.add("slots")
                    ahead()
                    act.wait_ge(g["x_full"], q.at("slots"))
                    nc.scalar.activation(xe[p][:, :, 0:SLOTS], PS[:, 6, :].rearrange("p (k s) -> p k s", k=KC), ACT.Copy)\
                        .then_inc(g["x_hi"], 1)
                    act.wait_ge(g["map_full"], q.at("slots"))
                    nc.scalar.activation(st[:, p, 0:1], PS[:, 7, TOK:TOK + 1], ACT.Copy)
                    nc.scalar.activation(slot_map[:, p, :], PS[:, 7, 0:TOK], ACT.Copy).then_inc(g["map_ready"], 1)

                def gu():
                    n = q.get("gu")
                    ahead()
                    act.wait_ge(tile_used, c.at("tile", 1))
                    nc.scalar.activation(gu_rows[:, n % 2, :], PS[:, 4 + n % 2, 0:2 * P], ACT.Copy).then_inc(g["gu_copied"], 1)
                    c.add("tile")
                    q.add("gu")

                def hidden():
                    n = q.get("hidden")
                    q.add("hidden")
                    act.wait_ge(g["hidden_full"], q.at("hidden"))
                    nc.scalar.activation(hid_silu[:, n % 2, :], PS[:, 4 + n % 2, 2 * P:2 * P + SLOTS], ACT.Silu)\
                        .then_inc(g["hidden_silu"], 1)

                def outputs():
                    p = q.get("spread") % 2
                    q.add("spread")
                    act.wait_ge(tile_used, c.at("tile"))
                    nc.scalar.activation(o_parts[0].rearrange("p (m n) -> p m n", m=2), PS[:, 6:8, :], ACT.Identity,
                                         scale=st[:, p, 0:1]).then_inc(g["o_hi"], 1)

                def step(m, first=False, last=False):
                    if m % 2 == 0 and not first:
                        outputs()
                    gu()
                    hidden()
                    if m % 2 == 0 and not last:
                        slots()
                    gu()
                    hidden()
                    c.add("tile")
                    q.add("down")
                    ahead(3)

                slots()
                gu()
                gu()
                hidden()
                step(0, first=True)
                steps, loops = steps_of(N_EXP * F_EXPERT // P)
                with act.Fori(0, loops) as i:
                    c.enter(i)
                    q.enter(i)
                    before = c.get("split")
                    for m in range(1, 5):
                        step(m)
                    assert c.get("split") - before == LOOP_TILES
                    c.leave(loops)
                    q.leave(loops)
                    c.add("split", LOOP_TILES * (loops - 1))
                for m in range(1 + 4 * loops, steps):
                    step(m, last=m == steps - 1)
                hidden()
                c.add("tile")
                outputs()
                act.sem_inc(silu_done, N_EXP * F_EXPERT // P)
                act.sem_inc(he_hi_done, N_EXP * F_EXPERT // P)

            def o_bank():
                b = PS[:, 2 * (c.get("y") % 2), :]
                c.add("y")
                return b

            def rms():
                for t in range(NT):
                    stat()
                    nc.scalar.activation(H[:, t, D:2 * D], X[:, t, :], ACT.Square, accum_out=ms[:, t:t + 1]).then_inc(act_step, 1)
                    c.add("own")
                    act.wait_ge(act_step, 1 + c.get("own"))
                    nc.scalar.activation(ms[:, 2 + t:3 + t], ms[:, t:t + 1], ACT.Sqrt, scale=1.0 / D, bias=ms[:, 4:5])\
                        .then_inc(stat_done, 1)

            loads = [(ident[:, :], A["c_ident"]), (colin[C_LAT:C_LAT + 8, :], A["c_2"].rearrange("a (k p) -> (a k) p", p=P)),
                     (colin[C_CTX:C_CTX + 8, :], A["c_ctx_2"].rearrange("(k p) -> k p", p=P)),
                     (colin[C_N1:C_N1 + 16, :], A["norm1_g_2"].rearrange("l (k p) -> (l k) p", p=P)),
                     (colin[C_N2:C_N2 + 16, :], A["norm2_g_2"].rearrange("l (k p) -> (l k) p", p=P)),
                     (colin[C_POOL:C_POOL + 8, :], A["l1_pool_scale"].rearrange("(k p) -> k p", p=P)),
                     (colin[C_SGUB:C_SGUB + 8, :], A["l0_sgu_b"]),
                     (bc[:, B_SINK:B_SINK + 8], rowb(A["l0_sinks"])),
                     (bc[:, B_RBIAS:B_RBIAS + 16], rowb(A["router_bias"])),
                     (bc[:, B_DQ:B_DQ + 64], rowb(A["diff_q_norm_2"][0])),
                     (bc[:, B_DK:B_DK + 64], rowb(A["diff_k_norm_2"][0])),
                     (bc[:, B_SUB:B_SUB + 128], rowb(A["diff_subln_2"][0])),
                     (bc[:, B_GQ:B_GQ + 128], rowb(A["gqa_q_norm_2"][0])),
                     (bc[:, B_GK:B_GK + 128], rowb(A["gqa_k_norm_2"][0])),
                     (bc[:, B_LAM:B_LAM + 64], rowb(A["diff_lambda_q1_2"][0])),
                     (bc[:, B_LAM + 64:B_LAM + 128], rowb(A["diff_lambda_k1_2"][0])),
                     (bc[:, B_LAM + 128:B_LAM + 192], rowb(A["diff_lambda_q2_2"][0])),
                     (bc[:, B_LAM + 192:B_LAM + 256], rowb(A["diff_lambda_k2_2"][0])),
                     (bc[:, B_INVF:B_INVF + 8], rowb(A["c_invf"])),
                     (rw[:, :, :], A["router_w"].rearrange("(k p) n -> p k n", p=P)),
                     (pos_i[:, :], A["positions"][0].rearrange("(t p) -> p t", p=P))]
            bias = A["ada_b_2"].rearrange("l n -> (l n)")
            for layer, rows in enumerate(mod_rows):
                col0 = layer * 6 * D
                for buf, at, n in rows:
                    loads.append((buf[0:2, at:at + n], bias[col0:col0 + n].partition_broadcast(2)))
                    col0 += n
            assert len(loads) == N_SETUP
            for dst, src in loads:
                act.dma_start(dst, src, allow_slow_non_contiguous=True).then_inc(setup_landed, 16)
            act.dma_start(X[:, :, :], A["ctx_2"][0].rearrange("(t p) d -> p t d", p=P)).then_inc(x_landed, 16)
            act.wait_ge(setup_landed, 16 * N_SETUP)
            nc.scalar.activation(rw_hi[:, :, :], rw[:, :, :], ACT.Copy).then_inc(hi_evac, 1)
            c.add("full")
            act.wait_ge(wb_full, 1)
            b = bank()
            nc.scalar.activation(cond[:, :, :], b[:, 0:16].rearrange("p (c k) -> p c k", c=2), ACT.Silu).then_inc(act_step, 1)
            c.add("split", N_MOD)
            c.add("wb", 24)
            def mod_to_dram(layer):
                stat()
                col0 = layer * 6 * D
                for buf, at, n in mod_rows[layer]:
                    act.dma_start(mods_d[:, col0:col0 + n], buf[0:2, at:at + n]).then_inc(mod_out, 16)
                    col0 += n

            def mod_from_dram(layer):
                act.wait_ge(mod_out, (32, 80)[layer])
                for cnd in range(2):
                    act.dma_start(mod_staged[layer][48 * cnd:48 * cnd + 48, :], mods_rows[layer, cnd]).then_inc(mod_in, 16)

            tiles(N_MOD // 2)
            mod_to_dram(0)
            mod_from_dram(0)
            tiles(4)
            rms()
            tiles(N_MOD // 2 - 4)
            mod_to_dram(1)
            plain(1)
            stat()
            nc.scalar.activation(lam[:, 0:2], lam[:, 0:2], ACT.Exp).then_inc(stat_done, 1)
            mod_from_dram(1)

            def heads(n):
                root(hs[:, 1, 0:n])

            def diff(path):
                nk = TOK * (1 + path)
                if path:
                    act.dma_start(KT[:, :, 0:TOK], kd_d).then_inc(kv_in, 16)
                    act.dma_start(V[:, 0:2, :], vd_d).then_inc(kv_in, 16)
                    act.dma_start(TAB[:, 0:256].rearrange("p (t c) -> p t c", t=NT),
                                  A["c_ax64"].rearrange("(t p) c -> p t c", p=P)).then_inc(tab_landed, 16)
                    rms()
                to_at(True)
                prm()
                tiles(8)
                for t in range(NT):
                    heads(32)
                tiles(4)
                plain(8)
                if not path:
                    ahead()
                    c.add("stat")
                    act.wait_ge(stat_ready, c.get("stat"))
                    act.dma_start(kd_d, KT[:, :, 0:TOK]).then_inc(kv_out, 16)
                    act.dma_start(vd_d, V[:, 0:2, :]).then_inc(kv_out, 16)
                attention(16, 2, lambda i: nk, "diff", 64 ** -0.5, chunks=lambda i: nk // P)
                c.add("y", 4)
                c.add("o", 4)
                for t in range(NT):
                    heads(8)
                to_at()
                c.add("y", 2)
                tiles(4)
                rms()
                prm()
                to_at(True)
                c.add("y", 2)
                gated(F_FFN // P, False)

            c.add("y", 6)
            diff(0)
            plain(1)
            rms()
            to_at(True)
            c.add("y", 1)
            tiles(2)
            for t in range(NT):
                heads(2)
                plain(1)
            ahead()
            c.add("stat")
            act.wait_ge(stat_ready, c.get("stat"))
            act.dma_start(kg_d, KT[:, 0:2, 0:TOK]).then_inc(kv_out, 16)
            act.dma_start(vg_d, V[:, 0:2, 0:TOK]).then_inc(kv_out, 16)
            act.wait_ge(kv_out, 64)
            act.dma_start(X[:, :, :], A["x"][0].rearrange("(t p) d -> p t d", p=P)).then_inc(x_landed, 16)
            act.dma_start(TAB[:, :], A["c_masks"]).then_inc(tab_landed, 16)
            for q in range(4):
                act.dma_start(sgu_raw[:, 2 * q:2 * q + 2, :], A["l0_sgu_w"][2 * q:2 * q + 2].rearrange("g t s -> t g s"))\
                    .then_inc(tab_landed, 16)

            def norm():
                for _ in range(NT):
                    root(mv[:, 0:1])

            for layer in range(2):
                to_at()
                if layer == 0:
                    prm()
                    c.add("y", 4)
                    stat()
                    nc.scalar.activation(trig[:, 2:4, :, :], trig[:, 2:4, :, :], ACT.Sin).then_inc(stat_done, 1)
                    tiles(7)
                    for t in range(NT):
                        stat()
                        nc.scalar.activation(H[:, t, 768:1792], H[:, t, 768:1792], ACT.Gelu_apprx_tanh).then_inc(stat_done, 1)
                    plain(2)
                    plain(4)
                    attention(16, 1, lambda i: (i // 8 + 1) * P, "sink", 1.0,
                              o_at=lambda i: i % 8 == 7, chunks=lambda i: i // 8 + 1,
                              evac=lambda i: (at_hi[:, 0:4, (i // 8) * P:(i // 8 + 1) * P],
                                              o_bank().rearrange("p (k q) -> p k q", k=4)))
                    for t in range(NT):
                        root(hs[:, 1, 0:8])
                    plain(2)
                    for t in range(NT):
                        full()
                        hi_of(at_hi[:, 4:8, t * P:(t + 1) * P], bank().rearrange("p (k q) -> p k q", k=4))
                else:
                    c.add("y", 2)
                    act.dma_start(V[:, 0:2, :], A["c_band"]).then_inc(tab_landed, 16)
                    tiles(4)
                    for j2 in range(4):
                        full()
                        hi_of(at_hi[:, 2 * j2:2 * j2 + 2, :], bank().rearrange("p (k t) -> p k t", k=2))
                    tiles(1)
                    for g in range(4):
                        ahead()
                        c.add("aff")
                        act.wait_ge(aff_ready, c.get("aff"))
                        bank()
                        hi_of(at_hi[:, 2 * g:2 * g + 2, :], PBf[:, 0:512].rearrange("p (k t) -> p k t", k=2))
                act.dma_start(H[:, :, 0:D], A["mem"][0].rearrange("(t p) d -> p t d", p=P)).then_inc(x_landed, 16)
                prm()
                c.add("y", 2)
                tiles(4)
                to_at()
                norm()
                c.add("wb", 4)
                c.add("y", 2)
                tiles(8)
                to_at()
                c.add("wb", 4)
                tiles(4)
                prm()
                attention(8, 1, lambda i: TOK, "cross", 256 ** -0.5, o_at=lambda i: i % 2 == 1, chunks=lambda i: 2,
                          evac=lambda i: (at_hi[:, 2 * (i // 2):2 * (i // 2) + 2, :], o_bank().rearrange("p (k q) -> p k q", k=2)))
                c.add("y", 2)
                tiles(4)
                norm()
                prm()
                to_at()
                plain(2)
                stat()
                nc.scalar.activation(rt[:, 1, :, :], rt[:, 1, :, :], ACT.Exp).then_inc(stat_done, 1)
                plain(1)
                act.wait_ge(route_ready, layer + 1)
                most = act.value_load(route[0:1, 0:1], min_val=0, max_val=TOK)
                with act.If(most <= SLOTS):
                    before = dict(c.n)
                    experts_gathered(layer)
                    split_to = c.get("split")
                    c.n = before
                with act.Else():
                    plain(8)
                    c.add("y", 2)
                    gated(N_EXP * F_EXPERT // P, True)
                    while c.get("split") < split_to:
                        split()
                assert c.get("split") == split_to
                norm()

            diff(1)
            act.dma_start(KT[:, 0:2, 0:TOK], kg_d).then_inc(kv_in, 16)
            act.dma_start(V[:, 0:2, 0:TOK], vg_d).then_inc(kv_in, 16)
            act.dma_start(TAB[:, :].rearrange("p (t c) -> p t c", t=NT),
                          A["c_ax128"].rearrange("(t p) c -> p t c", p=P)).then_inc(tab_landed, 16)
            rms()
            to_at(True)
            c.add("y", 3)
            prm()
            tiles(6)
            for t in range(NT):
                heads(10)
                plain(3)
            attention(16, 1, lambda i: 512, "gqa", 128 ** -0.5, o_at=lambda i: i % 4 == 3, chunks=lambda i: 4,
                      evac=lambda i: (at_hi[:, 2 * (i // 4):2 * (i // 4) + 2, :], o_bank().rearrange("p (k q) -> p k q", k=2)))
            c.add("y", 2)
            tiles(4)
            rms()
            prm()
            to_at(True)
            c.add("y", 2)
            gated(F_FFN // P, False)

        @block.vector
        def _(dve):
            c = Count()

            def D1(ins):
                ins.then_inc(dve_step, 1)
                c.add("step")
                dve.wait_ge(dve_step, c.get("step"))

            def freed(ins):
                ins.then_inc(wb_freed, 1)
                dve.wait_ge(wb_freed, c.at("wb"))

            def y_done(ins):
                ins.then_inc(y_freed, 1)
                c.add("y")
                dve.wait_ge(y_freed, c.get("y"))

            def full():
                c.add("full")
                dve.wait_ge(wb_full, c.get("full"))

            def bank():
                b = PS[:, 4 + c.get("wb") % 4, :]
                c.add("wb")
                return b

            def hi_wait():
                c.add("hi")
                dve.wait_ge(hi_evac, c.get("hi"))

            def lo_of(dst, src, hi):
                return dve.tensor_tensor(dst, src, hi.bitcast(F32), ALU.subtract)

            def done():
                c.add("done")
                dve.wait_ge(stat_done, c.get("done"))

            def lo_tile(n):
                assert by_vector(n)
                value = n + 1 - N_MOD
                dve.wait_ge(hi_done, value if c.i is None else c.i * LOOP_TILES + value)
                lo_of(w_lo[:, n % RING, :], raw[:, n % RAW, :], w_hi[:, n % RING, :]).then_inc(lo_done_v, 1)

            def lo_tiles(m, steps):
                if m % 2 == 0:
                    lo_tile(c.get("tile") + 1)
                if m + 1 < steps:
                    lo_tile(c.get("tile") + (3 if m % 2 == 0 else 2))

            def ask(ins):
                ins.then_inc(stat_ready, 1)
                c.add("ask")
                dve.wait_ge(stat_ready, c.get("ask"))

            def ready(ins):
                ins.then_inc(src_ready, 1)
                c.add("src")
                dve.wait_ge(src_ready, c.get("src"))

            def tiles(n):
                c.add("tile", n)
                dve.wait_ge(tile_used, c.get("tile"))

            def ybank(pair, t):
                return PS[:, 2 * (pair % 2) + t, :]

            def to_at(A8=None, B8=None):
                quarters = [(t, h) for t in range(NT) for h in range(2)]
                freed_before = c.get("wb")
                banks = []

                def scale(j):
                    h = quarters[j][1]
                    full()
                    banks.append(bank().rearrange("p (k t) -> p k t", k=4))
                    if A8 is not None:
                        tmp = PBf[:, j % 2 * 512:(j % 2 + 1) * 512].rearrange("p (k t) -> p k t", k=4)
                        for i in range(4):
                            k = 4 * h + i
                            ins = dve.tensor_scalar(tmp[:, i, :], banks[j][:, i, :], A8[:, k:k + 1], B8[:, k:k + 1],
                                                    ALU.mult, ALU.add)
                        ins.then_inc(aff_ready, 1)
                        c.add("aff")
                        banks[j] = tmp

                def lo(j):
                    t, h = quarters[j]
                    sl = (slice(None), slice(4 * h, 4 * h + 4), slice(t * P, (t + 1) * P))
                    hi_wait()
                    lo_of(at_lo[sl], banks[j], at_hi[sl]).then_inc(wb_freed, 1)
                    dve.wait_ge(wb_freed, freed_before + j + 1)

                for j in range(len(quarters) + 1):
                    if j < len(quarters):
                        scale(j)
                    if j:
                        lo(j - 1)

            def mean_var(t):
                for h in range(2):
                    D1(dve.bn_stats(bn[:, h, :], X[:, t, h * 512:(h + 1) * 512]))
                D1(dve.bn_aggr(mv[:, :], bn[:, :, :]))

            def prm_wait():
                n = c.get("prm")
                need = sum(sum(len(s) if isinstance(s, tuple) else 1 for _, s in prm_loads[j]) for j in range(n + 1))
                dve.wait_ge(prm_landed, 16 * need)
                c.add("prm")

            def layer_norm_tiles(signal=True):
                prm_wait()
                for t in range(NT):
                    mean_var(t)
                    D1(dve.tensor_copy(hs[:, 0, 0:1], mv[:, 0:1]))
                    ask(dve.tensor_scalar(mv[:, 0:1], mv[:, 1:2], LN_EPS, None, ALU.add))
                    done()
                    D1(dve.reciprocal(mv[:, 1:2], mv[:, 0:1]))
                    D1(dve.tensor_scalar(X[:, t, :], X[:, t, :], hs[:, 0, 0:1], mv[:, 1:2], ALU.subtract, ALU.mult))
                    D1(dve.tensor_tensor(X[:, t, :], X[:, t, :], PRM[:, 0, :], ALU.mult))
                    (ready if signal else D1)(dve.tensor_tensor(X[:, t, :], X[:, t, :], PRM[:, 1, :], ALU.add))
                if signal:
                    dve.wait_ge(src_ready, c.get("src"))
                dve.tensor_copy(mv[:, 0:1], mv[:, 1:2]).then_inc(prm_used, 1)

            def residual_add(per_pair):
                for p in range(2):
                    pair = c.get("y")
                    if per_pair:
                        tiles(per_pair)
                    for t in range(NT):
                        x = X[:, t, p * 512:(p + 1) * 512]
                        ins = dve.scalar_tensor_tensor(x, x, ALPHA, ybank(pair, t), ALU.mult, ALU.add)
                        if t == NT - 1:
                            ins.then_inc(y_freed, 1)
                        else:
                            ins.then_inc(dve_step, 1)
                            c.add("step")
                    c.add("y")
                settled()

            def residual_gate(per_pair, to_rms=True):
                prm_wait()
                order = [(p, t) for p in range(2) for t in range(NT)] if per_pair else [(p, t) for t in range(NT) for p in range(2)]
                first, gated_by, last_of_pair = c.get("y"), {}, {p: max(j for j, o in enumerate(order) if o[0] == p) for p in range(2)}
                seen = set()
                for j in range(len(order) + 1):
                    if j < len(order):
                        p, t = order[j]
                        if per_pair and p not in seen:
                            tiles(per_pair)
                            seen.add(p)
                        ins = dve.tensor_tensor(PBf[:, j * 512:(j + 1) * 512], ybank(first + p, t),
                                                PRM[:, 0, p * 512:(p + 1) * 512], ALU.mult)
                        if j == last_of_pair[p]:
                            ins.then_inc(y_freed, 1)
                            c.add("y")
                            gated_by[j] = (y_freed, c.get("y"))
                        else:
                            ins.then_inc(dve_step, 1)
                            c.add("step")
                            gated_by[j] = (dve_step, c.get("step"))
                    if j:
                        p, t = order[j - 1]
                        dve.wait_ge(*gated_by[j - 1])
                        x = X[:, t, p * 512:(p + 1) * 512]
                        ins = dve.tensor_tensor(x, x, PBf[:, (j - 1) * 512:j * 512], ALU.add)
                        if p == 1 and to_rms:
                            ins.then_inc(stat_ready, 1)
                            c.add("ask")
                        else:
                            ins.then_inc(dve_step, 1)
                            c.add("step")
                settled()
                dve.tensor_copy(mv[:, 0:1], mv[:, 1:2]).then_inc(prm_used, 1)

            def rms_to_h(asked=False):
                if not asked:
                    for _ in range(NT):
                        ask(dve.tensor_copy(hs[:, 0, 0:1], hs[:, 0, 0:1]))
                for t in range(NT):
                    done()
                    D1(dve.reciprocal(mv[:, 1:2], ms[:, 2 + t:3 + t]))
                    ready(dve.tensor_scalar(H[:, t, 0:D], X[:, t, :], mv[:, 1:2], None, ALU.mult))

            def affine_of(cnd, layer, norm):
                first = cnd * 48 + (0 if norm == 0 else 24)
                g0 = (C_N1 if norm == 0 else C_N2) + 8 * layer
                D1(dve.tensor_scalar(affA[:, :], modcol[:, layer, first + 8:first + 16], 1.0, None, ALU.add))
                D1(dve.tensor_tensor(affA[:, :], affA[:, :], col[:, g0:g0 + 8], ALU.mult))
                return affA, modcol[:, layer, first:first + 8]

            def y_to(dsts, width=512, per=2):
                pair = c.get("y")
                tiles(per)
                for t in range(NT):
                    ins = dve.tensor_copy(dsts[t], ybank(pair, t)[:, 0:width])
                    if t == NT - 1:
                        ins.then_inc(y_freed, 1)
                    else:
                        ins.then_inc(dve_step, 1)
                        c.add("step")
                c.add("y")

            def settled():
                dve.wait_ge(dve_step, c.get("step"))
                dve.wait_ge(stat_ready, c.get("ask"))
                dve.wait_ge(y_freed, c.get("y"))

            def head_norm(t, n, dh, at, eps):
                v = H[:, t, at:at + n * dh].rearrange("p (h d) -> p h d", h=n)
                sq = PBf[:, 0:n * dh].rearrange("p (h d) -> p h d", h=n)
                D1(dve.tensor_tensor(sq, v, v, ALU.mult))
                D1(dve.tensor_reduce(hs[:, 0, 0:n], sq, AXX, ALU.add))
                ask(dve.tensor_scalar(hs[:, 1, 0:n], hs[:, 0, 0:n], 1.0 / dh, eps, ALU.mult, ALU.add))
                done()
                D1(dve.reciprocal(hs[:, 2, 0:n], hs[:, 1, 0:n]))
                D1(dve.tensor_tensor(v, v, hs[:, 2, 0:n].unsqueeze(2).to_broadcast([P, n, dh]), ALU.mult))

            def head_gain(t, n, dh, at, gain):
                v = H[:, t, at:at + n * dh].rearrange("p (h d) -> p h d", h=n)
                ins = dve.tensor_tensor(v, v, bc[:, gain:gain + dh].unsqueeze(1).to_broadcast([P, n, dh]), ALU.mult)
                D1(ins)

            def axial(t, n, dh):
                q = dh // 4
                tab = TAB[:, 0:NT * 2 * dh].rearrange("p (t c) -> p t c", t=NT)[:, t, :]
                v = H[:, t, 0:n * dh].rearrange("p (h d) -> p h d", h=n)
                v4 = H[:, t, 0:n * dh].rearrange("p (h a b q) -> p h a b q", h=n, a=2, b=2)
                r4 = PBf[:, 0:n * dh].rearrange("p (h a b q) -> p h a b q", h=n, a=2, b=2)
                s4 = tab[:, dh:2 * dh].rearrange("p (a b q) -> p a b q", a=2, b=2)
                for b in range(2):
                    D1(dve.tensor_tensor(r4[:, :, :, b, :], v4[:, :, :, 1 - b, :],
                                         s4[:, :, b, :].unsqueeze(1).to_broadcast([P, n, 2, q]), ALU.mult))
                D1(dve.tensor_tensor(v, v, tab[:, 0:dh].unsqueeze(1).to_broadcast([P, n, dh]), ALU.mult))
                return dve.tensor_tensor(v, v, PBf[:, 0:n * dh].rearrange("p (h d) -> p h d", h=n), ALU.add)

            def cols_out(dst):
                full()
                b = bank()
                n = dst.shape[1] if len(dst.shape) == 3 else 1
                freed(dve.tensor_copy(dst, b[:, 0:n * P].rearrange("p (k t) -> p k t", k=n)))

            def gated(n_f, moe):
                def gu(e):
                    dve.wait_ge(tile_used, c.at("tile", 1))
                    c.add("tile")
                    f = c.get("gu")
                    c.add("gu")
                    dve.wait_ge(silu_done, c.at("gu"))
                    b = bank()
                    h = he_buf[:, f % 2, :]
                    freed(dve.tensor_tensor(h, silu_buf[:, f % 2, :], b[:, TOK:2 * TOK], ALU.mult))
                    if moe:
                        dve.tensor_tensor(h, h, cbc[:, e, :], ALU.mult).then_inc(he_f32, 1)
                        c.add("he32")
                        v = c.get("he32")
                        dve.wait_ge(he_f32, v if c.i is None else c.i * 8 + v)
                    dve.wait_ge(he_hi_done, c.at("gu"))
                    lo_of(he_lo[:, f % 4, :], h, he_hi[:, f % 4, :]).then_inc(he_ready, 1)

                steps, loops = steps_of(n_f)

                def step(i, m):
                    for f in (2 * m + 2, 2 * m + 3):
                        gu(i * 2 + f // 4 if moe else 0)
                        if moe and f % 2 == 0:
                            lo_tiles(m, steps)
                    c.add("tile")
                if moe:
                    lo_tile(c.get("tile") + 2)
                gu(0)
                gu(0)
                step(0, 0)
                with dve.Fori(0, loops) as i:
                    c.enter(i)
                    before = c.get("he32")
                    for m in range(1, 5):
                        step(i, m)
                    c.leave(loops)
                    c.add("he32", (c.get("he32") - before) * (loops - 1))
                for m in range(1 + 4 * loops, steps):
                    step(0, m)
                c.add("tile")
                dve.wait_ge(tile_used, c.get("tile"))

            def attention(n, s_groups, nk, kind, scale, o_at, o_evac):
                t0 = c.get("t")

                def m(i):
                    w = nk(i)
                    for g in range(s_groups):
                        full()
                        b = bank()
                        s = st[:, (s_groups * i + g) % 8, :]
                        if kind == "sink":
                            t, h = divmod(i, 8)
                            p = PB[:, i % 4, 0:w]
                            if i >= 4:
                                dve.wait_ge(t_freed, t0 + i - 3)
                            dve.scalar_tensor_tensor(p, b[:, 0:w], 0.125, TAB[:, 256 - w:256], ALU.mult, ALU.add)\
                                .then_inc(wb_freed, 1)
                            dve.wait_ge(wb_freed, c.get("wb"))
                            D1(dve.tensor_reduce(s[:, 3:4], p, AXX, ALU.max))
                            ins = dve.tensor_scalar(s[:, 0:1], s[:, 3:4], bc[:, B_SINK + h:B_SINK + h + 1], -1.0, ALU.max, ALU.mult)
                        else:
                            D1(dve.tensor_reduce(s[:, 3:4], b[:, 0:w], AXX, ALU.max))
                            ins = dve.tensor_scalar(s[:, 0:1], s[:, 3:4], -scale, None, ALU.mult)
                    ins.then_inc(max_ready, 1)

                def norm(i):
                    c.add("exp")
                    dve.wait_ge(exp_done, c.get("exp"))
                    w = nk(i)
                    if kind == "diff":
                        s0, s1 = st[:, (2 * i) % 8, :], st[:, (2 * i + 1) % 8, :]
                        p0, p1 = PB[:, 2 * (i % 2), 0:w], PB[:, 2 * (i % 2) + 1, 0:w]
                        dve.reciprocal(s0[:, 3:4], s0[:, 1:2]).then_inc(wb_freed, 1)
                        dve.reciprocal(s1[:, 2:3], s1[:, 1:2]).then_inc(wb_freed, 1)
                        dve.wait_ge(wb_freed, c.get("wbn") + 2)
                        c.add("wbn", 2)
                        D1(dve.tensor_scalar(p1, p1, s1[:, 2:3], lam[:, 2:3], ALU.mult, ALU.mult))
                        dve.scalar_tensor_tensor(p0, p0, s0[:, 3:4], p1, ALU.mult, ALU.add).then_inc(p_ready, 1)
                        return
                    s = st[:, i % 8, :]
                    p = PB[:, i % 4, 0:w]
                    if kind == "sink":
                        D1(dve.tensor_tensor(s[:, 1:2], s[:, 1:2], s[:, 2:3], ALU.add))
                        D1(dve.reciprocal(s[:, 3:4], s[:, 1:2]))
                    else:
                        dve.reciprocal(s[:, 3:4], s[:, 1:2]).then_inc(wb_freed, 1)
                        c.add("wbn")
                        dve.wait_ge(wb_freed, c.get("wbn"))
                    dve.tensor_scalar(p, p, s[:, 3:4], None, ALU.mult).then_inc(p_ready, 1)

                c.n["wbn"] = c.get("wb")
                for it in range(n + 3):
                    if it < n:
                        m(it)
                    if 0 <= it - 1 < n:
                        norm(it - 1)
                    if 0 <= it - 3 < n and o_at(it - 3):
                        o_evac(it - 3)
                c.add("t", n)

            def o_split(dst_hi, dst_lo, k):
                b = ybank(c.get("y"), 0).rearrange("p (k q) -> p k q", k=k)
                hi_wait()
                c.add("o")
                y_done(lo_of(dst_lo, b, dst_hi))

            for small in (hs[:, :, :], mv[:, :], lam[:, :]):
                D1(dve.memset(small, 0.0))
            D1(dve.memset(ms[:, 4:5], RMS_EPS))
            dve.wait_ge(setup_landed, 16 * N_SETUP)
            full()
            hi_wait()
            D1(lo_of(rw_lo[:, :, :], rw[:, :, :], rw_hi[:, :, :]))
            dve.wait_ge(act_step, 1)
            freed(dve.tensor_copy(col[:, :], bank()[:, 0:C_ROWS]))
            def mod_cols(layer):
                full()
                freed(dve.tensor_copy(modcol[:, layer, :], bank()[:, 0:96]))
                dve.wait_ge(wb_freed, c.get("wb"))

            for j, group in enumerate(mod_groups):
                tiles(2)
                freed(dve.tensor_tensor(group, group, bank()[0:2, :], ALU.add))
                if j % 12 == 11:
                    ask(dve.tensor_copy(hs[:, 0, 0:1], hs[:, 0, 0:1]))
                if j == 13:
                    dve.wait_ge(x_landed, 16)
                    rms_to_h()
                if j == MOD_COLS_AT:
                    mod_cols(0)
            for j in range(2):
                l0 = B_LAM + 128 * j
                D1(dve.tensor_tensor(bc[:, l0:l0 + 64], bc[:, l0:l0 + 64], bc[:, l0 + 64:l0 + 128], ALU.mult))
                D1(dve.tensor_reduce(lam[:, j:j + 1], bc[:, l0:l0 + 64], AXX, ALU.add))
            ask(dve.tensor_scalar(lam[:, 3:4], lam[:, 0:1], 1.0, None, ALU.mult))
            done()
            D1(dve.tensor_tensor(lam[:, 2:3], lam[:, 1:2], lam[:, 0:1], ALU.subtract))
            D1(dve.tensor_scalar(lam[:, 2:3], lam[:, 2:3], -LAMBDA_INIT, None, ALU.add))
            D1(dve.tensor_scalar(bc[:, B_SUB:B_SUB + 128], bc[:, B_SUB:B_SUB + 128], 1.0 - LAMBDA_INIT, None, ALU.mult))

            def diff(path):
                nk = TOK * (1 + path)
                a, b8 = affine_of(1 - path, 0, 0)
                if path:
                    rms_to_h()
                to_at(a, b8)
                for n in range(4):
                    y_to([H[:, t, n * 512:(n + 1) * 512] for t in range(NT)])
                settled()
                if path:
                    dve.wait_ge(tab_landed, 16 * 7)
                for t in range(NT):
                    head_norm(t, 32, 64, 0, RMS_EPS)
                    head_gain(t, 16, 64, 0, B_DQ)
                    v = H[:, t, D:2 * D].rearrange("p (h d) -> p h d", h=16)
                    g = bc[:, B_DK:B_DK + 64].unsqueeze(1).to_broadcast([P, 16, 64])
                    if path:
                        D1(dve.tensor_tensor(v, v, g, ALU.mult))
                        ready(axial(t, 32, 64))
                    else:
                        ready(dve.tensor_tensor(v, v, g, ALU.mult))
                for n in range(2):
                    y_to([V[:, 2 * path + u, n * 512:(n + 1) * 512] for u in range(NT)])
                settled()
                for t in range(NT):
                    for j in range(4):
                        if j < 2:
                            cols_out(QT[:, 4 * j:4 * j + 4, t * P:(t + 1) * P])
                        else:
                            k0 = path * TOK + t * P
                            cols_out(KT[:, 4 * j - 8:4 * j - 4, k0:k0 + P])
                dve.wait_ge(wb_freed, c.get("wb"))
                if not path:
                    ask(dve.tensor_copy(hs[:, 0, 0:1], hs[:, 0, 0:1]))

                def o_evac(i):
                    c.add("o")
                    dve.wait_ge(o_full, c.get("o"))
                    t, h = divmod(i, 8)
                    y_done(dve.tensor_copy(H[:, t, (h // 4) * 512:(h // 4 + 1) * 512], ybank(c.get("y"), 0)))
                attention(16, 2, lambda i: nk, "diff", 64 ** -0.5, lambda i: i % 4 == 3, o_evac)
                dve.wait_ge(y_freed, c.get("y"))
                for t in range(NT):
                    head_norm(t, 8, P, 0, RMS_EPS)
                    v = H[:, t, 0:D].rearrange("p (h d) -> p h d", h=8)
                    ready(dve.tensor_tensor(v, v, bc[:, B_SUB:B_SUB + P].unsqueeze(1).to_broadcast([P, 8, P]), ALU.mult))
                to_at()
                residual_gate(2)
                a, b8 = affine_of(1 - path, 0, 1)
                rms_to_h(asked=True)
                to_at(a, b8)
                gated(F_FFN // P, False)
                residual_gate(0)

            diff(0)
            mod_cols(1)
            a, b8 = affine_of(1, 1, 0)
            rms_to_h(asked=True)
            to_at(a, b8)
            y_to_split = c.get("y")
            tiles(2)
            for t in range(NT):
                D1(dve.tensor_copy(H[:, t, 0:256], ybank(y_to_split, t)[:, 0:256]))
                ins = dve.tensor_copy(V[:, t, 0:256], ybank(y_to_split, t)[:, 256:512])
                if t == NT - 1:
                    ins.then_inc(y_freed, 1)
                else:
                    D1(ins)
            c.add("y")
            for t in range(NT):
                head_norm(t, 2, P, 0, RMS_EPS)
                v = H[:, t, 0:256].rearrange("p (h d) -> p h d", h=2)
                ready(dve.tensor_tensor(v, v, bc[:, B_GK:B_GK + P].unsqueeze(1).to_broadcast([P, 2, P]), ALU.mult))
            for t in range(NT):
                cols_out(KT[:, 0:2, t * P:(t + 1) * P])
            dve.wait_ge(wb_freed, c.get("wb"))
            dve.wait_ge(y_freed, c.get("y"))
            ask(dve.tensor_copy(hs[:, 0, 0:1], hs[:, 0, 0:1]))

            def cross(layer):
                dve.wait_ge(x_landed, 16 * (3 + layer))
                for _ in range(NT):
                    ready(dve.tensor_copy(hs[:, 0, 0:1], hs[:, 0, 0:1]))
                residual_add(2)
                to_at()
                layer_norm_tiles()
                for j in range(4):
                    tiles(1)
                    freed(dve.tensor_copy(KT[:, 2 * j:2 * j + 2, 0:TOK], bank().rearrange("p (k t) -> p k t", k=2)))
                for n in range(2):
                    y_to([V[:, t, n * 512:(n + 1) * 512] for t in range(NT)])
                to_at()
                for j in range(4):
                    tiles(1)
                    freed(dve.tensor_copy(QT[:, 2 * j:2 * j + 2, :], bank().rearrange("p (k t) -> p k t", k=2)))
                settled()

                def o_evac(i):
                    h = i // 2
                    o_split(at_hi[:, 2 * h:2 * h + 2, :], at_lo[:, 2 * h:2 * h + 2, :], 2)
                attention(8, 1, lambda i: TOK, "cross", 256 ** -0.5, lambda i: i % 2 == 1, o_evac)
                residual_add(2)
                layer_norm_tiles()

            def top2(v, n, rank, cmp):
                D1(dve.memset(rank, 0.0))
                for i in range(n):
                    if i + 1 < n:
                        w = n - 1 - i
                        D1(dve.tensor_tensor(cmp[:, :, 0:w], v[:, :, i:i + 1].to_broadcast([P, v.shape[1], w]), v[:, :, i + 1:n], ALU.is_ge))
                        D1(dve.tensor_tensor(rank[:, :, i + 1:n], rank[:, :, i + 1:n], cmp[:, :, 0:w], ALU.add))
                    if i:
                        D1(dve.tensor_tensor(cmp[:, :, 0:i], v[:, :, i:i + 1].to_broadcast([P, v.shape[1], i]), v[:, :, 0:i], ALU.is_gt))
                        D1(dve.tensor_tensor(rank[:, :, 0:i], rank[:, :, 0:i], cmp[:, :, 0:i], ALU.add))

            def router():
                full()
                freed(dve.tensor_copy(PBf[0:N_EXP, 0:TOK], bank()[0:N_EXP, 0:TOK]))
                ready(dve.tensor_copy(hs[:, 0, 0:1], hs[:, 0, 0:1]))
                full()
                b = bank()[:, 0:NT * N_EXP].rearrange("p (t e) -> p t e", t=NT)

                def R(j):
                    return rt[:, j, :, :]

                def small(j, k=0):
                    return rt[:, j, :, k:k + 1]
                D1(dve.tensor_reduce(small(0), b, AXX, ALU.max))
                freed(dve.tensor_tensor(R(1), b, small(0).to_broadcast([P, NT, N_EXP]), ALU.subtract))
                dve.wait_ge(wb_freed, c.get("wb"))
                ask(dve.tensor_copy(hs[:, 0, 0:1], hs[:, 0, 0:1]))
                done()
                D1(dve.tensor_reduce(small(0), R(1), AXX, ALU.add))
                D1(dve.reciprocal(small(0, 1), small(0)))
                D1(dve.tensor_tensor(R(1), R(1), small(0, 1).to_broadcast([P, NT, N_EXP]), ALU.mult))
                D1(dve.tensor_tensor(R(2), R(1), bc[:, B_RBIAS:B_RBIAS + N_EXP].unsqueeze(1).to_broadcast([P, NT, N_EXP]), ALU.add))
                v = R(2).rearrange("p t (g e) -> p (t g) e", e=4)
                rank = R(3).rearrange("p t (g e) -> p (t g) e", e=4)
                top2(v, 4, rank, R(4).rearrange("p t (g e) -> p (t g) e", e=4))
                D1(dve.tensor_scalar(R(3), R(3), 2.0, None, ALU.is_lt))
                D1(dve.tensor_tensor(R(4), R(2), R(3), ALU.mult))
                gs = rt[:, 5, :, 0:4]
                D1(dve.tensor_reduce(gs, R(4).rearrange("p t (g e) -> p t g e", e=4), AXX, ALU.add))
                grank = rt[:, 6, :, 0:4]
                top2(gs, 4, grank, rt[:, 7, :, 0:4])
                D1(dve.tensor_scalar(grank, grank, 1.0, None, ALU.is_lt))
                D1(dve.tensor_tensor(rank.rearrange("p (t g) e -> p t g e", t=NT), rank.rearrange("p (t g) e -> p t g e", t=NT),
                                     grank.unsqueeze(3).to_broadcast([P, NT, 4, 4]), ALU.mult))
                D1(dve.tensor_tensor(R(4), R(1), R(3), ALU.mult))
                D1(dve.tensor_reduce(small(0), R(4), AXX, ALU.add))
                D1(dve.reciprocal(small(0, 1), small(0)))
                ready(dve.tensor_tensor(R(11), R(4), small(0, 1).to_broadcast([P, NT, N_EXP]), ALU.mult))
                full()
                b = bank()
                D1(dve.tensor_tensor(R(9), b[:, 0:NT * N_EXP].rearrange("p (t e) -> p t e", t=NT), R(3), ALU.mult))
                freed(dve.tensor_reduce(rt[:, 0, 0, 0:1], b[:, NT * N_EXP:(NT + 1) * N_EXP], AXX, ALU.max))
                dve.wait_ge(wb_freed, c.get("wb"))
                D1(dve.tensor_scalar(R(9), R(9), -1.0, None, ALU.add))
                dve.tensor_copy(route[0:1, 0:1], rt[0:1, 0, 0, 0:1]).then_inc(route_ready, 1)

            def experts_gathered(layer):
                g, q = gs[layer], Count(PAIR)
                for name in PAIR:
                    q.add(name, 0)
                steps, loops = steps_of(N_EXP * F_EXPERT // P)
                own = dict(n=0)

                def chain(ins):
                    own["n"] += 1
                    ins.then_inc(g["own"], 1)
                    dve.wait_ge(g["own"], own["n"] if q.i is None else q.i * own["stride"] + own["n"])

                def made(e):
                    p = q.get("made") % 2
                    q.add("made")
                    chain(dve.tensor_copy(rt[:, 10, :, 2 * p], rt[:, 9, :, e]))
                    chain(dve.tensor_copy(rt[:, 10, :, 2 * p + 1], rt[:, 11, :, e]))
                    shape = [P, NT, 2, SLOTS]
                    dve.tensor_tensor(onehot[:, p, :, :].rearrange("p t (j s) -> p t j s", j=2),
                                      TAB[:, T_IOTA:T_IOTA + SLOTS].unsqueeze(1).unsqueeze(1).to_broadcast(shape),
                                      rt[:, 10, :, 2 * p:2 * p + 1].unsqueeze(3).to_broadcast(shape), ALU.is_equal)\
                        .then_inc(g["slots_made"], 1)
                    dve.wait_ge(g["slots_made"], q.at("made"))

                def slots():
                    p = q.get("slots") % 2
                    q.add("slots")
                    dve.wait_ge(g["x_hi"], q.at("slots"))
                    lo_of(xe[p][:, :, SLOTS:P], PS[:, 6, :].rearrange("p (k s) -> p k s", k=KC), xe[p][:, :, 0:SLOTS])\
                        .then_inc(g["x_ready"], 1)

                def hidden():
                    n = q.get("hidden")
                    q.add("hidden")
                    dve.wait_ge(g["hidden_silu"], q.at("hidden"))
                    h, h_hi = hid_f32[:, n % 2, :], hid[:, n % 4, 0:SLOTS]
                    dve.tensor_tensor(h, hid_silu[:, n % 2, :], PS[:, 4 + n % 2, 2 * P + SLOTS:3 * P], ALU.mult)\
                        .then_inc(g["hidden_read"], 1)
                    dve.wait_ge(g["hidden_read"], q.at("hidden"))
                    chain(dve.tensor_copy(h_hi, h))
                    lo_of(hid[:, n % 4, SLOTS:P], h, h_hi).then_inc(g["hidden_ready"], 1)

                def outputs():
                    p = q.get("spread") % 2
                    q.add("spread")
                    dve.wait_ge(g["o_hi"], q.at("spread"))
                    dve.scalar_tensor_tensor(o_parts[1].rearrange("p (m n) -> p m n", m=2), PS[:, 6:8, :], st[:, p, 0:1],
                                             o_parts[0].bitcast(F32).rearrange("p (m n) -> p m n", m=2),
                                             ALU.mult, ALU.subtract).then_inc(g["o_ready"], 1)

                def step(m, e, first=False, last=False):
                    if m % 2 == 0 and not first:
                        outputs()
                    if m % 2 == 1 and e is not None:
                        dve.wait_ge(g["map_full"], q.at("made", -1))
                        made(e)
                    c.add("tile")
                    hidden()
                    lo_tiles(m, steps)
                    if m % 2 == 0 and not last:
                        slots()
                    c.add("tile")
                    hidden()
                    c.add("tile")

                chain(dve.memset(zero_row, 0.0))
                made(0)
                made(1)
                lo_tile(c.get("tile") + 2)
                slots()
                c.add("tile", 2)
                hidden()
                step(0, None, first=True)
                before = own["n"]
                own["stride"] = 8 + 2 * 2
                with dve.Fori(0, loops) as i:
                    c.enter(i)
                    q.enter(i)
                    for m in range(1, 5):
                        step(m, i * 2 + (m + 3) // 2)
                    c.leave(loops)
                    q.leave(loops)
                assert own["n"] - before == own["stride"]
                own["n"] += own["stride"] * (loops - 1)
                for m in range(1 + 4 * loops, steps):
                    step(m, None, last=m == steps - 1)
                hidden()
                c.add("tile")
                outputs()
                dve.wait_ge(g["y_full"], 1)
                n_f = N_EXP * F_EXPERT // P
                for signal, times in ((wb_freed, N_EXP // 2 + n_f), (he_f32, n_f), (he_ready, n_f)):
                    dve.sem_inc(signal, times)

            def experts_dense():
                for e2 in range(N_EXP // 2):
                    full()
                    freed(dve.tensor_copy(cbc[:, 2 * e2:2 * e2 + 2, :], bank().rearrange("p (e t) -> p e t", e=2)))
                dve.wait_ge(wb_freed, c.get("wb"))
                gated(N_EXP * F_EXPERT // P, True)

            def moe(layer):
                to_at()
                router()
                dve.wait_ge(route_ready, layer + 1)
                most = dve.value_load(route[0:1, 0:1], min_val=0, max_val=TOK)
                with dve.If(most <= SLOTS):
                    before = dict(c.n)
                    experts_gathered(layer)
                    c.n = before
                with dve.Else():
                    experts_dense()
                residual_add(0)
                layer_norm_tiles(layer == 0)

            for layer in range(2):
                if layer == 0:
                    dve.wait_ge(x_landed, 32)
                    ready(dve.tensor_copy(hs[:, 0, 0:1], hs[:, 0, 0:1]))
                    ready(dve.tensor_copy(hs[:, 0, 0:1], hs[:, 0, 0:1]))
                to_at()
                if layer == 0:
                    D1(dve.tensor_copy(pos_f[:, :], pos_i[:, :]))
                    for t in range(NT):
                        D1(dve.tensor_scalar(trig[:, 0, t, :], bc[:, B_INVF:B_INVF + 8], pos_f[:, t:t + 1], None, ALU.mult))
                    D1(dve.tensor_scalar(trig[:, 1, :, :], trig[:, 0, :, :], 1.0 / TWO_PI, ROUND, ALU.mult, ALU.add))
                    D1(dve.tensor_scalar(trig[:, 1, :, :], trig[:, 1, :, :], -ROUND, None, ALU.add))
                    for k in (PI_HI, PI_MID, PI_LO):
                        D1(dve.scalar_tensor_tensor(trig[:, 0, :, :], trig[:, 1, :, :], -k, trig[:, 0, :, :], ALU.mult, ALU.add))
                    D1(dve.tensor_scalar(trig[:, 3, :, :], trig[:, 0, :, :], 3.1415925, -3.1415925, ALU.min, ALU.max))
                    D1(dve.tensor_scalar(trig[:, 1, :, :], trig[:, 3, :, :], -1.0, None, ALU.mult))
                    D1(dve.tensor_tensor(trig[:, 1, :, :], trig[:, 1, :, :], trig[:, 3, :, :], ALU.max))
                    ask(dve.tensor_scalar(trig[:, 2, :, :], trig[:, 1, :, :], -1.0, math.pi / 2, ALU.mult, ALU.add))
                    done()
                    for n in range(3):
                        y_to([H[:, t, n * 512:(n + 1) * 512] for t in range(NT)])
                    y_to([H[:, t, 1536:1792] for t in range(NT)], 256, 1)
                    settled()
                    dve.wait_ge(tab_landed, 16 * 5)
                    for t in range(NT):
                        ask(dve.tensor_copy(hs[:, 0, 0:1], hs[:, 0, 0:1]))
                    for g2 in range(2):
                        full()
                        freed(dve.tensor_tensor(WT[:, 4 * g2:4 * g2 + 4, :], bank().rearrange("p (g t) -> p g t", g=4),
                                          TAB[:, 256:384].unsqueeze(1).to_broadcast([P, 4, P]), ALU.mult))
                    for t in range(NT):
                        v = H[:, t, 0:640].rearrange("p (h d) -> p h d", h=10)
                        cos = trig[:, 2, t, :].unsqueeze(1).to_broadcast([P, 10, 8])
                        sin = trig[:, 3, t, :].unsqueeze(1).to_broadcast([P, 10, 8])
                        r = PBf[:, 0:320].rearrange("p (j h d) -> p j h d", j=4, h=10)
                        D1(dve.tensor_tensor(r[:, 0, :, :], v[:, :, 0:8], cos, ALU.mult))
                        D1(dve.tensor_tensor(r[:, 1, :, :], v[:, :, 8:16], sin, ALU.mult))
                        D1(dve.tensor_tensor(r[:, 2, :, :], v[:, :, 8:16], cos, ALU.mult))
                        D1(dve.tensor_tensor(r[:, 3, :, :], v[:, :, 0:8], sin, ALU.mult))
                        D1(dve.tensor_tensor(v[:, :, 0:8], r[:, 0, :, :], r[:, 1, :, :], ALU.subtract))
                        D1(dve.tensor_tensor(v[:, :, 8:16], r[:, 2, :, :], r[:, 3, :, :], ALU.add))
                        kd = PB[:, 3, t * 256:(t + 1) * 256].rearrange("p (h r d) -> p h r d", h=2, r=2)
                        k2 = H[:, t, 512:640].rearrange("p (h d) -> p h d", h=2)
                        D1(dve.tensor_copy(kd[:, :, 0, :], k2))
                        ready(dve.tensor_copy(kd[:, :, 1, :], k2))
                        cols_out(QT[:, 0:4, t * P:(t + 1) * P])
                        cols_out(KT[:, 0:2, t * P:(t + 1) * P])
                    dve.wait_ge(wb_freed, c.get("wb"))

                    def o_evac(i):
                        t = i // 8
                        o_split(at_hi[:, 0:4, t * P:(t + 1) * P], at_lo[:, 0:4, t * P:(t + 1) * P], 4)
                    attention(16, 1, lambda i: (i // 8 + 1) * P, "sink", 1.0, lambda i: i % 8 == 7, o_evac)
                    done()
                    done()
                    prm_wait()
                    for t in range(NT):
                        v = H[:, t, 1280:1792].rearrange("p (g c) -> p g c", g=8)
                        sq = PBf[:, 0:512].rearrange("p (g c) -> p g c", g=8)
                        D1(dve.tensor_reduce(hs[:, 0, 0:8], v, AXX, ALU.add))
                        D1(dve.tensor_scalar(hs[:, 0, 0:8], hs[:, 0, 0:8], 1.0 / 64, None, ALU.mult))
                        D1(dve.tensor_tensor(v, v, hs[:, 0, 0:8].unsqueeze(2).to_broadcast([P, 8, 64]), ALU.subtract))
                        D1(dve.tensor_tensor(sq, v, v, ALU.mult))
                        D1(dve.tensor_reduce(hs[:, 2, 0:8], sq, AXX, ALU.add))
                        ask(dve.tensor_scalar(hs[:, 1, 0:8], hs[:, 2, 0:8], 1.0 / 64, LN_EPS, ALU.mult, ALU.add))
                        done()
                        D1(dve.reciprocal(hs[:, 2, 0:8], hs[:, 1, 0:8]))
                        D1(dve.tensor_tensor(v, v, hs[:, 2, 0:8].unsqueeze(2).to_broadcast([P, 8, 64]), ALU.mult))
                        D1(dve.tensor_tensor(H[:, t, 1280:1792], H[:, t, 1280:1792], PRM[:, 0, 0:512], ALU.mult))
                        ready(dve.tensor_tensor(H[:, t, 1280:1792], H[:, t, 1280:1792], PRM[:, 0, 512:1024], ALU.add))
                    dve.tensor_copy(mv[:, 0:1], mv[:, 1:2]).then_inc(prm_used, 1)
                    for t in range(NT):
                        full()
                        b = bank().rearrange("p (g c) -> p g c", g=8)
                        sq = PBf[:, t * 512:(t + 1) * 512].rearrange("p (g c) -> p g c", g=8)
                        freed(dve.tensor_tensor(sq, b, col[:, C_SGUB:C_SGUB + 8].unsqueeze(2).to_broadcast([P, 8, 64]), ALU.add))
                        dve.wait_ge(wb_freed, c.get("wb"))
                        ready(dve.tensor_tensor(H[:, t, 768:1280], H[:, t, 768:1280], PBf[:, t * 512:(t + 1) * 512], ALU.mult))
                    for t in range(NT):
                        full()
                        b = bank().rearrange("p (k q) -> p k q", k=4)
                        hi_wait()
                        sl = (slice(None), slice(4, 8), slice(t * P, (t + 1) * P))
                        freed(lo_of(at_lo[sl], b, at_hi[sl]))
                else:
                    for n in range(2):
                        y_to([H[:, t, n * 512:(n + 1) * 512] for t in range(NT)])
                    settled()
                    ready(dve.tensor_copy(hs[:, 0, 0:1], hs[:, 0, 0:1]))
                    for j2 in range(4):
                        full()
                        hi_wait()
                        freed(lo_of(at_lo[:, 2 * j2:2 * j2 + 2, :], bank().rearrange("p (k t) -> p k t", k=2),
                              at_hi[:, 2 * j2:2 * j2 + 2, :]))
                    tiles(1)
                    for g in range(4):
                        b = bank()
                        for m in range(2):
                            ins = dve.tensor_scalar(PBf[:, m * TOK:(m + 1) * TOK], b[:, m * TOK:(m + 1) * TOK],
                                                    col[:, C_POOL + 2 * g + m:C_POOL + 2 * g + m + 1], None, ALU.mult)
                        ins.then_inc(aff_ready, 1)
                        c.add("aff")
                        dve.wait_ge(aff_ready, c.get("aff"))
                        hi_wait()
                        freed(lo_of(at_lo[:, 2 * g:2 * g + 2, :], PBf[:, 0:512].rearrange("p (k t) -> p k t", k=2),
                              at_hi[:, 2 * g:2 * g + 2, :]))
                cross(layer)
                moe(layer)

            diff(1)
            a, b8 = affine_of(0, 1, 0)
            rms_to_h(asked=True)
            to_at(a, b8)
            dve.wait_ge(tab_landed, 16 * 8)
            for n in range(2):
                y_to([H[:, t, n * 512:(n + 1) * 512] for t in range(NT)])
            pair = c.get("y")
            tiles(2)
            for t in range(NT):
                D1(dve.tensor_copy(H[:, t, D:D + 256], ybank(pair, t)[:, 0:256]))
                ins = dve.tensor_copy(V[:, 2 + t, 0:256], ybank(pair, t)[:, 256:512])
                if t == NT - 1:
                    ins.then_inc(y_freed, 1)
                else:
                    D1(ins)
            c.add("y")
            settled()
            for t in range(NT):
                head_norm(t, 10, P, 0, RMS_EPS)
                head_gain(t, 8, P, 0, B_GQ)
                head_gain(t, 2, P, D, B_GK)
                ready(axial(t, 10, P))
            for t in range(NT):
                for j in range(2):
                    cols_out(QT[:, 4 * j:4 * j + 4, t * P:(t + 1) * P])
                cols_out(KT[:, 0:2, TOK + t * P:TOK + (t + 1) * P])
            dve.wait_ge(wb_freed, c.get("wb"))

            def o_evac(i):
                j = i // 4
                o_split(at_hi[:, 2 * j:2 * j + 2, :], at_lo[:, 2 * j:2 * j + 2, :], 2)
            attention(16, 1, lambda i: 512, "gqa", 128 ** -0.5, lambda i: i % 4 == 3, o_evac)
            residual_gate(2)
            a, b8 = affine_of(0, 1, 1)
            rms_to_h(asked=True)
            to_at(a, b8)
            gated(F_FFN // P, False)
            residual_gate(0, to_rms=False)
            dve.tensor_copy(hs[:, 0, 0:1], hs[:, 0, 0:1]).then_inc(result_ready, 1)



_INS = ["x", "mem", "positions", "router_w", "router_bias",
        "l0_w_in", "l0_sinks", "l0_sgu_ln_g", "l0_sgu_ln_b", "l0_sgu_w", "l0_sgu_b", "l0_w_out",
        "l0_ln1_g", "l0_ln1_b", "l0_xq", "l0_xkv", "l0_xo", "l0_ln2_g", "l0_ln2_b",
        "l0_e_gate", "l0_e_up", "l0_e_down", "l0_ln3_g", "l0_ln3_b",
        "l1_w_in", "l1_pool_w", "l1_pool_scale", "l1_w_out",
        "l1_ln1_g", "l1_ln1_b", "l1_xq", "l1_xkv", "l1_xo", "l1_ln2_g", "l1_ln2_b",
        "l1_e_gate", "l1_e_up", "l1_e_down", "l1_ln3_g", "l1_ln3_b",
        "c_2", "ctx_2", "c_ctx_2", "ada_w_2", "ada_b_2", "norm1_g_2", "norm2_g_2", "ffn_w_gu_2", "ffn_w_down_2",
        "diff_w_in_2", "diff_w_out_2", "diff_q_norm_2", "diff_k_norm_2", "diff_lambda_q1_2", "diff_lambda_k1_2",
        "diff_lambda_q2_2", "diff_lambda_k2_2", "diff_subln_2", "gqa_w_in_2", "gqa_w_out_2", "gqa_q_norm_2",
        "gqa_k_norm_2"]


def constants():
    f = np.float32
    i = np.arange(P)
    prev = np.where(i[None, :] > i[:, None], 0.0, -1e30)
    own = np.where(i[None, :] <= i[:, None], 0.0, -1e30)
    slots = np.arange(SLOTS)
    masks = np.concatenate([prev, own, (i[:, None] <= i[None, :]).astype(f), np.broadcast_to(slots, (P, SLOTS)),
                            i[:, None] % SLOTS == slots[None, :]], axis=1)
    t, s = np.arange(TOK)[:, None], np.arange(TOK)[None, :]
    band = np.zeros((P, NT, 4, TOK), f)
    for g, w in enumerate(WINDOWS):
        m = ((t - s >= 0) & (t - s < w)) / np.minimum(t + 1, w) - (t == s)
        band[:, :, g, :] = m.T.reshape(NT, P, TOK).transpose(1, 0, 2)
    out = {"c_ident": np.eye(P, dtype=f), "c_masks": masks.astype(f), "c_band": band.reshape(P, NT, 4 * TOK),
           "c_invf": (500000.0 ** (-(np.arange(8) * 2.0 / 16))).astype(f)}
    row, cl = np.arange(TOK) // 64, np.arange(TOK) % 64
    for dh in (64, 128):
        half = dh // 2
        inv = (f(10000.0) ** (-np.arange(0, half, 2, dtype=f) / f(half))).astype(f)
        ang = [np.concatenate([a, a], axis=-1) for a in (row.astype(f)[:, None] * inv, cl.astype(f)[:, None] * inv)]
        ang = np.concatenate(ang, axis=-1)
        sign = np.tile(np.concatenate([-np.ones(half // 2), np.ones(half // 2)]), 2)
        out[f"c_ax{dh}"] = np.concatenate([np.cos(ang), np.sin(ang) * sign], axis=1).astype(f)
    return out


def kernel(**inputs):
    import concourse.bacc as bacc
    from concourse.bass_utils import run_bass_kernel_spmd

    nc = bacc.Bacc("TRN2", target_bir_lowering=False, num_devices=1, dynamic_dma_scratch_size=1024)
    arrays = {name: np.ascontiguousarray(inputs[name]) for name in _INS}
    arrays.update(constants())
    aps = {name: nc.dram_tensor(name, a.shape, mybir.dt.from_np(a.dtype), kind="ExternalInput").ap()
           for name, a in arrays.items()}
    out = nc.dram_tensor("out", (1, TOK, D), F32, kind="ExternalOutput").ap()
    build(nc, aps, out)
    r = run_bass_kernel_spmd(nc, [arrays], core_ids=[0])
    return r.results[0]["out"]
```
